# Optimizing a Trainium2 kernel written in Bass

```python
import jax, jax.numpy as jnp
from jax import lax
import numpy as np

D_MODEL = 1024
BATCH = 1
SEQ = 128
DEPTH = 1
DEC_BATCH = 1
DEC_SEQ = 512
PAST_LEN = 128

GRID_W = 64
RET_HEADS = 4
RET_DK = 128
RET_DV = 256
RET_CHUNK = 128
HG_HEADS = 8
HG_DK = 128
HG_DV = 128
HG_CHUNK = 32
D_FF = 2816
N_MOD = 9
ROPE_BASE = 10000.0
EPS = 1e-6
RET_QK = RET_HEADS * RET_DK
RET_V = RET_HEADS * RET_DV
HG_KW = HG_HEADS * HG_DK
HG_VW = HG_HEADS * HG_DV
SPLITS = (RET_QK, RET_QK, RET_V, RET_V, HG_KW, HG_KW, HG_KW, HG_VW, HG_VW, D_MODEL, D_MODEL)
IN_WIDTH = sum(SPLITS)

kernel_name = 'hybrid_retention_hgrn2_diffusion_step'

def rms_norm(x, w):
    xf = x.astype(jnp.float32)
    y = xf * lax.rsqrt(jnp.mean(xf * xf, axis=-1, keepdims=True) + EPS)
    return (y * w.astype(jnp.float32)).astype(x.dtype)

def head_rms(x):
    return x * lax.rsqrt(jnp.mean(x * x, axis=-1, keepdims=True) + EPS)

def modulate(x, shift, scale):
    return x * (1.0 + scale) + shift

def swiglu(h, w13, w2):
    a, b = jnp.split(h @ w13, 2, axis=-1)
    return (jax.nn.silu(a) * b) @ w2

def rope_2d(x, n_tokens):
    rows = n_tokens // GRID_W
    r, cl = jnp.meshgrid(jnp.arange(rows), jnp.arange(GRID_W), indexing='ij')
    r = r.reshape(-1).astype(jnp.float32)
    cl = cl.reshape(-1).astype(jnp.float32)
    half = x.shape[-1] // 2
    quarter = half // 2
    inv_freq = ROPE_BASE ** (-jnp.arange(quarter, dtype=jnp.float32) / quarter)

    def rot(xh, pos):
        ang = pos[:, None] * inv_freq[None, :]
        cos = jnp.cos(ang)[None, :, None, :]
        sin = jnp.sin(ang)[None, :, None, :]
        x1, x2 = jnp.split(xh, 2, axis=-1)
        return jnp.concatenate([x1 * cos - x2 * sin, x2 * cos + x1 * sin], axis=-1)

    return jnp.concatenate([rot(x[..., :half], r), rot(x[..., half:], cl)], axis=-1)

def to_chunks(x, chunk):
    b, n = x.shape[:2]
    return x.reshape(b, n // chunk, chunk, *x.shape[2:]).swapaxes(0, 1)

def from_chunks(y):
    n, b, chunk = y.shape[:3]
    return y.swapaxes(0, 1).reshape(b, n * chunk, *y.shape[3:])

def retention_scan(q, k, v, log_g, s0):
    C = RET_CHUNK
    idx = jnp.arange(C, dtype=jnp.float32)
    diff = idx[:, None] - idx[None, :]
    causal = diff >= 0
    dmat = jnp.where(causal[None], jnp.exp(jnp.where(causal, diff, 0.0)[None] * log_g[:, None, None]), 0.0)
    q_dec = jnp.exp((idx + 1.0)[:, None] * log_g[None, :])
    k_dec = jnp.exp((C - 1.0 - idx)[:, None] * log_g[None, :])
    c_dec = jnp.exp(C * log_g)

    def step(s, inp):
        qc, kc, vc = inp
        scores = jnp.einsum('bihd,bjhd->bhij', qc, kc) * dmat[None]
        o = (jnp.einsum('bhij,bjhe->bihe', scores, vc)
             + jnp.einsum('bihd,bhde->bihe', qc * q_dec[None, :, :, None], s))
        s = c_dec[None, :, None, None] * s + jnp.einsum('bjhd,bjhe->bhde', kc * k_dec[None, :, :, None], vc)
        return s, o

    s_fin, o = lax.scan(step, s0, (to_chunks(q, C), to_chunks(k, C), to_chunks(v, C)))
    return from_chunks(o), s_fin

def gla_scan(q, k, v, log_f, s0):
    C = HG_CHUNK
    tri = jnp.tril(jnp.ones((C, C), dtype=bool))[None, :, :, None, None]

    def step(s, inp):
        qc, kc, vc, gc = inp
        b = jnp.cumsum(gc, axis=1)
        diff = b[:, :, None] - b[:, None, :]
        dec = jnp.where(tri, jnp.exp(jnp.where(tri, diff, 0.0)), 0.0)
        a = jnp.einsum('bthk,bshk,btshk->bhts', qc, kc, dec)
        o = jnp.einsum('bhts,bshv->bthv', a, vc) + jnp.einsum('bthk,bhkv->bthv', qc * jnp.exp(b), s)
        b_last = b[:, -1]
        s = (jnp.exp(b_last)[..., None] * s
             + jnp.einsum('bshk,bshv->bhkv', kc * jnp.exp(b_last[:, None] - b), vc))
        return s, o

    s_fin, o = lax.scan(step, s0, (to_chunks(q, C), to_chunks(k, C), to_chunks(v, C), to_chunks(log_f, C)))
    return from_chunks(o), s_fin

def flip(t):
    return jnp.flip(t, axis=1)

def mixer(h, s0_ret, s0_hg, use_rope, lp):
    f32 = jnp.float32
    B, L, _ = h.shape
    proj = h @ lp['w_in']
    cuts = np.cumsum(SPLITS)[:-1].tolist()
    rq, rk, rv, rg, hq, hff, hfb, hi, hog, gr, gh = jnp.split(proj, cuts, axis=-1)

    rq = rq.reshape(B, L, RET_HEADS, RET_DK).astype(f32)
    rk = rk.reshape(B, L, RET_HEADS, RET_DK).astype(f32)
    rv = rv.reshape(B, L, RET_HEADS, RET_DV).astype(f32)
    if use_rope:
        rq = rope_2d(rq, L)
        rk = rope_2d(rk, L)
    rk = rk * (RET_DK ** -0.5)
    log_gam = jax.nn.log_sigmoid(lp['ret_decay'].astype(f32))
    of, sf = retention_scan(rq, rk, rv, log_gam[0], s0_ret[:, 0])
    ob, sb = retention_scan(flip(rq), flip(rk), flip(rv), log_gam[1], s0_ret[:, 1])
    o_ret = head_rms(of + flip(ob)).reshape(B, L, RET_V) * jax.nn.silu(rg.astype(f32))
    y_ret = o_ret.astype(h.dtype) @ lp['w_ret_proj']

    q = jax.nn.silu(hq.reshape(B, L, HG_HEADS, HG_DK).astype(f32)) * (HG_DK ** -0.5)
    iv = hi.reshape(B, L, HG_HEADS, HG_DV).astype(f32)
    lb = lp['lb'].reshape(2, HG_HEADS, HG_DK)
    f_f = lb[0] + (1.0 - lb[0]) * jax.nn.sigmoid(hff.reshape(B, L, HG_HEADS, HG_DK).astype(f32))
    f_b = lb[1] + (1.0 - lb[1]) * jax.nn.sigmoid(hfb.reshape(B, L, HG_HEADS, HG_DK).astype(f32))
    of2, sf2 = gla_scan(q, 1.0 - f_f, iv, jnp.log(f_f), s0_hg[:, 0])
    ob2, sb2 = gla_scan(flip(q), flip(1.0 - f_b), flip(iv), flip(jnp.log(f_b)), s0_hg[:, 1])
    o_hg = head_rms(of2 + flip(ob2)) * lp['hg_norm_w'].astype(f32).reshape(HG_HEADS, HG_DV)
    o_hg = o_hg.reshape(B, L, HG_VW) * jax.nn.silu(hog.astype(f32))
    y_hg = o_hg.astype(h.dtype) @ lp['w_hg_proj']

    merged = jax.nn.sigmoid(gr) * y_ret + jax.nn.sigmoid(gh) * y_hg
    out = merged @ lp['w_o']
    return out, jnp.stack([sf, sb], axis=1), jnp.stack([sf2, sb2], axis=1)

def trunk_layer(x, mod, s0_ret, s0_hg, use_rope, lp):
    sh1, sc1, g1, sh2, sc2, g2, sh3, sc3, g3 = jnp.split(mod, N_MOD, axis=-1)
    nw = lp['norm_w']
    x = x + 0.5 * g1 * swiglu(modulate(rms_norm(x, nw[0]), sh1, sc1), lp['ffn1_w13'], lp['ffn1_w2'])
    mix, s_ret, s_hg = mixer(modulate(rms_norm(x, nw[1]), sh2, sc2), s0_ret, s0_hg, use_rope, lp)
    x = x + g2 * mix
    x = x + 0.5 * g3 * swiglu(modulate(rms_norm(x, nw[2]), sh3, sc3), lp['ffn2_w13'], lp['ffn2_w2'])
    return x, s_ret, s_hg

def setup_inputs(seed: int = 0) -> dict:
    key = jax.random.key(seed)
    ks = jax.random.split(key, 24)
    f32 = jnp.float32

    def nrm(k, shape, scale):
        return jax.random.normal(k, shape, f32) * scale

    ret_base = jnp.asarray(np.log(2.0 ** (5.0 + np.arange(RET_HEADS)) - 1.0), f32)
    return {
        'x_prompt': nrm(ks[0], (BATCH, SEQ, D_MODEL), 1.0),
        'x_sample': nrm(ks[1], (DEC_BATCH, DEC_SEQ, D_MODEL), 1.0),
        'state_ret': nrm(ks[2], (DEC_BATCH, DEPTH, 2, RET_HEADS, RET_DK, RET_DV), 0.5),
        'state_hgrn': nrm(ks[3], (DEC_BATCH, DEPTH, 2, HG_HEADS, HG_DK, HG_DV), 0.5),
        'c': nrm(ks[4], (DEC_BATCH, D_MODEL), 1.0),
        'c_ctx': nrm(ks[5], (D_MODEL,), 1.0),
        'ada_w': nrm(ks[6], (DEPTH, D_MODEL, N_MOD * D_MODEL), 0.5 * D_MODEL ** -0.5),
        'ada_b': nrm(ks[7], (DEPTH, N_MOD * D_MODEL), 0.01),
        'norm_w': 1.0 + nrm(ks[8], (DEPTH, 3, D_MODEL), 0.01),
        'ffn1_w13': nrm(ks[9], (DEPTH, D_MODEL, 2 * D_FF), D_MODEL ** -0.5),
        'ffn1_w2': nrm(ks[10], (DEPTH, D_FF, D_MODEL), D_FF ** -0.5),
        'ffn2_w13': nrm(ks[11], (DEPTH, D_MODEL, 2 * D_FF), D_MODEL ** -0.5),
        'ffn2_w2': nrm(ks[12], (DEPTH, D_FF, D_MODEL), D_FF ** -0.5),
        'w_in': nrm(ks[13], (DEPTH, D_MODEL, IN_WIDTH), D_MODEL ** -0.5),
        'ret_decay': ret_base[None, None, :] + nrm(ks[14], (DEPTH, 2, RET_HEADS), 0.1),
        'hg_lb_logits': nrm(ks[15], (2, DEPTH + 1, HG_KW), 0.1),
        'hg_norm_w': 1.0 + nrm(ks[16], (DEPTH, HG_VW), 0.01),
        'w_ret_proj': nrm(ks[17], (DEPTH, RET_V, D_MODEL), RET_V ** -0.5),
        'w_hg_proj': nrm(ks[18], (DEPTH, HG_VW, D_MODEL), HG_VW ** -0.5),
        'w_o': nrm(ks[19], (DEPTH, D_MODEL, D_MODEL), D_MODEL ** -0.5),
        'final_norm_w': 1.0 + nrm(ks[20], (D_MODEL,), 0.01),
    }

def reference(x_prompt, x_sample, state_ret, state_hgrn, c, c_ctx, ada_w, ada_b, norm_w,
              ffn1_w13, ffn1_w2, ffn2_w13, ffn2_w2, w_in, ret_decay, hg_lb_logits, hg_norm_w,
              w_ret_proj, w_hg_proj, w_o, final_norm_w):
    f32 = jnp.float32
    lb_all = jnp.cumsum(jax.nn.softmax(hg_lb_logits.astype(f32), axis=1), axis=1)
    bp = x_prompt.shape[0]
    zero_ret = jnp.zeros((bp, 2, RET_HEADS, RET_DK, RET_DV), f32)
    zero_hg = jnp.zeros((bp, 2, HG_HEADS, HG_DK, HG_DV), f32)
    xp, xs = x_prompt, x_sample
    new_ret, new_hg = [], []
    for l in range(DEPTH):
        lp = {
            'norm_w': norm_w[l], 'ffn1_w13': ffn1_w13[l], 'ffn1_w2': ffn1_w2[l],
            'ffn2_w13': ffn2_w13[l], 'ffn2_w2': ffn2_w2[l], 'w_in': w_in[l],
            'ret_decay': ret_decay[l], 'lb': lb_all[:, l], 'hg_norm_w': hg_norm_w[l],
            'w_ret_proj': w_ret_proj[l], 'w_hg_proj': w_hg_proj[l], 'w_o': w_o[l],
        }
        mod_ctx = (jax.nn.silu(c_ctx) @ ada_w[l] + ada_b[l])[None, None, :]
        mod_lat = (jax.nn.silu(c) @ ada_w[l] + ada_b[l])[:, None, :]
        xp, s_ret, s_hg = trunk_layer(xp, mod_ctx, zero_ret, zero_hg, False, lp)
        new_ret.append(s_ret)
        new_hg.append(s_hg)
        xs, _, _ = trunk_layer(xs, mod_lat, state_ret[:, l].astype(f32), state_hgrn[:, l].astype(f32), True, lp)
    y_prompt = rms_norm(xp, final_norm_w)
    y_sample = rms_norm(xs, final_norm_w)
    new_state_ret = jnp.stack(new_ret, axis=1).astype(x_prompt.dtype)
    new_state_hgrn = jnp.stack(new_hg, axis=1).astype(x_prompt.dtype)
    return (y_prompt, y_sample, new_state_ret, new_state_hgrn)


_drawn_inputs = setup_inputs


def setup_inputs(seed=0):
    import zlib

    import numpy as np

    out = dict(_drawn_inputs(seed))
    spreads = {}
    factors = {'state_ret': 25.176,
     'state_hgrn': 31.125,
     'norm_w': 5.296,
     'hg_norm_w': 48.202,
     'final_norm_w': 34.274}
    for name, (base, spread) in spreads.items():
        noise = np.random.default_rng([zlib.crc32(name.encode()), seed]).standard_normal(out[name].shape)
        drawn = base * np.exp(spread * noise) if base else spread * noise
        out[name] = __import__('jax').numpy.asarray(drawn.astype(out[name].dtype))
    for name, factor in factors.items():
        out[name] = (out[name] * factor).astype(out[name].dtype)
    return out
```

```python
from contextlib import ExitStack

import numpy as np

import concourse.bass as bass
from concourse import mybir

F32 = mybir.dt.float32
F32R = mybir.dt.float32r
U32 = mybir.dt.uint32
ALU = mybir.AluOpType
ACT = mybir.ActivationFunctionType

P = 128
D_MODEL = 1024
KT = D_MODEL // P
CTX, LAT = 128, 512
T = CTX + LAT
NT = T // P
HT = T // 2
D_FF = 2816
RET_HEADS, RET_DK, RET_DV = 4, 128, 256
HG_HEADS, HG_DK, HG_DV = 8, 128, 128
GRID_W = 64
ROPE_BASE = 10000.0
EPS = 1e-6
N_MOD = 9
LEVELS = 7
TINY = 2.0 ** -62
SH1, SC1, G1, SH2, SC2, G2, SH3, SC3, G3 = range(N_MOD)

FF_CHUNKS = (8, 8, 6)
ADA_HEAD = 24
ADA_SLOTS = 4
SLOTS = 3
CREDIT = 2

PHASES = []
for _f in (1, 2):
    if _f == 2:
        PHASES += [("hg", HG_HEADS, (0, 1, 2, 0, 1), (0, 1, 0, 1, 0)),
                   ("ret", RET_HEADS, (0, 1, 2, 0, 1, 2), (0, 1, 0, 1, 0, 1)),
                   ("gate", KT, (0, 1, 2, 1), (0, 1, 0, 1)),
                   ("wo", KT // 2, (0, 1), (0, 1))]
    for _c, _n in enumerate(FF_CHUNKS):
        PHASES += [(f"up{_f}{_c}", _n, (0, 1), (0, 1)), (f"down{_f}{_c}", KT // 2, (0, 1), (0, 1))]


class Stream:

    def __init__(self):
        self.phase, at, slots, sets, order = {}, 0, [0] * SLOTS, [0, 0], []
        for name, steps, slot, group in PHASES:
            self.phase[name] = (steps, slot, group, at, tuple(slots), tuple(sets))
            order += list(slot) * steps
            at += steps * len(slot)
            for s in slot:
                slots[s] += steps
            for g in group:
                sets[g] += steps
        self.total, self.gap = at, {}
        for name, (steps, slot, _, base, _, _) in self.phase.items():
            for p in range(len(slot)):
                gaps = []
                for i in range(steps):
                    n = base + i * len(slot) + p
                    before = [m for m in range(n) if order[m] == order[n]]
                    gaps.append(n - before[-1] if before else 2)
                self.gap[name, p] = min(gaps)

    def index(self, name, p, i):
        _, slot, _, base, _, _ = self.phase[name]
        return base + i * len(slot) + p

    def after(self, name, p, i):
        return self.index(name, p, i) + 1 + CREDIT

    def slot_clear(self, name, p, i):
        return self.after(name, p, i) - self.gap[name, p]

    def loads(self, name, p, i):
        _, slot, _, _, slots, _ = self.phase[name]
        return slots[slot[p]] + i * slot.count(slot[p]) + slot[:p].count(slot[p]) + 1

    def uses(self, name, p, i):
        _, _, group, _, _, sets = self.phase[name]
        return sets[group[p]] + i * group.count(group[p]) + group[:p].count(group[p]) + 1


ST = Stream()
C_NAMES = [("c", 16), ("ada_b", 72), ("norm_w", 24), ("final_w", 8), ("hg_w", 8), ("lb", 32), ("decay", 8), ("kpos", 2)]


def shape_constants():
    s, t = np.arange(P)[:, None], np.arange(P)[None, :]
    ident = (s == t).astype(np.float32)
    q = RET_DK // 4
    perm = np.zeros((P, P), np.float32)
    for base in (0, 2 * q):
        for j in range(q):
            perm[base + q + j, base + j] = -1.0
            perm[base + j, base + q + j] = 1.0
    freq = np.float32(ROPE_BASE) ** (-np.arange(q, dtype=np.float32) / np.float32(q))
    n = np.arange(LAT)
    row, col = (n // GRID_W).astype(np.float32), (n % GRID_W).astype(np.float32)
    ang = np.concatenate([freq[:, None] * row, freq[:, None] * row, freq[:, None] * col, freq[:, None] * col])
    ang = ang.astype(np.float32)
    cos = np.concatenate([np.ones((P, CTX), np.float32), np.cos(ang)], 1)
    sin = np.concatenate([np.zeros((P, CTX), np.float32), np.sin(ang)], 1)
    dist = np.abs(t - s).astype(np.float32)
    upper, lower = (t >= s).astype(np.float32), (t <= s).astype(np.float32)
    rows = np.stack([np.broadcast_to(t + 1, (P, P)), np.broadcast_to(P - t, (P, P))], 1).astype(np.float32)
    masks = np.zeros((P, LEVELS, P), np.uint32)
    for u in range(LEVELS):
        half = 1 << u
        masks[:, u, :] = (s // (2 * half) == t // (2 * half)) & (s // half != t // half)
    kpos = np.stack([P - 1 - np.arange(P), np.arange(P)], 1).astype(np.float32)
    return dict(ident=ident, perm=perm, cos=cos, sin=sin, dist=dist, upper=upper, lower=lower,
                rows=rows.reshape(P, 2 * P), masks=masks.reshape(P, LEVELS * P)), kpos


def build(nc, d):
    ctx = ExitStack()
    with ctx:
        def sb(name, shape, dt=F32, scope=ctx):
            return scope.enter_context(nc.sbuf_tensor(name, shape, dt))

        def sem(name):
            return ctx.enter_context(nc.semaphore(name))

        x = sb("x", [P, KT, T])
        h_hi, h_lo = sb("h_hi", [P, KT, T], F32R), sb("h_lo", [P, KT, T], F32R)
        raw = sb("raw", [P, SLOTS, KT * P])
        w_hi = sb("w_hi", [P, SLOTS, KT * P], F32R)
        w_lo = sb("w_lo", [P, SLOTS, KT * P], F32R)
        small = {n: sb("in_" + n, [P, w]) for n, w in C_NAMES}
        silu_c = sb("silu_c", [P, KT, 2])
        mod = sb("mod", [P, N_MOD, KT, 2])
        ident, perm, ones = sb("ident", [P, P]), sb("perm", [P, P]), sb("ones", [P, P])
        eps = sb("eps", [P, 1])
        lb, lb_rest = sb("lb", [P, 2 * KT]), sb("lb_rest", [P, 2 * KT])
        log_gam, gam_tmp = sb("log_gam", [P, 8]), sb("gam_tmp", [P, 5, 8])
        k_decay, c_decay = sb("k_decay", [P, 8]), sb("c_decay", [P, 8])
        soft = sb("soft", [P, 4, 16])
        scope = ExitStack()
        u_hi, u_lo = sb("u_hi", [P, 8, T], F32R, scope), sb("u_lo", [P, 8, T], F32R, scope)
        gate_a, u_full = sb("gate_a", [P, T], F32, scope), sb("u_full", [P, T], F32, scope)
        square = sb("square", [P, 2, T], F32, scope)
        root, rstd = sb("root", [P, T], F32, scope), sb("rstd", [P, T], F32, scope)
        x_norm, h_full = sb("x_norm", [P, 2, T], F32, scope), sb("h_full", [P, 2, T], F32, scope)
        ada_raw = sb("ada_raw", [P, ADA_SLOTS, KT * P], F32, scope)
        scope.close()
        mixer = ExitStack()
        o_hg = sb("o_hg", [P, KT, T], F32, mixer)
        scope = ExitStack()
        pre = sb("hg_pre", [P, 5, T], F32, scope)
        q, k_f, k_b = (sb(n, [P, T], F32, scope) for n in ("hg_q", "hg_kf", "hg_kb"))
        g_f, g_b, b_f = (sb(n, [P, T], F32, scope) for n in ("hg_gf", "hg_gb", "hg_bf"))
        p_b = sb("hg_pb", [P, NT, P + 1], F32, scope)
        out_gate = sb("hg_outgate", [P, T], F32, scope)
        v_tok = sb("hg_v", [P, NT, P], F32, scope)
        e_f, e_b = sb("hg_ef", [P, 2, T], F32, scope), sb("hg_eb", [P, 2, T], F32, scope)
        q_lev, k_lev = sb("hg_qlev", [P, 2, T], F32, scope), sb("hg_klev", [P, 2, T], F32, scope)
        att = sb("hg_att", [P, NT, P], F32, scope)
        k_tok = sb("hg_ktok", [P, 2, 4, P], F32, scope)
        s_in, s_run = sb("hg_sin", [P, 2, P], F32, scope), sb("hg_srun", [P, 2, 3, P], F32, scope)
        masks = sb("hg_masks", [P, LEVELS, P], U32, scope)
        s_fin, s_dec = sb("hg_sfin", [P, 2, P], F32, scope), sb("hg_sdec", [P, 2, NT], F32, scope)
        scope.close()
        o_ret = sb("o_ret", [P, KT, T], F32, mixer)
        scope = ExitStack()
        r_pre = sb("ret_pre", [P, 6, T], F32, scope)
        r_rot = sb("ret_rot", [P, 2, T], F32, scope)
        r_tmp = sb("ret_tmp", [P, 2, T], F32, scope)
        r_att = sb("ret_att", [P, NT, P], F32, scope)
        r_v = sb("ret_v", [P, NT, 2, P], F32, scope)
        r_ktok = sb("ret_ktok", [P, 2, 4, P], F32, scope)
        r_qdec = sb("ret_qdec", [P, 2, LAT], F32, scope)
        r_sin = sb("ret_sin", [P, 2, RET_DV], F32, scope)
        r_srun = sb("ret_srun", [P, 2, 3, RET_DV], F32, scope)
        r_sfin = sb("ret_sfin", [P, 2, RET_DV], F32, scope)
        cos, sin = sb("cos", [P, T], F32, scope), sb("sin", [P, T], F32, scope)
        d_mat = sb("ret_d", [P, RET_HEADS, P], F32, scope)
        q_rows = sb("ret_qrows", [P, 8, P], F32, scope)
        scope.close()
        mixer.close()
        scope = ExitStack()
        hg_lo, ret_lo = sb("hg_lo", [P, KT, T], F32R, scope), sb("ret_lo", [P, KT, T], F32R, scope)
        hg_hi, ret_hi = sb("hg_hi", [P, KT, T], F32R, scope), sb("ret_hi", [P, KT, T], F32R, scope)
        merged, sig_buf = sb("merged", [P, KT, T], F32, scope), sb("sig_buf", [P, 2, T], F32, scope)
        scope.close()
        dist = r_tmp[:, 0, 0:P]
        upper, lower = r_tmp[:, 0, P:2 * P], r_tmp[:, 0, 2 * P:3 * P]
        rows = r_tmp[:, 0, 3 * P:5 * P].rearrange("p (d t) -> p d t", d=2)
        e_mat = r_tmp[:, 1, 0:2 * P].rearrange("p (d t) -> p d t", d=2)

        acc = [ctx.enter_context(nc.psum_tensor(f"acc{g}", [P, 2, 512], F32)) for g in range(2)]
        mix = [ctx.enter_context(nc.psum_tensor(f"mix{g}", [P, 2, 512], F32)) for g in range(2)]
        acc_v = [a[:, :, 0:HT] for a in acc]
        mix_v = [m[:, :, 0:HT] for m in mix]
        mix_r = [m[:].rearrange("p b n -> p (b n)") for m in mix]

        def halves(ap):
            return ap.rearrange("p (b n) -> p b n", b=2)

        loaded = [sem(f"slab_loaded{s}") for s in range(SLOTS)]
        hi_done, split_done, slab_done = sem("hi_done"), sem("split_done"), sem("slab_done")
        evacuated = [sem(f"acc_evacuated{g}") for g in range(2)]
        mixed = [sem(f"mix_evacuated{g}") for g in range(2)]
        in_small, in_x, in_tab = sem("in_small"), sem("in_x"), sem("in_tab")
        ones_set, silu_done = sem("ones_set"), sem("silu_done")
        ada_loaded = [sem(f"ada_loaded{s}") for s in range(ADA_SLOTS)]
        ada_read, ada_done, ada_moved = sem("ada_read"), sem("ada_done"), sem("ada_moved")
        small_done, small_act = sem("small_done"), sem("small_act")
        coef_done = sem("coef_done")
        sq_done, sq_summed, root_done, rstd_done = sem("sq_done"), sem("sq_summed"), sem("root_done"), sem("rstd_done")
        xn_done, mod_done, hhi_done, hlo_done = sem("xn_done"), sem("mod_done"), sem("hhi_done"), sem("hlo_done")
        uhi_done, ulo_done = sem("uhi_done"), sem("ulo_done")
        x_updated = sem("x_updated")
        y_out, states_out = sem("y_out"), sem("states_out")

        def wait(eng, s, value):
            if isinstance(value, int) and value <= 0:
                return
            eng.wait_ge(s, value)

        pool_waited, dve_waited = sem("pool_waited"), sem("dve_waited")

        def load_slab(sp, name, p, i):
            slot = ST.phase[name][1][p]
            wait(sp, split_done, ST.slot_clear(name, p, i))
            sp.dma_start(raw[:, slot, :], d["w"][ST.index(name, p, i)]).then_inc(loaded[slot], 16)

        def split_slab(pool, name, p, i):
            slot = ST.phase[name][1][p]
            wait(pool, loaded[slot], 16 * ST.loads(name, p, i))
            wait(pool, slab_done, ST.slot_clear(name, p, i))
            pool.sem_inc(pool_waited, 1)
            pool.tensor_copy(w_hi[:, slot, :], raw[:, slot, :]).then_inc(hi_done, 1)
            wait(pool, hi_done, ST.index(name, p, i) + 1)
            pool.tensor_tensor(w_lo[:, slot, :], raw[:, slot, :], w_hi[:, slot, :].bitcast(F32),
                               ALU.subtract).then_inc(split_done, 1)

        def project(pe, name, p, i, src_hi, src_lo, k_tiles=KT):
            _, slots, sets, _, _, _ = ST.phase[name]
            s, g = slots[p], sets[p]
            wait(pe, split_done, ST.after(name, p, i))
            wait(pe, evacuated[g], ST.uses(name, p, i))
            for k in range(k_tiles):
                for n, (w, r) in enumerate(((w_hi, src_hi), (w_hi, src_lo), (w_lo, src_hi))):
                    for b in range(2):
                        last = pe.matmul(acc[g][:, b, 0:HT], w[:, s, k * P:(k + 1) * P],
                                         r[:, k, b * HT:(b + 1) * HT],
                                         start=(k == 0 and n == 0), stop=(k == k_tiles - 1 and n == 2))
            last.then_inc(slab_done, 1)

        def projected(eng, name, p, i):
            wait(eng, slab_done, ST.after(name, p, i))

        def acc_read(eng, name, p, i):
            wait(eng, evacuated[ST.phase[name][2][p]], ST.uses(name, p, i) + 1)

        HG0, HG1, RT0, RT1 = 7, 6, 5, 4

        class Uses:
            norm1 = [1, 1]
            ada_head = [1, 2]
            down1 = [ada_head[0] + ADA_HEAD // ADA_SLOTS, 2]
            norm2 = [down1[0] + (KT // 2) * len(FF_CHUNKS), 2]
            hg = [norm2[0], norm2[1] + 1]
            ret = [hg[0] + HG0 * HG_HEADS, hg[1] + HG1 * HG_HEADS]
            norm3 = [ret[0] + RT0 * RET_HEADS, ret[1] + RT1 * RET_HEADS]
            norm4 = [norm3[0], norm3[1] + 1]

        def mix_free(pe, g, n):
            wait(pe, mixed[g], n)

        def load_ada(sp, m, slot, before):
            wait(sp, ada_read, before)
            sp.dma_start(ada_raw[:, slot, :], d["ada"][m]).then_inc(ada_loaded[slot], 16)

        def ada_tile(pe, g, col, slot, n_load):
            wait(pe, ada_loaded[slot], 16 * n_load)
            for k in range(KT):
                last = pe.matmul(mix_r[g][:, 2 * col:2 * col + 2], ada_raw[:, slot, k * P:(k + 1) * P],
                                 silu_c[:, k, :], start=(k == 0), stop=(k == KT - 1))
            last.then_inc(ada_read, 1)

        LAST = {1: "down12", 2: "wo", 3: "down22"}

        def residual_final(eng, n):
            if n == 0:
                wait(eng, in_x, 16)
            else:
                for p in range(2):
                    acc_read(eng, LAST[n], p, KT // 2 - 1)

        def norm_stats_act(act, n):
            residual_final(act, n)
            for k in range(KT):
                if k >= 2:
                    wait(act, sq_summed, KT * n + k - 1)
                act.activation(square[:, k % 2, :], x[:, k, :], ACT.Square).then_inc(sq_done, 1)
            wait(act, sq_summed, KT * (n + 1))
            act.activation(halves(root[:]), mix_v[1], ACT.Sqrt, bias=eps[:, 0:1],
                           scale=1.0 / D_MODEL).then_inc(mixed[1], 1)

        def norm_rows_act(act, n):
            for k in range(KT):
                wait(act, xn_done, KT * n + k + 1)
                if k >= 2:
                    wait(act, hlo_done, KT * n + k - 1)
                act.activation(h_full[:, k % 2, 0:CTX], x_norm[:, k % 2, 0:CTX], ACT.Identity,
                               bias=mod[:, 3 * n, k, 0:1], scale=mod[:, 3 * n + 1, k, 0:1])
                act.activation(h_full[:, k % 2, CTX:T], x_norm[:, k % 2, CTX:T], ACT.Identity,
                               bias=mod[:, 3 * n, k, 1:2], scale=mod[:, 3 * n + 1, k, 1:2]).then_inc(mod_done, 1)
                wait(act, mod_done, KT * n + k + 1)
                act.activation(h_hi[:, k, :], h_full[:, k % 2, :], ACT.Copy).then_inc(hhi_done, 1)

        def norm_pe(pe, n, use):
            mix_free(pe, 1, use)
            for k in range(KT):
                wait(pe, sq_done, KT * n + k + 1)
                for b in range(2):
                    last = pe.matmul(mix[1][:, b, 0:HT], ones[:], square[:, k % 2, b * HT:(b + 1) * HT],
                                     start=(k == 0), stop=(k == KT - 1))
                last.then_inc(sq_summed, 1)

        def norm_dve(dve, n, use):
            residual_final(dve, n)
            wait(dve, mixed[1], use + 1)
            dve.reciprocal(rstd[:], root[:]).then_inc(rstd_done, 1)
            wait(dve, rstd_done, n + 1)
            for k in range(KT):
                if n == 3:
                    dve.scalar_tensor_tensor(out=x[:, k, :], in0=x[:, k, :], scalar=small["final_w"][:, k:k + 1],
                                             in1=rstd[:], op0=ALU.mult, op1=ALU.mult).then_inc(xn_done, 1)
                    continue
                if k >= 2:
                    wait(dve, mod_done, KT * n + k - 1)
                dve.tensor_tensor(x_norm[:, k % 2, :], x[:, k, :], rstd[:], ALU.mult).then_inc(xn_done, 1)
                if k:
                    lo_part(dve, n, k - 1)
            if n < 3:
                lo_part(dve, n, KT - 1)

        def lo_part(dve, n, k):
            wait(dve, hhi_done, KT * n + k + 1)
            dve.tensor_tensor(h_lo[:, k, :], h_full[:, k % 2, :], h_hi[:, k, :].bitcast(F32),
                              ALU.subtract).then_inc(hlo_done, 1)

        def residual(dve, name, i, part):
            for p in range(2):
                g = ST.phase[name][2][p]
                projected(dve, name, p, i)
                tile = i * 2 + p
                for lo, hi, e in ((0, CTX, 0), (CTX, HT, 1), (HT, T, 1)):
                    src = acc[g][:, lo // HT, lo % HT:lo % HT + hi - lo]
                    last = dve.scalar_tensor_tensor(out=x[:, tile, lo:hi], in0=src, scalar=mod[:, part, tile, e:e + 1],
                                                    in1=x[:, tile, lo:hi], op0=ALU.mult, op1=ALU.add)
                last.then_inc(evacuated[g], 1)

        def up_act(act, f, c, base):
            name = f"up{f}{c}"
            with act.Fori(0, FF_CHUNKS[c]) as j:
                projected(act, name, 0, j)
                wait(act, evacuated[1], ST.uses(name, 1, j))
                act.activation(halves(gate_a[:]), acc_v[0], ACT.Silu).then_inc(evacuated[0], 1)
                acc_read(act, name, 1, j)
                act.activation(u_hi[:, j, :], u_full[:], ACT.Copy).then_inc(uhi_done, 1)

        def up_dve(dve, f, c, base):
            name = f"up{f}{c}"
            with dve.Fori(0, FF_CHUNKS[c]) as j:
                acc_read(dve, name, 0, j)
                projected(dve, name, 1, j)
                wait(dve, ulo_done, base + j + 1)
                dve.tensor_tensor(halves(u_full[:]), halves(gate_a[:]), acc_v[1], ALU.mult).then_inc(evacuated[1], 1)
                wait(dve, uhi_done, base + j + 1)
                dve.tensor_tensor(u_lo[:, j, :], u_full[:], u_hi[:, j, :].bitcast(F32),
                                  ALU.subtract).then_inc(ulo_done, 1)

        def ff_pe(pe, f, c, base):
            name = f"up{f}{c}"
            with pe.Fori(0, FF_CHUNKS[c]) as j:
                project(pe, name, 0, j, h_hi, h_lo)
                project(pe, name, 1, j, h_hi, h_lo)
            wait(pe, ulo_done, base + FF_CHUNKS[c] + 1)
            name = f"down{f}{c}"
            with pe.Fori(0, KT // 2) as i:
                project(pe, name, 0, i, u_hi, u_lo, FF_CHUNKS[c])
                project(pe, name, 1, i, u_hi, u_lo, FF_CHUNKS[c])
                if f == 1:
                    step = (KT // 2) * c + i
                    mix_free(pe, 0, Uses.down1[0] + step)
                    for s in range(ADA_SLOTS):
                        ada_tile(pe, 0, s, s, ADA_HEAD // ADA_SLOTS + step + 1)

        def u_base(f, c):
            return (f - 1) * (D_FF // P) + sum(FF_CHUNKS[:c])

        def ada_move(dve, tiles):
            count = ADA_SLOTS
            wait(dve, ada_read, ADA_SLOTS + tiles + count)
            out = mod[:].rearrange("p a k e -> p (a k) e")[:, bass.ds(tiles, count), :]
            bias = small["ada_b"][:, bass.ds(tiles, count)].unsqueeze(2).to_broadcast([P, count, 2])
            dve.tensor_tensor(out, mix_r[0][:, 0:2 * count].rearrange("p (m e) -> p m e", e=2), bias,
                              ALU.add).then_inc(mixed[0], 1)

        def make_scale(dve, n):
            wait(dve, mixed[0], Uses.down1[0] if n == 0 else Uses.norm2[0])
            sc = mod[:, 3 * n + 1, :, :]
            nw = small["norm_w"][:, KT * n:KT * (n + 1)].unsqueeze(2).to_broadcast([P, KT, 2])
            dve.tensor_scalar(sc, sc, 1.0, None, ALU.add).then_inc(coef_done, 1)
            wait(dve, coef_done, 3 * n + 1)
            dve.tensor_tensor(sc, sc, nw, ALU.mult).then_inc(coef_done, 1)
            g = mod[:, 3 * n + 2, :, :]
            dve.tensor_scalar(g, g, 1.0 if n == 1 else 0.5, None, ALU.mult).then_inc(coef_done, 1)

        def small_chain(dve):
            done = [0]

            def step(instruction):
                done[0] += 1
                instruction.then_inc(small_done, 1)
                dve.wait_ge(small_done, done[0])

            logits = small["lb"][:].rearrange("p (w l k) -> p w l k", w=2, l=2)
            top, e0, e1, total = (soft[:, n, :].rearrange("p (w k) -> p w k", w=2) for n in range(4))
            step(dve.tensor_tensor(top, logits[:, :, 0, :], logits[:, :, 1, :], ALU.max))
            step(dve.tensor_tensor(e0, logits[:, :, 0, :], top, ALU.subtract))
            step(dve.tensor_tensor(e1, logits[:, :, 1, :], top, ALU.subtract))
            y, u, log_u, diff, is_zero = (gam_tmp[:, n, :] for n in range(5))
            z = small["decay"][:]
            step(dve.scalar_tensor_tensor(out=y, in0=z, scalar=-1.0, in1=z, op0=ALU.mult, op1=ALU.max))
            dve.wait_ge(small_act, 1)
            step(dve.tensor_scalar(u, y, 1.0, None, ALU.add))
            step(dve.tensor_scalar(diff, u, -1.0, None, ALU.add))
            step(dve.tensor_scalar(is_zero, diff, 0.0, None, ALU.is_equal))
            step(dve.tensor_tensor(diff, diff, is_zero, ALU.add))
            step(dve.reciprocal(diff, diff))
            dve.wait_ge(small_act, 2)
            step(dve.tensor_tensor(log_u, log_u, y, ALU.mult))
            step(dve.tensor_tensor(log_u, log_u, diff, ALU.mult))
            step(dve.tensor_tensor(is_zero, is_zero, y, ALU.mult))
            step(dve.tensor_tensor(log_u, log_u, is_zero, ALU.add))
            step(dve.scalar_tensor_tensor(out=log_gam[:], in0=z, scalar=0.0, in1=log_u, op0=ALU.min, op1=ALU.subtract))
            step(dve.tensor_tensor(total, e0, e1, ALU.add))
            step(dve.reciprocal(total, total))
            step(dve.tensor_tensor(lb[:].rearrange("p (w k) -> p w k", w=2), e0, total, ALU.mult))
            step(dve.tensor_scalar(lb_rest[:], lb[:], -1.0, 1.0, ALU.mult, ALU.add))

        V_, F_, B_, Q_, O_ = range(5)
        hg_sig, hg_gate, hg_key, hg_query, hg_og = (sem("hg_" + n) for n in ("sig", "gate", "key", "query", "og"))
        hg_ln, hg_scan, hg_arg, hg_exp, hg_qk = (sem("hg_" + n) for n in ("ln", "scan", "arg", "exp", "qk"))
        hg_lev, hg_ktok, hg_kt, hg_kv, hg_state = (sem("hg_" + n) for n in ("lev", "ktok", "kt", "kv", "state"))
        hg_o, hg_osq, hg_ss, hg_rstd, hg_gated, hg_out = (sem("hg_" + n) for n in ("o", "osq", "ss", "rstd", "gated", "out"))
        hg_vt, hg_sin_ld, hg_dec, hg_fin, hg_att_done = (sem("hg_" + n) for n in ("vt", "sin", "dec", "fin", "att"))
        N_ARG = LEVELS + 2
        N_QK = LEVELS + 3

        def tiles5(ap):
            return ap.rearrange("p (c t) -> p c t", c=NT)

        def blocks(ap, u):
            return ap.rearrange("p (a i) -> p a i", i=2 << u)

        def hg_evac(act, h, p):
            projected(act, "hg", p, h)
            if p == V_:
                wait(act, hg_vt, h)
            if p in (F_, B_):
                wait(act, hg_sig, 6 * h)
            if p == Q_:
                wait(act, hg_query, h)
            if p == O_:
                wait(act, hg_og, h)
            g = ST.phase["hg"][2][p]
            act.activation(halves(pre[:, p, :]), acc_v[g], ACT.Copy).then_inc(evacuated[g], 1)

        def hg_act(act, m, h):
            wait(act, hg_out, m + 1)
            wait(act, hg_vt, m + 1)
            act.activation(v_tok[:].rearrange("p c t -> p (c t)"), mix_r[0][:, 0:T], ACT.Copy).then_inc(mixed[0], 1)
            act.dma_start(s_in[:], d["s_hg"][m]).then_inc(hg_sin_ld, 16)
            for n, (src, dst, sc) in enumerate(((F_, g_f, 1.0), (B_, g_b, 1.0), (F_, k_f, -1.0), (B_, k_b, -1.0),
                                                (Q_, q, 1.0), (O_, out_gate, 1.0))):
                acc_read(act, "hg", src, m)
                act.activation(dst[:], pre[:, src, :], ACT.Sigmoid, scale=sc).then_inc(hg_sig, 1)
            for n, g in enumerate((g_f, g_b)):
                wait(act, hg_gate, 2 * m + n + 1)
                act.activation(g[:], g[:], ACT.Ln, bias=lb[:, bass.ds(KT * n + m, 1)]).then_inc(hg_ln, 1)
            for u in range(LEVELS):
                wait(act, hg_arg, N_ARG * m + u + 1)
                act.activation(e_f[:, u % 2, :], e_f[:, u % 2, :], ACT.Exp)
                act.activation(e_b[:, u % 2, :], e_b[:, u % 2, :], ACT.Exp).then_inc(hg_exp, 1)
                if h is not None and u in (1, 3, 5, 6):
                    hg_evac(act, h, (1, 3, 5, 6).index(u))
            u = LEVELS
            wait(act, hg_arg, N_ARG * m + u + 1)
            act.activation(e_f[:, u % 2, :], e_f[:, u % 2, :], ACT.Exp)
            act.activation(e_b[:, u % 2, :], b_f[:], ACT.Exp).then_inc(hg_exp, 1)
            u = LEVELS + 1
            wait(act, hg_arg, N_ARG * m + u + 1)
            act.activation(e_f[:, u % 2, :], e_f[:, u % 2, :], ACT.Exp)
            act.activation(tiles5(e_b[:, u % 2, :]), p_b[:, :, 0:P], ACT.Exp).then_inc(hg_exp, 1)
            act.activation(s_dec[:, 0, :], tiles5(b_f[:])[:, :, P - 1], ACT.Exp)
            act.activation(s_dec[:, 1, :], p_b[:, :, P], ACT.Exp).then_inc(hg_dec, 1)
            if h is not None:
                hg_evac(act, h, O_)
            for n in range(2):
                wait(act, hg_ktok, 2 * m + n + 1)
                act.activation(k_tok[:, n].rearrange("p c t -> p (c t)"), mix_r[n][:, 0:4 * P],
                               ACT.Copy).then_inc(mixed[n], 1)
            wait(act, hg_fin, m + 1)
            act.dma_start(d["out_hg"][m], s_fin[:]).then_inc(states_out, 16)
            wait(act, hg_o, m + 1)
            act.activation(e_f[:, 0, :], mix_r[0][:, 0:T], ACT.Square).then_inc(hg_osq, 1)
            wait(act, hg_ss, m + 1)
            act.activation(halves(e_f[:, 1, :]), mix_v[1], ACT.Ln, bias=eps[:, 0:1], scale=1.0 / HG_DV).then_inc(mixed[1], 1)
            wait(act, mixed[1], Uses.hg[1] + HG1 * (m + 1))
            act.activation(e_b[:, 1, :], e_f[:, 1, :], ACT.Exp, scale=-0.5).then_inc(hg_rstd, 1)

        def hg_arguments(dve, m, u):
            f, b, half = e_f[:, u % 2, :], e_b[:, u % 2, :], 1 << u
            if u >= 2:
                wait(dve, hg_qk, N_QK * m + u)
            if u < LEVELS:
                fb, src = blocks(f, u), blocks(b_f[:], u)
                na = T // (2 * half)
                mid = src[:, :, half - 1:half].to_broadcast([P, na, half])
                dve.tensor_tensor(fb[:, :, 0:half], mid, src[:, :, 0:half], ALU.subtract)
                dve.tensor_tensor(fb[:, :, half:], src[:, :, half:], mid, ALU.subtract)
                nb = P // (2 * half)
                bb = b.rearrange("p (c a i) -> p c a i", c=NT, a=nb)
                src = p_b[:, :, 0:P].rearrange("p c (a i) -> p c a i", a=nb)
                mid = src[:, :, :, half:half + 1].to_broadcast([P, NT, nb, half])
                dve.tensor_tensor(bb[:, :, :, 0:half], mid, src[:, :, :, 0:half], ALU.subtract)
                dve.tensor_tensor(bb[:, :, :, half:], src[:, :, :, half:], mid, ALU.subtract).then_inc(hg_arg, 1)
            elif u == LEVELS:
                last = tiles5(b_f[:])[:, :, P - 1:P].to_broadcast([P, NT, P])
                dve.tensor_tensor(tiles5(f), last, tiles5(b_f[:]), ALU.subtract).then_inc(hg_arg, 1)
            else:
                last = p_b[:, :, P:P + 1].to_broadcast([P, NT, P])
                dve.tensor_tensor(tiles5(f), last, p_b[:, :, 0:P], ALU.subtract).then_inc(hg_arg, 1)

        def hg_operands(dve, m, u):
            s, half = u % 2, 1 << u
            wait(dve, hg_exp, N_ARG * m + u + 1)
            if u >= 1:
                wait(dve, hg_lev, (LEVELS + 1) * m + u)
            if u < LEVELS:
                fb, bb = blocks(e_f[:, s, :], u), blocks(e_b[:, s, :], u)
                qb, kb_ = blocks(q_lev[:, s, :], u), blocks(k_lev[:, s, :], u)
                first, second = slice(0, half), slice(half, 2 * half)
                dve.tensor_tensor(kb_[:, :, first], blocks(k_f[:], u)[:, :, first], fb[:, :, first], ALU.mult)
                dve.tensor_tensor(qb[:, :, second], blocks(q[:], u)[:, :, second], fb[:, :, second], ALU.mult)
                dve.tensor_tensor(qb[:, :, first], blocks(q[:], u)[:, :, first], bb[:, :, first], ALU.mult)
                dve.tensor_tensor(kb_[:, :, second], blocks(k_b[:], u)[:, :, second], bb[:, :, second],
                                  ALU.mult).then_inc(hg_qk, 1)
            elif u == LEVELS:
                dve.tensor_tensor(k_lev[:, s, :], k_f[:], e_f[:, s, :], ALU.mult)
                dve.tensor_tensor(q_lev[:, s, :], q[:], e_b[:, s, :], ALU.mult).then_inc(hg_qk, 1)
            else:
                dve.tensor_tensor(k_lev[:, s, :], k_b[:], e_b[:, s, :], ALU.mult)
                dve.tensor_tensor(q_lev[:, s, :], q[:], e_f[:, s, :], ALU.mult).then_inc(hg_qk, 1)

        def hg_score_read(dve, m, u):
            wait(dve, hg_lev, (LEVELS + 1) * m + u + 1)
            flat = att[:].rearrange("p c t -> p (c t)")
            if u == 0:
                dve.tensor_copy(flat, mix_r[0][:, 0:T]).then_inc(mixed[0], 1)
            else:
                g, before = (u - 1) % 2, (u - 1) // 2
                wait(dve, mixed[g], (Uses.hg[0] + HG0 * m + 2 if g == 0 else Uses.hg[1] + HG1 * m + 1) + before)
                mask = masks[:, u - 1, :].unsqueeze(1).to_broadcast([P, NT, P])
                dve.sem_inc(dve_waited, 1)
                dve.copy_predicated(att[:], mask, tiles5(mix_r[u % 2][:, 0:T])).then_inc(mixed[u % 2], 1)

        def hg_dve(dve, m):
            wait(dve, hg_out, m + 1)
            for n, g in enumerate((g_f, g_b)):
                wait(dve, hg_sig, 6 * m + n + 1)
                dve.tensor_scalar(g[:], g[:], TINY, lb_rest[:, bass.ds(KT * n + m, 1)], ALU.max, ALU.mult).then_inc(hg_gate, 1)
            for n, k in enumerate((k_f, k_b)):
                wait(dve, hg_sig, 6 * m + n + 3)
                dve.tensor_scalar(k[:], k[:], lb_rest[:, bass.ds(KT * n + m, 1)], None, ALU.mult).then_inc(hg_key, 1)
            wait(dve, hg_sig, 6 * m + 5)
            dve.scalar_tensor_tensor(out=q[:], in0=pre[:, Q_, :], scalar=float(HG_DK) ** -0.5, in1=q[:],
                                     op0=ALU.mult, op1=ALU.mult).then_inc(hg_query, 1)
            wait(dve, hg_sig, 6 * m + 6)
            dve.tensor_tensor(out_gate[:], pre[:, O_, :], out_gate[:], ALU.mult).then_inc(hg_og, 1)
            wait(dve, hg_key, 2 * m + 2)
            dve.tensor_tensor(k_lev[:, 1, :], k_f[:], k_b[:], ALU.add).then_inc(hg_qk, 1)
            for n, g in enumerate((g_f, g_b)):
                wait(dve, hg_ln, 2 * m + n + 1)
                for c in range(NT):
                    out = b_f[:, c * P:(c + 1) * P] if n == 0 else p_b[:, c, 1:P + 1]
                    last = dve.tensor_tensor_scan(out, ones[:], g[:, c * P:(c + 1) * P], 0.0, ALU.mult, ALU.add)
                last.then_inc(hg_scan, 1)
            wait(dve, hg_scan, 2 * m + 2)
            wait(dve, hg_query, m + 1)
            hg_arguments(dve, m, 0)
            for u in range(LEVELS):
                hg_arguments(dve, m, u + 1)
                hg_operands(dve, m, u)
                hg_score_read(dve, m, u)
            hg_arguments(dve, m, LEVELS + 1)
            hg_score_read(dve, m, LEVELS)
            hg_operands(dve, m, LEVELS)
            hg_operands(dve, m, LEVELS + 1)
            wait(dve, hg_dec, m + 1)
            wait(dve, hg_sin_ld, 16 * (m + 1))
            wait(dve, hg_kv, 2 * m + 2)
            wait(dve, states_out, 16 * (m + 1))
            dve.tensor_copy(s_fin[:, 0, :], mix[0][:, 1, 0:P])
            dve.tensor_copy(s_fin[:, 1, :], mix[1][:, 1, 0:P]).then_inc(hg_fin, 1)
            for n in range(3):
                for w in range(2):
                    tile = 1 + n if w == 0 else 4 - n
                    kv = mix[w][:, 1, (1 + n) * P:(2 + n) * P] if w == 0 else mix[w][:, 1, (3 - n) * P:(4 - n) * P]
                    old = s_in[:, w, :] if n == 0 else s_run[:, w, n - 1, :]
                    if n:
                        wait(dve, hg_state, 6 * m + 2 * (n - 1) + w + 1)
                    last = dve.scalar_tensor_tensor(out=s_run[:, w, n, :], in0=old, scalar=s_dec[:, w, tile:tile + 1],
                                                    in1=kv, op0=ALU.mult, op1=ALU.add)
                    last.then_inc(hg_state, 1)
            wait(dve, hg_o, m + 1)
            wait(dve, hg_osq, m + 1)
            dve.scalar_tensor_tensor(out=e_b[:, 0, :], in0=mix_r[0][:, 0:T], scalar=small["hg_w"][:, bass.ds(m, 1)],
                                     in1=out_gate[:], op0=ALU.mult, op1=ALU.mult).then_inc(mixed[0], 1)
            wait(dve, mixed[0], Uses.hg[0] + HG0 * (m + 1))
            wait(dve, hg_rstd, m + 1)
            dve.tensor_tensor(o_hg[:, m, :], e_b[:, 0, :], e_b[:, 1, :], ALU.mult).then_inc(hg_out, 1)

        def hg_vt_pe(pe, m):
            acc_read(pe, "hg", V_, m)
            mix_free(pe, 0, Uses.hg[0] + HG0 * m)
            for c in range(NT):
                last = pe.transpose(mix_r[0][:, c * P:(c + 1) * P], pre[:, V_, c * P:(c + 1) * P], ident[:])
            last.then_inc(hg_vt, 1)

        def hg_unit_pe(pe, m, u):
            wait(pe, hg_qk, N_QK * m + u + 1)
            if u == 0:
                wait(pe, hg_query, m + 1)
            g = u % 2
            mix_free(pe, g, (Uses.hg[0] + HG0 * m + 1 + u // 2) if g == 0 else (Uses.hg[1] + HG1 * m + u // 2))
            ks, qs = (k_lev[:, 1, :], q[:]) if u == 0 else (k_lev[:, (u - 1) % 2, :], q_lev[:, (u - 1) % 2, :])
            for c in range(NT):
                cols = slice(c * P, (c + 1) * P)
                last = pe.matmul(mix_r[g][:, cols], ks[:, cols], qs[:, cols], start=True, stop=True)
            last.then_inc(hg_lev, 1)

        def hg_post_pe(pe, m):
            u0, u1 = Uses.hg[0] + HG0 * m, Uses.hg[1] + HG1 * m
            tiles = ((0, 1, 2, 3), (0, 2, 3, 4))
            for w in range(2):
                wait(pe, hg_qk, N_QK * m + N_QK - 1 + w)
                mix_free(pe, w, (u0 + 5, u1 + 4)[w])
                for j, c in enumerate(tiles[w]):
                    last = pe.transpose(mix_r[w][:, j * P:(j + 1) * P], k_lev[:, (LEVELS + w) % 2, c * P:(c + 1) * P], ident[:])
                last.then_inc(hg_ktok, 1)
            for w in range(2):
                mix_free(pe, w, (u0 + 6, u1 + 5)[w])
                for j, c in enumerate(tiles[w]):
                    last = pe.matmul(mix[w][:, 1, j * P:(j + 1) * P], k_tok[:, w, j, :], v_tok[:, c, :], start=True, stop=True)
                last.then_inc(hg_kv, 1)
            wait(pe, hg_state, 6 * m + 6)
            wait(pe, mixed[1], u1 + 4)
            for c in range(NT):
                cols = slice(c * P, (c + 1) * P)
                last = pe.matmul(mix_r[0][:, cols], v_tok[:, c, :], att[:, c, :], start=True, stop=(c == 0))
                if c:
                    for w in range(2):
                        n = c - 1 if w == 0 else 4 - c
                        st = s_in[:, w, :] if n == 0 else s_run[:, w, n - 1, :]
                        last = pe.matmul(mix_r[0][:, cols], st, q_lev[:, (LEVELS + w) % 2, cols], start=False, stop=(w == 1))
            last.then_inc(hg_o, 1)
            wait(pe, hg_osq, m + 1)
            for b in range(2):
                last = pe.matmul(mix[1][:, b, 0:HT], ones[:], e_f[:, 0, b * HT:(b + 1) * HT], start=True, stop=True)
            last.then_inc(hg_ss, 1)

        K_, Q2_, V0_, V1_, G0_, G1_ = range(6)
        rt_rot, rt_tmp, rt_kq, rt_sc, rt_att = (sem("ret_" + n) for n in ("rot", "tmp", "kq", "scores", "att"))
        rt_kt, rt_ktok, rt_kv, rt_qdec, rt_state = (sem("ret_" + n) for n in ("kt", "ktok", "kv", "qdec", "state"))
        rt_o, rt_osq, rt_ss, rt_ln, rt_rstd, rt_out = (sem("ret_" + n) for n in ("o", "osq", "ss", "ln", "rstd", "out"))
        rt_vt, rt_sin_ld, rt_fin, rt_dmat, rt_exp = (sem("ret_" + n) for n in ("vt", "sin", "fin", "dmat", "exp"))
        tab_in, masks_in = sem("tab_in"), sem("masks_in")

        def ret_tables_act(act):
            wait(act, hg_out, HG_HEADS + 1)
            wait(act, states_out, 16 * (HG_HEADS + 1))
            for n, (dst, src) in enumerate(((cos[:], d["cos"]), (sin[:], d["sin"]), (dist, d["dist"]), (upper, d["upper"]),
                                            (lower, d["lower"]), (rows, d["rows"].rearrange("p (d t) -> p d t", d=2)))):
                act.dma_start(dst, src).then_inc(tab_in, 16)
            wait(act, tab_in, 16 * 6)
            for n in range(RET_HEADS):
                for w in range(2):
                    col = RET_HEADS * w + n
                    act.activation(q_rows[:, col, :], rows[:, w, :], ACT.Exp, scale=log_gam[:, col:col + 1])
                wait(act, rt_dmat, n)
                act.activation(e_mat[:, 0, :], dist, ACT.Exp, scale=log_gam[:, n:n + 1])
                act.activation(e_mat[:, 1, :], dist, ACT.Exp, scale=log_gam[:, RET_HEADS + n:RET_HEADS + n + 1]).then_inc(rt_exp, 1)

        def ret_tables_dve(dve):
            for n in range(RET_HEADS):
                wait(dve, rt_exp, n + 1)
                dve.tensor_tensor(r_tmp[:, 1, 2 * P:3 * P], e_mat[:, 0, :], upper, ALU.mult)
                dve.tensor_tensor(r_tmp[:, 1, 3 * P:4 * P], e_mat[:, 1, :], lower, ALU.mult).then_inc(rt_tmp, 1)
                wait(dve, rt_tmp, n + 1)
                dve.tensor_tensor(d_mat[:, n, :], r_tmp[:, 1, 2 * P:3 * P], r_tmp[:, 1, 3 * P:4 * P], ALU.add).then_inc(rt_dmat, 1)

        def ret_evac(act, h, p):
            projected(act, "ret", p, h)
            if p in (K_, Q2_):
                wait(act, rt_kq, 2 * h)
            elif p in (V0_, V1_):
                wait(act, rt_vt, 2 * h)
            else:
                wait(act, rt_out, 2 * h + 1)
            g = ST.phase["ret"][2][p]
            func, scale = (ACT.Silu if p >= G0_ else ACT.Copy), (float(RET_DK) ** -0.5 if p == K_ else 1.0)
            act.activation(halves(r_pre[:, p, :]), acc_v[g], func, scale=scale).then_inc(evacuated[g], 1)

        def ret_act(act, m, h):
            wait(act, rt_out, 2 * m + 1)
            for e in range(2):
                wait(act, rt_vt, 2 * m + e + 1)
                act.activation(r_v[:, :, e, :], tiles5(mix_r[e][:, 0:T]), ACT.Copy).then_inc(mixed[e], 1)
            act.dma_start(r_sin[:], d["s_ret"][m]).then_inc(rt_sin_ld, 16)
            if h is not None:
                for p in range(3):
                    ret_evac(act, h, p)
            wait(act, rt_fin, m + 1)
            act.dma_start(d["out_ret"][m], r_sfin[:]).then_inc(states_out, 16)
            for e in range(2):
                wait(act, rt_o, 2 * m + e + 1)
                act.activation(r_tmp[:, e, :], mix_r[e][:, 0:T], ACT.Square).then_inc(rt_osq, 1)
            if h is not None:
                ret_evac(act, h, V1_)
            wait(act, rt_ss, m + 1)
            act.activation(halves(r_tmp[:, 0, :]), mix_v[0], ACT.Ln, bias=eps[:, 0:1], scale=1.0 / RET_DV).then_inc(mixed[0], 1)
            wait(act, mixed[0], Uses.ret[0] + RT0 * (m + 1))
            act.activation(r_tmp[:, 1, :], r_tmp[:, 0, :], ACT.Exp, scale=-0.5).then_inc(rt_rstd, 1)
            if h is not None:
                for p in range(4, 6):
                    ret_evac(act, h, p)

        def ret_dve(dve, m):
            wait(dve, rt_out, 2 * m + 1)
            for w, (p, dst) in enumerate(((K_, 0), (Q2_, 1))):
                wait(dve, rt_rot, 2 * m + w + 1)
                dve.tensor_tensor(halves(r_tmp[:, w, :]), mix_v[w], halves(sin[:]), ALU.mult).then_inc(mixed[w], 1)
                acc_read(dve, "ret", p, m)
                dve.tensor_tensor(r_rot[:, dst, :], r_pre[:, p, :], cos[:], ALU.mult).then_inc(rt_tmp, 1)
                wait(dve, rt_tmp, RET_HEADS + 2 * m + w + 1)
                wait(dve, mixed[w], (Uses.ret[w] + (RT0, RT1)[w] * m + 2))
                dve.tensor_tensor(r_rot[:, dst, :], r_rot[:, dst, :], r_tmp[:, w, :], ALU.add).then_inc(rt_kq, 1)
            wait(dve, rt_kq, 2 * m + 2)
            for w in range(2):
                row = q_rows[:, bass.ds(RET_HEADS * w + m, 1), :].to_broadcast([P, 4, P])
                dve.tensor_tensor(r_qdec[:, w, :].rearrange("p (c t) -> p c t", c=4),
                                  r_rot[:, 1, CTX:T].rearrange("p (c t) -> p c t", c=4), row, ALU.mult).then_inc(rt_qdec, 1)
            wait(dve, rt_sc, m + 1)
            wait(dve, rt_dmat, RET_HEADS)
            dve.tensor_tensor(r_att[:], tiles5(mix_r[0][:, 0:T]), d_mat[:, bass.ds(m, 1), :].to_broadcast([P, NT, P]),
                              ALU.mult).then_inc(mixed[0], 1)
            wait(dve, rt_kt, m + 1)
            kt5 = tiles5(mix_r[1][:, 0:T])
            dve.tensor_scalar(r_ktok[:, 0], kt5[:, 0:4, :], k_decay[:, bass.ds(m, 1)], None, ALU.mult)
            dve.tensor_scalar(r_ktok[:, 1, 0, :], kt5[:, 0, :], k_decay[:, bass.ds(RET_HEADS + m, 1)], None, ALU.mult)
            dve.tensor_scalar(r_ktok[:, 1, 1:4, :], kt5[:, 2:5, :], k_decay[:, bass.ds(RET_HEADS + m, 1)], None,
                              ALU.mult).then_inc(mixed[1], 1)
            wait(dve, rt_kv, 2 * m + 2)
            wait(dve, states_out, 16 * (HG_HEADS + m + 1))
            wait(dve, rt_sin_ld, 16 * (m + 1))
            dve.tensor_copy(r_sfin[:, 0, :], mix_r[0][:, 0:RET_DV])
            dve.tensor_copy(r_sfin[:, 1, :], mix_r[1][:, 0:RET_DV]).then_inc(rt_fin, 1)
            for n in range(3):
                for w in range(2):
                    j = 1 + n if w == 0 else 3 - n
                    kv = mix_r[w][:, j * RET_DV:(j + 1) * RET_DV]
                    old = r_sin[:, w, :] if n == 0 else r_srun[:, w, n - 1, :]
                    if n:
                        wait(dve, rt_state, 6 * m + 2 * (n - 1) + w + 1)
                    dve.scalar_tensor_tensor(out=r_srun[:, w, n, :], in0=old,
                                             scalar=c_decay[:, bass.ds(RET_HEADS * w + m, 1)],
                                             in1=kv, op0=ALU.mult, op1=ALU.add).then_inc(rt_state, 1)
            for e in range(2):
                wait(dve, rt_osq, 2 * m + e + 1)
                acc_read(dve, "ret", G0_ + e, m)
                dve.tensor_tensor(r_pre[:, G0_ + e, :], mix_r[e][:, 0:T], r_pre[:, G0_ + e, :], ALU.mult).then_inc(mixed[e], 1)
            wait(dve, mixed[1], Uses.ret[1] + RT1 * (m + 1))
            wait(dve, mixed[0], Uses.ret[0] + RT0 * (m + 1))
            wait(dve, rt_rstd, m + 1)
            for e in range(2):
                dve.tensor_tensor(o_ret[:, m * 2 + e, :], r_pre[:, G0_ + e, :], r_tmp[:, 1, :], ALU.mult).then_inc(rt_out, 1)

        def ret_vt_pe(pe, m):
            for e in range(2):
                acc_read(pe, "ret", V0_ + e, m)
                mix_free(pe, e, Uses.ret[e] + (RT0, RT1)[e] * m)
                for c in range(NT):
                    last = pe.transpose(mix_r[e][:, c * P:(c + 1) * P], r_pre[:, V0_ + e, c * P:(c + 1) * P], ident[:])
                last.then_inc(rt_vt, 1)

        def ret_rot_pe(pe, m):
            for w, p in enumerate((K_, Q2_)):
                acc_read(pe, "ret", p, m)
                mix_free(pe, w, Uses.ret[w] + (RT0, RT1)[w] * m + 1)
                for b in range(2):
                    last = pe.matmul(mix[w][:, b, 0:HT], perm[:], r_pre[:, p, b * HT:(b + 1) * HT], start=True, stop=True)
                last.then_inc(rt_rot, 1)

        def ret_scores_pe(pe, m):
            wait(pe, rt_kq, 2 * m + 2)
            mix_free(pe, 0, Uses.ret[0] + RT0 * m + 2)
            for c in range(NT):
                cols = slice(c * P, (c + 1) * P)
                last = pe.matmul(mix_r[0][:, cols], r_rot[:, 0, cols], r_rot[:, 1, cols], start=True, stop=True)
            last.then_inc(rt_sc, 1)
            mix_free(pe, 1, Uses.ret[1] + RT1 * m + 2)
            for c in range(NT):
                cols = slice(c * P, (c + 1) * P)
                last = pe.transpose(mix_r[1][:, cols], r_rot[:, 0, cols], ident[:])
            last.then_inc(rt_kt, 1)

        def ret_kv_pe(pe, m):
            tiles = ((0, 1, 2, 3), (0, 2, 3, 4))
            for w in (1, 0):
                mix_free(pe, 1, Uses.ret[1] + RT1 * m + 3)
                if w == 0:
                    mix_free(pe, 0, Uses.ret[0] + RT0 * m + 3)
                for j, c in enumerate(tiles[w]):
                    last = pe.matmul(mix_r[w][:, j * RET_DV:(j + 1) * RET_DV], r_ktok[:, w, j, :],
                                     r_v[:, c].rearrange("p e t -> p (e t)"), start=True, stop=True)
                last.then_inc(rt_kv, 1)

        def ret_out_pe(pe, m):
            wait(pe, rt_qdec, 2 * m + 2)
            wait(pe, rt_state, 6 * m + 6)
            for e in range(2):
                dv = slice(e * P, (e + 1) * P)
                for c in range(NT):
                    cols, lat = slice(c * P, (c + 1) * P), slice((c - 1) * P, c * P)
                    last = pe.matmul(mix_r[e][:, cols], r_v[:, c, e, :], r_att[:, c, :], start=True, stop=(c == 0))
                    if c:
                        for w in range(2):
                            n = c - 1 if w == 0 else 4 - c
                            st = r_sin[:, w, dv] if n == 0 else r_srun[:, w, n - 1, dv]
                            last = pe.matmul(mix_r[e][:, cols], st, r_qdec[:, w, lat], start=False, stop=(w == 1))
                last.then_inc(rt_o, 1)

        def ret_ss_pe(pe, m):
            wait(pe, rt_osq, 2 * m + 2)
            mix_free(pe, 0, Uses.ret[0] + RT0 * m + 4)
            for b in range(2):
                for e in range(2):
                    last = pe.matmul(mix[0][:, b, 0:HT], ones[:], r_tmp[:, e, b * HT:(b + 1) * HT],
                                     start=(e == 0), stop=(e == 1))
            last.then_inc(rt_ss, 1)

        part_hi, part_lo = sem("part_hi"), sem("part_lo")
        merge_done = sem("merge_done")

        block = ctx.enter_context(nc.Block())

        @block.sync
        def _(sp):
            for n, w in C_NAMES:
                sp.dma_start(small[n][:], d["in_" + n]).then_inc(in_small, 16)
            sp.dma_start(x[:], d["x"]).then_inc(in_x, 16)
            sp.dma_start(ident[:], d["ident"]).then_inc(in_tab, 16)
            sp.dma_start(perm[:], d["perm"]).then_inc(in_tab, 16)
            with sp.Fori(0, ADA_HEAD // ADA_SLOTS) as i:
                for s in range(ADA_SLOTS):
                    load_ada(sp, i * ADA_SLOTS + s, s, i * ADA_SLOTS + s + 1)
            for f in (1, 2):
                if f == 2:
                    for name in ("hg", "ret", "gate", "wo"):
                        steps, slots, _, _, _, _ = ST.phase[name]
                        with sp.Fori(0, steps) as i:
                            for p in range(len(slots)):
                                load_slab(sp, name, p, i)
                for c in range(len(FF_CHUNKS)):
                    with sp.Fori(0, FF_CHUNKS[c]) as i:
                        for p in range(2):
                            load_slab(sp, f"up{f}{c}", p, i)
                    with sp.Fori(0, KT // 2) as i:
                        for p in range(2):
                            load_slab(sp, f"down{f}{c}", p, i)
                        if f == 1:
                            for s in range(ADA_SLOTS):
                                m = ADA_HEAD + ((KT // 2) * c + i) * ADA_SLOTS + s
                                load_ada(sp, m, s, m + 1)
            for k in range(KT):
                wait(sp, xn_done, 3 * KT + k + 1)
                sp.dma_start(d["y"][:, k, :], x[:, k, :]).then_inc(y_out, 16)
            sp.wait_ge(y_out, 16 * KT)
            sp.wait_ge(states_out, 16 * (HG_HEADS + RET_HEADS + 1))

        @block.gpsimd
        def _(pool):
            pool.sem_inc(split_done, CREDIT)
            for name, steps, slots, _ in PHASES:
                with pool.Fori(0, steps) as i:
                    for p in range(len(slots)):
                        split_slab(pool, name, p, i)

        @block.tensor
        def _(pe):
            pe.sem_inc(slab_done, CREDIT)
            pe.sem_inc(evacuated[0], 1)
            pe.sem_inc(evacuated[1], 1)
            pe.sem_inc(ada_read, ADA_SLOTS)
            pe.sem_inc(mixed[0], 1)
            pe.sem_inc(mixed[1], 1)
            pe.wait_ge(ones_set, 1)
            norm_pe(pe, 0, Uses.norm1[1])
            pe.wait_ge(silu_done, 2)
            with pe.Fori(0, ADA_HEAD // ADA_SLOTS) as i:
                mix_free(pe, 0, Uses.ada_head[0] + i)
                for s in range(ADA_SLOTS):
                    ada_tile(pe, 0, s, s, i + 1)
            pe.wait_ge(hlo_done, KT)
            for c in range(len(FF_CHUNKS)):
                ff_pe(pe, 1, c, u_base(1, c))
            norm_pe(pe, 1, Uses.norm2[1])
            pe.wait_ge(hlo_done, 2 * KT)
            pe.wait_ge(in_tab, 32)
            for p in range(5):
                project(pe, "hg", p, 0, h_hi, h_lo)
            hg_vt_pe(pe, 0)
            with pe.Fori(1, HG_HEADS) as h:
                project(pe, "hg", 0, h, h_hi, h_lo)
                for p in range(1, 5):
                    project(pe, "hg", p, h, h_hi, h_lo)
                    hg_unit_pe(pe, h - 1, 2 * p - 2)
                    hg_unit_pe(pe, h - 1, 2 * p - 1)
                hg_post_pe(pe, h - 1)
                hg_vt_pe(pe, h)
            for u in range(LEVELS + 1):
                hg_unit_pe(pe, HG_HEADS - 1, u)
            hg_post_pe(pe, HG_HEADS - 1)
            for p in range(6):
                project(pe, "ret", p, 0, h_hi, h_lo)
            ret_vt_pe(pe, 0)
            with pe.Fori(1, RET_HEADS) as h:
                ret_rot_pe(pe, h - 1)
                project(pe, "ret", 0, h, h_hi, h_lo)
                ret_scores_pe(pe, h - 1)
                project(pe, "ret", 1, h, h_hi, h_lo)
                ret_kv_pe(pe, h - 1)
                project(pe, "ret", 2, h, h_hi, h_lo)
                ret_out_pe(pe, h - 1)
                project(pe, "ret", 3, h, h_hi, h_lo)
                ret_ss_pe(pe, h - 1)
                project(pe, "ret", 4, h, h_hi, h_lo)
                project(pe, "ret", 5, h, h_hi, h_lo)
                ret_vt_pe(pe, h)
            m = RET_HEADS - 1
            ret_rot_pe(pe, m)
            ret_scores_pe(pe, m)
            ret_kv_pe(pe, m)
            ret_out_pe(pe, m)
            ret_ss_pe(pe, m)
            with pe.Fori(0, KT) as n:
                project(pe, "gate", 0, n, h_hi, h_lo)
                project(pe, "gate", 1, n, h_hi, h_lo)
                pe.wait_ge(part_lo, 2 * KT)
                project(pe, "gate", 2, n, ret_hi, ret_lo)
                project(pe, "gate", 3, n, hg_hi, hg_lo)
            pe.wait_ge(part_lo, 3 * KT)
            with pe.Fori(0, KT // 2) as i:
                project(pe, "wo", 0, i, h_hi, h_lo)
                project(pe, "wo", 1, i, h_hi, h_lo)
            norm_pe(pe, 2, Uses.norm3[1])
            pe.wait_ge(hlo_done, 3 * KT)
            for c in range(len(FF_CHUNKS)):
                ff_pe(pe, 2, c, u_base(2, c))
            norm_pe(pe, 3, Uses.norm4[1])

        @block.scalar
        def _(act):
            act.wait_ge(in_small, 16 * len(C_NAMES))
            act.activation(silu_c[:].rearrange("p k e -> p (k e)"), small["c"][:], ACT.Sigmoid).then_inc(silu_done, 1)
            act.sem_inc(states_out, 16)
            act.wait_ge(small_done, 4)
            act.activation(soft[:, 1, :], soft[:, 1, :], ACT.Exp)
            act.activation(soft[:, 2, :], soft[:, 2, :], ACT.Exp)
            act.activation(gam_tmp[:, 0, :], gam_tmp[:, 0, :], ACT.Exp, scale=-1.0).then_inc(small_act, 1)
            act.wait_ge(small_done, 5)
            act.activation(gam_tmp[:, 2, :], gam_tmp[:, 1, :], ACT.Ln).then_inc(small_act, 1)
            act.wait_ge(small_done, 14)
            for w in range(2):
                cols = slice(RET_HEADS * w, RET_HEADS * (w + 1))
                act.activation(k_decay[:, cols], log_gam[:, cols], ACT.Exp, scale=small["kpos"][:, w:w + 1])
            act.activation(c_decay[:], log_gam[:], ACT.Exp, scale=float(P))
            norm_stats_act(act, 0)
            act.wait_ge(coef_done, 3)
            norm_rows_act(act, 0)
            for c in range(len(FF_CHUNKS)):
                up_act(act, 1, c, u_base(1, c))
            norm_stats_act(act, 1)
            act.wait_ge(coef_done, 9)
            norm_rows_act(act, 1)
            act.wait_ge(hlo_done, 2 * KT)
            act.dma_start(masks[:].rearrange("p u t -> p (u t)"), d["masks"]).then_inc(masks_in, 16)
            for p in range(5):
                hg_evac(act, 0, p)
            with act.Fori(1, HG_HEADS) as h:
                hg_act(act, h - 1, h)
            hg_act(act, HG_HEADS - 1, None)
            ret_tables_act(act)
            act.wait_ge(rt_dmat, RET_HEADS)
            for p in range(6):
                ret_evac(act, 0, p)
            with act.Fori(1, RET_HEADS) as h:
                ret_act(act, h - 1, h)
            ret_act(act, RET_HEADS - 1, None)
            act.wait_ge(rt_out, 2 * RET_HEADS + 1)
            act.wait_ge(states_out, 16 * (HG_HEADS + RET_HEADS + 1))
            for src, dst in ((o_ret, ret_hi), (o_hg, hg_hi)):
                for k in range(KT):
                    act.activation(dst[:, k, :], src[:, k, :], ACT.Copy).then_inc(part_hi, 1)
            with act.Fori(0, KT) as n:
                for p in range(2):
                    projected(act, "gate", p, n)
                    act.wait_ge(merge_done, n + 1)
                    act.activation(halves(sig_buf[:, p, :]), acc_v[p], ACT.Sigmoid).then_inc(evacuated[p], 1)
            act.wait_ge(merge_done, KT + 1)
            for k in range(KT):
                act.activation(h_hi[:, k, :], merged[:, k, :], ACT.Copy).then_inc(part_hi, 1)
            norm_stats_act(act, 2)
            norm_rows_act(act, 2)
            for c in range(len(FF_CHUNKS)):
                up_act(act, 2, c, u_base(2, c))
            norm_stats_act(act, 3)

        @block.vector
        def _(dve):
            for credited, n in ((ulo_done, 1), (hg_out, 1), (rt_out, 1), (merge_done, 1)):
                dve.sem_inc(credited, n)
            dve.memset(eps[:], EPS)
            dve.memset(ones[:], 1.0).then_inc(ones_set, 1)
            dve.wait_ge(in_small, 16 * len(C_NAMES))
            dve.wait_ge(silu_done, 1)
            dve.tensor_tensor(silu_c[:].rearrange("p k e -> p (k e)"), small["c"][:],
                              silu_c[:].rearrange("p k e -> p (k e)"), ALU.mult).then_inc(silu_done, 1)
            small_chain(dve)
            with dve.Fori(0, ADA_HEAD // ADA_SLOTS) as i:
                ada_move(dve, i * ADA_SLOTS)
            make_scale(dve, 0)
            norm_dve(dve, 0, Uses.norm1[1])
            for c in range(len(FF_CHUNKS)):
                up_dve(dve, 1, c, u_base(1, c))
                with dve.Fori(0, KT // 2) as i:
                    residual(dve, f"down1{c}", i, G1)
                    ada_move(dve, ADA_HEAD + ((KT // 2) * c + i) * ADA_SLOTS)
            make_scale(dve, 1)
            make_scale(dve, 2)
            norm_dve(dve, 1, Uses.norm2[1])
            dve.memset(p_b[:, :, 0:1], 0.0)
            dve.wait_ge(masks_in, 16)
            with dve.Fori(1, HG_HEADS) as h:
                hg_dve(dve, h - 1)
            hg_dve(dve, HG_HEADS - 1)
            ret_tables_dve(dve)
            with dve.Fori(1, RET_HEADS) as h:
                ret_dve(dve, h - 1)
            ret_dve(dve, RET_HEADS - 1)
            for n, (src, hi, lo) in enumerate(((o_ret, ret_hi, ret_lo), (o_hg, hg_hi, hg_lo))):
                for k in range(KT):
                    dve.wait_ge(part_hi, KT * n + k + 1)
                    dve.tensor_tensor(lo[:, k, :], src[:, k, :], hi[:, k, :].bitcast(F32), ALU.subtract).then_inc(part_lo, 1)
            with dve.Fori(0, KT) as n:
                for p in range(2):
                    acc_read(dve, "gate", p, n)
                    projected(dve, "gate", 2 + p, n)
                    dve.tensor_tensor(halves(sig_buf[:, p, :]), halves(sig_buf[:, p, :]), acc_v[p],
                                      ALU.mult).then_inc(evacuated[p], 1)
                for p in range(2):
                    acc_read(dve, "gate", 2 + p, n)
                dve.tensor_tensor(merged[:, n, :], sig_buf[:, 0, :], sig_buf[:, 1, :], ALU.add).then_inc(merge_done, 1)
            for k in range(KT):
                dve.wait_ge(part_hi, 2 * KT + k + 1)
                dve.tensor_tensor(h_lo[:, k, :], merged[:, k, :], h_hi[:, k, :].bitcast(F32), ALU.subtract).then_inc(part_lo, 1)
            with dve.Fori(0, KT // 2) as i:
                residual(dve, "wo", i, G2)
            norm_dve(dve, 2, Uses.norm3[1])
            for c in range(len(FF_CHUNKS)):
                up_dve(dve, 2, c, u_base(2, c))
                with dve.Fori(0, KT // 2) as i:
                    residual(dve, f"down2{c}", i, G3)
            norm_dve(dve, 3, Uses.norm4[1])


def _tiles(w):
    kt, n = w.shape[0] // P, w.shape[1] // P
    return w.reshape(kt, P, n, P).transpose(2, 1, 0, 3).reshape(n, P, kt * P)


def _columns(v):
    return np.ascontiguousarray(v.reshape(-1, P).T)


def _down(w2, c):
    lo = sum(FF_CHUNKS[:c]) * P
    part = _tiles(w2[lo:lo + FF_CHUNKS[c] * P])
    return np.pad(part, ((0, 0), (0, 0), (0, KT * P - part.shape[2])))


def _up(w13, c):
    t = _tiles(w13)
    n = D_FF // P
    lo = sum(FF_CHUNKS[:c])
    ab = np.stack([t[lo:lo + FF_CHUNKS[c]], t[n + lo:n + lo + FF_CHUNKS[c]]], 1)
    return ab.reshape(-1, P, KT * P)


def kernel(**inputs):
    import concourse.bacc as bacc
    from concourse.bass_utils import run_bass_kernel_spmd

    a = {k: np.asarray(v) for k, v in inputs.items()}
    win = _tiles(a["w_in"][0])
    cuts = np.cumsum([0, 512, 512, 1024, 1024, 1024, 1024, 1024, 1024, 1024, 1024, 1024]) // P
    rq, rk, rv, rg, hq, hff, hfb, hi, hog, gr, gh = [win[cuts[n]:cuts[n + 1]] for n in range(11)]
    hg = np.stack([hi, hff, hfb, hq, hog], 1).reshape(-1, P, KT * P)
    ret = np.stack([rk, rq, rv[0::2], rv[1::2], rg[0::2], rg[1::2]], 1).reshape(-1, P, KT * P)
    gate = np.stack([gr, gh, _tiles(a["w_ret_proj"][0]), _tiles(a["w_hg_proj"][0])], 1).reshape(-1, P, KT * P)
    stream = []
    for f in (1, 2):
        if f == 2:
            stream += [hg, ret, gate, _tiles(a["w_o"][0])]
        for c in range(len(FF_CHUNKS)):
            stream += [_up(a[f"ffn{f}_w13"][0], c), _down(a[f"ffn{f}_w2"][0], c)]
    tables, kpos = shape_constants()
    x = np.concatenate([a["x_prompt"][0], a["x_sample"][0]], 0)
    arrays = {
        "w": np.concatenate(stream, 0),
        "ada": _tiles(a["ada_w"][0]),
        "x": np.ascontiguousarray(x.T.reshape(KT, P, T).transpose(1, 0, 2)),
        "s_hg": np.ascontiguousarray(a["state_hgrn"][0, 0].transpose(1, 2, 0, 3)),
        "s_ret": np.ascontiguousarray(a["state_ret"][0, 0].transpose(1, 2, 0, 3)),
        "in_c": np.ascontiguousarray(np.stack([_columns(a["c_ctx"]), _columns(a["c"][0])], 2).reshape(P, 16)),
        "in_ada_b": _columns(a["ada_b"][0]),
        "in_norm_w": _columns(a["norm_w"][0]),
        "in_final_w": _columns(a["final_norm_w"]),
        "in_hg_w": _columns(a["hg_norm_w"][0]),
        "in_lb": _columns(a["hg_lb_logits"]),
        "in_decay": np.ascontiguousarray(np.broadcast_to(a["ret_decay"][0].reshape(1, 8), (P, 8))),
        "in_kpos": kpos,
        **tables,
    }
    outs = {"y": (P, KT, T), "out_hg": (HG_HEADS, P, 2, HG_DV), "out_ret": (RET_HEADS, P, 2, RET_DV)}
    nc = bacc.Bacc("TRN2", target_bir_lowering=False, num_devices=1)
    d = {}
    for n, v in arrays.items():
        d[n] = nc.dram_tensor(n + "_dram", v.shape, mybir.dt.from_np(v.dtype), kind="ExternalInput").ap()
    for n, shape in outs.items():
        d[n] = nc.dram_tensor(n + "_dram", shape, F32, kind="ExternalOutput").ap()
    build(nc, d)
    r = run_bass_kernel_spmd(nc, [{n + "_dram": v for n, v in arrays.items()}], core_ids=[0]).results[0]
    y = r["y_dram"].transpose(1, 0, 2).reshape(D_MODEL, T).T
    out_ret = r["out_ret_dram"].transpose(2, 0, 1, 3)[None, None]
    out_hg = r["out_hg_dram"].transpose(2, 0, 1, 3)[None, None]
    return (np.ascontiguousarray(y[:CTX])[None], np.ascontiguousarray(y[CTX:])[None],
            np.ascontiguousarray(out_ret), np.ascontiguousarray(out_hg))
```

```python
from contextlib import ExitStack

import numpy as np

import concourse.bass as bass
from concourse import mybir

F32 = mybir.dt.float32
F32R = mybir.dt.float32r
U32 = mybir.dt.uint32
ALU = mybir.AluOpType
ACT = mybir.ActivationFunctionType

P = 128
D_MODEL = 1024
KT = D_MODEL // P
CTX, LAT = 128, 512
T = CTX + LAT
NT = T // P
HT = T // 2
D_FF = 2816
RET_HEADS, RET_DK, RET_DV = 4, 128, 256
HG_HEADS, HG_DK, HG_DV = 8, 128, 128
GRID_W = 64
ROPE_BASE = 10000.0
EPS = 1e-6
N_MOD = 9
LEVELS = 7
TINY = 2.0 ** -62
SH1, SC1, G1, SH2, SC2, G2, SH3, SC3, G3 = range(N_MOD)

FF_CHUNKS = (8, 8, 6)
ADA_SLOTS = 4
ADA_PLAN = [("head", 4, 4), ("up10", FF_CHUNKS[0], 2), ("down10", 4, 1), ("up11", FF_CHUNKS[1], 2),
            ("down11", 4, 1), ("up12", FF_CHUNKS[2], 2), ("down12", 4, 1)]
SLOTS = 3
CREDIT = 2

PHASES = []
for _f in (1, 2):
    if _f == 2:
        PHASES += [("hg", HG_HEADS, (0, 1, 2, 0, 1), (0, 1, 0, 1, 0)),
                   ("ret", RET_HEADS, (0, 1, 2, 0, 1, 2), (0, 1, 0, 1, 0, 1)),
                   ("gate", KT, (0, 1, 2, 1), (0, 1, 0, 1)),
                   ("wo", KT // 2, (0, 1), (0, 1))]
    for _c, _n in enumerate(FF_CHUNKS):
        PHASES += [(f"up{_f}{_c}", _n, (0, 1), (0, 1)), (f"down{_f}{_c}", KT // 2, (0, 1), (0, 1))]


class Stream:

    def __init__(self):
        self.phase, at, slots, sets, order = {}, 0, [0] * SLOTS, [0, 0], []
        for name, steps, slot, group in PHASES:
            self.phase[name] = (steps, slot, group, at, tuple(slots), tuple(sets))
            order += list(slot) * steps
            at += steps * len(slot)
            for s in slot:
                slots[s] += steps
            for g in group:
                sets[g] += steps
        self.total, self.gap = at, {}
        for name, (steps, slot, _, base, _, _) in self.phase.items():
            for p in range(len(slot)):
                gaps = []
                for i in range(steps):
                    n = base + i * len(slot) + p
                    before = [m for m in range(n) if order[m] == order[n]]
                    gaps.append(n - before[-1] if before else 2)
                self.gap[name, p] = min(gaps)

    def index(self, name, p, i):
        _, slot, _, base, _, _ = self.phase[name]
        return base + i * len(slot) + p

    def after(self, name, p, i):
        return self.index(name, p, i) + 1 + CREDIT

    def slot_clear(self, name, p, i):
        return self.after(name, p, i) - self.gap[name, p]

    def loads(self, name, p, i):
        _, slot, _, _, slots, _ = self.phase[name]
        return slots[slot[p]] + i * slot.count(slot[p]) + slot[:p].count(slot[p]) + 1

    def uses(self, name, p, i):
        _, _, group, _, _, sets = self.phase[name]
        return sets[group[p]] + i * group.count(group[p]) + group[:p].count(group[p]) + 1


ST = Stream()


class Ada:

    def __init__(self):
        self.first, self.loads, self.total, loads = {}, {}, 0, [0] * ADA_SLOTS
        for name, steps, per in ADA_PLAN:
            self.first[name], self.loads[name] = self.total, tuple(loads)
            self.total += steps * per
            for s in range(per):
                loads[s] += steps


ADA = Ada()
assert ADA.total == N_MOD * KT
C_NAMES = [("ada_b", 72), ("norm_w", 24), ("final_w", 8), ("hg_w", 8), ("lb", 32), ("decay", 8), ("kpos", 2)]


def shape_constants():
    s, t = np.arange(P)[:, None], np.arange(P)[None, :]
    ident = (s == t).astype(np.float32)
    q = RET_DK // 4
    perm = np.zeros((P, P), np.float32)
    for base in (0, 2 * q):
        for j in range(q):
            perm[base + q + j, base + j] = -1.0
            perm[base + j, base + q + j] = 1.0
    freq = np.float32(ROPE_BASE) ** (-np.arange(q, dtype=np.float32) / np.float32(q))
    n = np.arange(LAT)
    row, col = (n // GRID_W).astype(np.float32), (n % GRID_W).astype(np.float32)
    ang = np.concatenate([freq[:, None] * row, freq[:, None] * row, freq[:, None] * col, freq[:, None] * col])
    ang = ang.astype(np.float32)
    cos = np.concatenate([np.ones((P, CTX), np.float32), np.cos(ang)], 1)
    sin = np.concatenate([np.zeros((P, CTX), np.float32), np.sin(ang)], 1)
    dist = np.abs(t - s).astype(np.float32)
    upper, lower = (t >= s).astype(np.float32), (t <= s).astype(np.float32)
    rows = np.stack([np.broadcast_to(t + 1, (P, P)), np.broadcast_to(P - t, (P, P))], 1).astype(np.float32)
    masks = np.zeros((P, LEVELS, P), np.uint32)
    for u in range(LEVELS):
        half = 1 << u
        masks[:, u, :] = (s // (2 * half) == t // (2 * half)) & (s // half != t // half)
    kpos = np.stack([P - 1 - np.arange(P), np.arange(P)], 1).astype(np.float32)
    return dict(ident=ident, perm=perm, cos=cos, sin=sin, dist=dist, upper=upper, lower=lower,
                rows=rows.reshape(P, 2 * P), masks=masks.reshape(P, LEVELS * P)), kpos


def build(nc, d):
    ctx = ExitStack()
    with ctx:
        def sb(name, shape, dt=F32, scope=ctx):
            return scope.enter_context(nc.sbuf_tensor(name, shape, dt))

        def sem(name):
            return ctx.enter_context(nc.semaphore(name))

        x = sb("x", [P, KT, T])
        h_hi, h_lo = sb("h_hi", [P, KT, T], F32R), sb("h_lo", [P, KT, T], F32R)
        raw = sb("raw", [P, SLOTS, KT * P])
        w_hi = sb("w_hi", [P, SLOTS, KT * P], F32R)
        w_lo = sb("w_lo", [P, SLOTS, KT * P], F32R)
        small = {n: sb("in_" + n, [P, w]) for n, w in C_NAMES}
        mod = sb("mod", [P, N_MOD, KT, 2])
        ident, perm, ones = sb("ident", [P, P]), sb("perm", [P, P]), sb("ones", [P, P])
        eps = sb("eps", [P, 1])
        lb, lb_rest = sb("lb", [P, 2 * KT]), sb("lb_rest", [P, 2 * KT])
        log_gam, gam_tmp = sb("log_gam", [P, 8]), sb("gam_tmp", [P, 5, 8])
        k_decay, c_decay = sb("k_decay", [P, 8]), sb("c_decay", [P, 8])
        soft = sb("soft", [P, 4, 16])
        scope = ExitStack()
        u_hi, u_lo = sb("u_hi", [P, 8, T], F32R, scope), sb("u_lo", [P, 8, T], F32R, scope)
        gate_a, u_full = sb("gate_a", [P, T], F32, scope), sb("u_full", [P, T], F32, scope)
        square = sb("square", [P, 2, T], F32, scope)
        log_ms, rstd = sb("log_ms", [P, T], F32, scope), sb("rstd", [P, T], F32, scope)
        x_norm, h_full = sb("x_norm", [P, 2, T], F32, scope), sb("h_full", [P, 2, T], F32, scope)
        ada_raw = sb("ada_raw", [P, ADA_SLOTS, D_MODEL], F32, scope)
        c_row, ada_prod = sb("c_row", [P, 2, D_MODEL], F32, scope), sb("ada_prod", [P, 2, D_MODEL], F32, scope)
        ada_sum = sb("ada_sum", [P, ADA_SLOTS, 2], F32, scope)
        sq_sum = sb("sq_sum", [P, 2, T], F32, scope)
        scope.close()
        mixer = ExitStack()
        o_hg = sb("o_hg", [P, KT, T], F32, mixer)
        pre = sb("pre", [P, 6, T], F32, mixer)
        scope = ExitStack()
        q, k_f, k_b = (sb(n, [P, T], F32, scope) for n in ("hg_q", "hg_kf", "hg_kb"))
        g_f, g_b, b_f = (sb(n, [P, T], F32, scope) for n in ("hg_gf", "hg_gb", "hg_bf"))
        p_b = sb("hg_pb", [P, NT, P + 1], F32, scope)
        out_gate, out_sig = sb("hg_outgate", [P, T], F32, scope), sb("hg_outsig", [P, T], F32, scope)
        o_sq, o_rstd, o_gated = (sb(n, [P, T], F32, scope) for n in ("hg_osquare", "hg_orstd", "hg_ogated"))
        v_tok = sb("hg_v", [P, NT, P], F32, scope)
        e_f, e_b = sb("hg_ef", [P, 2, T], F32, scope), sb("hg_eb", [P, 2, T], F32, scope)
        q_lev, k_lev = sb("hg_qlev", [P, 2, T], F32, scope), sb("hg_klev", [P, 2, T], F32, scope)
        att = sb("hg_att", [P, NT, P], F32, scope)
        k_tok = sb("hg_ktok", [P, 2, 4, P], F32, scope)
        s_in, s_run = sb("hg_sin", [P, 2, P], F32, scope), sb("hg_srun", [P, 2, 3, P], F32, scope)
        masks = sb("hg_masks", [P, LEVELS, P], U32, scope)
        s_fin, s_dec = sb("hg_sfin", [P, 2, P], F32, scope), sb("hg_sdec", [P, 2, NT], F32, scope)
        scope.close()
        o_ret = sb("o_ret", [P, KT, T], F32, mixer)
        scope = ExitStack()
        r_pre = pre
        r_rot = sb("ret_rot", [P, 2, T], F32, scope)
        r_tmp = sb("ret_tmp", [P, 2, T], F32, scope)
        r_att = sb("ret_att", [P, NT, P], F32, scope)
        r_v = sb("ret_v", [P, NT, 2, P], F32, scope)
        r_ktok = sb("ret_ktok", [P, 2, 4, P], F32, scope)
        r_qdec = sb("ret_qdec", [P, 2, LAT], F32, scope)
        r_sin = sb("ret_sin", [P, 2, RET_DV], F32, scope)
        r_srun = sb("ret_srun", [P, 2, 3, RET_DV], F32, scope)
        r_sfin = sb("ret_sfin", [P, 2, RET_DV], F32, scope)
        cos, sin = sb("cos", [P, T], F32, scope), sb("sin", [P, T], F32, scope)
        d_mat = sb("ret_d", [P, RET_HEADS, P], F32, scope)
        q_rows = sb("ret_qrows", [P, 8, P], F32, scope)
        scope.close()
        mixer.close()
        scope = ExitStack()
        hg_lo = sb("hg_lo", [P, KT, T], F32R, scope)
        sig_buf, hg_hi_a = sb("sig_buf", [P, 2, T], F32, scope), sb("hg_hi_a", [P, 4, T], F32R, scope)
        ret_lo = sb("ret_lo", [P, KT, T], F32R, scope)
        ret_hi, hg_hi_b = sb("ret_hi", [P, KT, T], F32R, scope), sb("hg_hi_b", [P, 4, T], F32R, scope)
        merged = sb("merged", [P, KT, T], F32, scope)
        hg_hi = [hg_hi_a[:, k, :] for k in range(4)] + [hg_hi_b[:, k, :] for k in range(4)]
        scope.close()
        dist = r_tmp[:, 0, 0:P]
        upper, lower = r_tmp[:, 0, P:2 * P], r_tmp[:, 0, 2 * P:3 * P]
        rows = r_tmp[:, 0, 3 * P:5 * P].rearrange("p (d t) -> p d t", d=2)
        e_mat = r_tmp[:, 1, 0:2 * P].rearrange("p (d t) -> p d t", d=2)

        acc = [ctx.enter_context(nc.psum_tensor(f"acc{g}", [P, 2, 512], F32)) for g in range(2)]
        mix = [ctx.enter_context(nc.psum_tensor(f"mix{g}", [P, 2, 512], F32)) for g in range(2)]
        acc_v = [a[:, :, 0:HT] for a in acc]
        mix_v = [m[:, :, 0:HT] for m in mix]
        mix_r = [m[:].rearrange("p b n -> p (b n)") for m in mix]

        def halves(ap):
            return ap.rearrange("p (b n) -> p b n", b=2)

        loaded = [sem(f"slab_loaded{s}") for s in range(SLOTS)]
        hi_done, split_done, slab_done = sem("hi_done"), sem("split_done"), sem("slab_done")
        evacuated = [sem(f"acc_evacuated{g}") for g in range(2)]
        mixed = [sem(f"mix_evacuated{g}") for g in range(2)]
        in_c, in_small, in_x, in_tab = sem("in_c"), sem("in_small"), sem("in_x"), sem("in_tab")
        ones_set, silu_done = sem("ones_set"), sem("silu_done")
        ada_loaded = [sem(f"ada_loaded{s}") for s in range(ADA_SLOTS)]
        ada_read, ada_done, ada_moved = sem("ada_read"), sem("ada_done"), sem("ada_moved")
        small_done, small_act = sem("small_done"), sem("small_act")
        coef_done = sem("coef_done")
        sq_done, sq_summed, rstd_done, log_done = sem("sq_done"), sem("sq_summed"), sem("rstd_done"), sem("log_done")
        xn_done, mod_done, hhi_done, hlo_done = sem("xn_done"), sem("mod_done"), sem("hhi_done"), sem("hlo_done")
        uhi_done, ulo_done = sem("uhi_done"), sem("ulo_done")
        x_updated = sem("x_updated")
        y_out, states_out = sem("y_out"), sem("states_out")

        pool_waited, dve_waited = sem("pool_waited"), sem("dve_waited")

        def load_slab(sp, name, p, i):
            slot = ST.phase[name][1][p]
            sp.wait_ge(split_done, ST.slot_clear(name, p, i))
            sp.dma_start(raw[:, slot, :], d["w"][ST.index(name, p, i)]).then_inc(loaded[slot], 16)

        def split_slab(pool, name, p, i):
            slot = ST.phase[name][1][p]
            pool.wait_ge(loaded[slot], 16 * ST.loads(name, p, i))
            pool.wait_ge(slab_done, ST.slot_clear(name, p, i))
            pool.sem_inc(pool_waited, 1)
            pool.tensor_scalar(w_hi[:, slot, :], raw[:, slot, :], 1.0, 1.0, ALU.mult, ALU.mult).then_inc(hi_done, 1)
            pool.wait_ge(hi_done, ST.index(name, p, i) + 1)
            pool.tensor_tensor(w_lo[:, slot, :], raw[:, slot, :], w_hi[:, slot, :].bitcast(F32),
                               ALU.subtract).then_inc(split_done, 1)

        def products(pe, name, p, k, src_hi, src_lo, k_tiles=KT):
            _, slots, sets, _, _, _ = ST.phase[name]
            s, g = slots[p], sets[p]
            for n, (w, r) in enumerate(((w_hi, src_hi), (w_hi, src_lo), (w_lo, src_hi))):
                tile = r[k] if isinstance(r, list) else r[:, k, :]
                for b in range(2):
                    last = pe.matmul(acc[g][:, b, 0:HT], w[:, s, k * P:(k + 1) * P], tile[:, b * HT:(b + 1) * HT],
                                     start=(k == 0 and n == 0), stop=(k == k_tiles - 1 and n == 2))
            if k == k_tiles - 1:
                last.then_inc(slab_done, 1)

        def project(pe, name, p, i, src_hi, src_lo, k_tiles=KT, ks=None, tiles_done=None):
            ks = ks or range(k_tiles)
            if ks[0] == 0:
                pe.wait_ge(split_done, ST.after(name, p, i))
                pe.wait_ge(evacuated[ST.phase[name][2][p]], ST.uses(name, p, i))
            for k in ks:
                if tiles_done:
                    pe.wait_ge(tiles_done[0], tiles_done[1] + k + 1)
                products(pe, name, p, k, src_hi, src_lo, k_tiles)

        def project_pair(pe, name, src_hi, src_lo, tiles_done):
            for p in range(2):
                pe.wait_ge(split_done, ST.after(name, p, 0))
                pe.wait_ge(evacuated[ST.phase[name][2][p]], ST.uses(name, p, 0))
            for k in range(KT):
                pe.wait_ge(tiles_done[0], tiles_done[1] + k + 1)
                for p in range(2):
                    products(pe, name, p, k, src_hi, src_lo)

        def projected(eng, name, p, i):
            eng.wait_ge(slab_done, ST.after(name, p, i))

        def acc_read(eng, name, p, i):
            eng.wait_ge(evacuated[ST.phase[name][2][p]], ST.uses(name, p, i) + 1)

        HG0, HG1, RT0, RT1 = 7, 6, 5, 4

        class Uses:
            norm1 = [1, 1]
            norm2 = [norm1[0], norm1[1] + 1]
            hg = [norm2[0], norm2[1] + 1]
            ret = [hg[0] + HG0 * HG_HEADS, hg[1] + HG1 * HG_HEADS]
            norm3 = [ret[0] + RT0 * RET_HEADS, ret[1] + RT1 * RET_HEADS]
            norm4 = [norm3[0], norm3[1] + 1]

        def mix_free(pe, g, n):
            pe.wait_ge(mixed[g], n)

        def load_ada(sp, m, slot, before):
            sp.wait_ge(ada_read, before + ADA_SLOTS)
            sp.dma_start(ada_raw[:, slot, :], d["ada"][m]).then_inc(ada_loaded[slot], 16)

        def load_ada_step(sp, name, i):
            per = dict((n, p) for n, _, p in ADA_PLAN)[name]
            m = ADA.first[name] + i * per
            for s in range(per):
                load_ada(sp, m + s, s, m)

        def ada_tiles(dve, m, slots, n_load):
            dve.wait_ge(ada_moved, m + 1)
            for n, s in enumerate(slots):
                dve.wait_ge(ada_loaded[s], 16 * n_load[n])
                if n:
                    dve.wait_ge(ada_read, ADA_SLOTS + m + n)
                for e in range(2):
                    last = dve.tensor_tensor_reduce(out=ada_prod[:, e, :], in0=ada_raw[:, s, :], in1=c_row[:, e, :],
                                                    scale=1.0, scalar=0.0, op0=ALU.mult, op1=ALU.add,
                                                    accum_out=ada_sum[:, n, e:e + 1])
                last.then_inc(ada_read, 1)
            count = len(slots)
            dve.wait_ge(ada_read, ADA_SLOTS + m + count)
            out = mod[:].rearrange("p a k e -> p (a k) e")[:, bass.ds(m, count), :]
            bias = small["ada_b"][:, bass.ds(m, count)].unsqueeze(2).to_broadcast([P, count, 2])
            dve.tensor_tensor(out, ada_sum[:, 0:count, :], bias, ALU.add).then_inc(ada_moved, count)

        SQ_CREDIT = 2
        sq_added = sem("sq_added")
        LAST = {1: "down12", 2: "wo", 3: "down22"}

        def residual_final(eng, n):
            if n == 0:
                eng.wait_ge(in_x, 16)
            else:
                for p in range(2):
                    acc_read(eng, LAST[n], p, KT // 2 - 1)

        def norm_stats_act(act, n):
            act.preload_act_table_set("natural_log_exp_and_others")
            if n == 0:
                residual_final(act, 0)
            with act.Fori(0, KT // 2) as i:
                for p in range(2):
                    k = i * 2 + p
                    if n:
                        acc_read(act, LAST[n], p, i)
                    act.wait_ge(sq_added, (KT + 1) * n + k + SQ_CREDIT)
                    act.activation(square[:, p, :], x[:, k, :], ACT.Square).then_inc(sq_done, 1)
            act.wait_ge(sq_summed, n + 1)
            act.activation(halves(log_ms[:]), mix_v[1], ACT.Ln, bias=eps[:, 0:1],
                           scale=1.0 / D_MODEL).then_inc(log_done, 1)
            act.wait_ge(log_done, n + 1)
            act.activation(rstd[:], log_ms[:], ACT.Exp, scale=-0.5).then_inc(rstd_done, 1)

        def norm_rows_act(act, n):
            for k in range(KT):
                act.wait_ge(xn_done, KT * n + k + 1)
                if k >= 2:
                    act.wait_ge(hlo_done, KT * n + k - 1)
                act.activation(h_full[:, k % 2, 0:CTX], x_norm[:, k % 2, 0:CTX], ACT.Identity,
                               bias=mod[:, 3 * n, k, 0:1], scale=mod[:, 3 * n + 1, k, 0:1])
                act.activation(h_full[:, k % 2, CTX:T], x_norm[:, k % 2, CTX:T], ACT.Identity,
                               bias=mod[:, 3 * n, k, 1:2], scale=mod[:, 3 * n + 1, k, 1:2]).then_inc(mod_done, 1)
                act.wait_ge(mod_done, KT * n + k + 1)
                act.activation(h_hi[:, k, :], h_full[:, k % 2, :], ACT.Copy).then_inc(hhi_done, 1)

        def square_clear(pool, n):
            if n:
                pool.wait_ge(sq_summed, n)
            pool.memset(sq_sum[:], 0.0).then_inc(sq_added, 1)

        def square_add(pool, n, i):
            for p in range(2):
                k = i * 2 + p
                pool.wait_ge(sq_done, KT * n + k + 1)
                pool.wait_ge(sq_added, (KT + 1) * n + k + 1 + SQ_CREDIT)
                pool.tensor_tensor(sq_sum[:, p, :], sq_sum[:, p, :], square[:, p, :], ALU.add).then_inc(sq_added, 1)

        def norm_pe(pe, n, use):
            mix_free(pe, 1, use)
            for p in range(2):
                pe.wait_ge(sq_added, (KT + 1) * n + SQ_CREDIT + KT + p)
                for b in range(2):
                    last = pe.matmul(mix[1][:, b, 0:HT], ones[:], sq_sum[:, p, b * HT:(b + 1) * HT],
                                     start=(p == 0), stop=(p == 1))
            last.then_inc(sq_summed, 1)

        def norm_dve(dve, n, use):
            residual_final(dve, n)
            dve.wait_ge(rstd_done, 3 * n + 1)
            dve.scalar_tensor_tensor(out=halves(log_ms[:]), in0=mix_v[1], scalar=D_MODEL * EPS, in1=halves(rstd[:]),
                                     op0=ALU.add, op1=ALU.mult).then_inc(mixed[1], 1)
            dve.wait_ge(mixed[1], use + 1)
            dve.scalar_tensor_tensor(out=log_ms[:], in0=log_ms[:], scalar=-0.5 / D_MODEL, in1=rstd[:],
                                     op0=ALU.mult, op1=ALU.mult).then_inc(rstd_done, 1)
            dve.wait_ge(rstd_done, 3 * n + 2)
            dve.scalar_tensor_tensor(out=rstd[:], in0=log_ms[:], scalar=1.5, in1=rstd[:],
                                     op0=ALU.add, op1=ALU.mult).then_inc(rstd_done, 1)
            dve.wait_ge(rstd_done, 3 * n + 3)
            for k in range(KT):
                if n == 3:
                    dve.scalar_tensor_tensor(out=x[:, k, :], in0=x[:, k, :], scalar=small["final_w"][:, k:k + 1],
                                             in1=rstd[:], op0=ALU.mult, op1=ALU.mult).then_inc(xn_done, 1)
                    continue
                if k >= 2:
                    dve.wait_ge(mod_done, KT * n + k - 1)
                dve.tensor_tensor(x_norm[:, k % 2, :], x[:, k, :], rstd[:], ALU.mult).then_inc(xn_done, 1)
                if k:
                    lo_part(dve, n, k - 1)
            if n < 3:
                lo_part(dve, n, KT - 1)

        def lo_part(dve, n, k):
            dve.wait_ge(hhi_done, KT * n + k + 1)
            dve.tensor_tensor(h_lo[:, k, :], h_full[:, k % 2, :], h_hi[:, k, :].bitcast(F32),
                              ALU.subtract).then_inc(hlo_done, 1)

        def residual(dve, name, i, part):
            for p in range(2):
                g = ST.phase[name][2][p]
                projected(dve, name, p, i)
                tile = i * 2 + p
                for lo, hi, e in ((0, CTX, 0), (CTX, HT, 1), (HT, T, 1)):
                    src = acc[g][:, lo // HT, lo % HT:lo % HT + hi - lo]
                    last = dve.scalar_tensor_tensor(out=x[:, tile, lo:hi], in0=src, scalar=mod[:, part, tile, e:e + 1],
                                                    in1=x[:, tile, lo:hi], op0=ALU.mult, op1=ALU.add)
                last.then_inc(evacuated[g], 1)

        def up_act(act, f, c, base):
            name = f"up{f}{c}"
            act.preload_act_table_set("silu_and_others")
            with act.Fori(0, FF_CHUNKS[c]) as j:
                projected(act, name, 0, j)
                act.wait_ge(evacuated[1], ST.uses(name, 1, j))
                act.activation(halves(gate_a[:]), acc_v[0], ACT.Silu).then_inc(evacuated[0], 1)
                acc_read(act, name, 1, j)
                act.activation(u_hi[:, j, :], u_full[:], ACT.Copy).then_inc(uhi_done, 1)

        def up_dve(dve, f, c, base):
            name = f"up{f}{c}"
            with dve.Fori(0, FF_CHUNKS[c]) as j:
                if f == 1:
                    ada_step(dve, name, j)
                acc_read(dve, name, 0, j)
                projected(dve, name, 1, j)
                dve.wait_ge(ulo_done, base + j + 1)
                dve.tensor_tensor(halves(u_full[:]), halves(gate_a[:]), acc_v[1], ALU.mult).then_inc(evacuated[1], 1)
                dve.wait_ge(uhi_done, base + j + 1)
                dve.tensor_tensor(u_lo[:, j, :], u_full[:], u_hi[:, j, :].bitcast(F32),
                                  ALU.subtract).then_inc(ulo_done, 1)

        def ff_pe(pe, f, c, base):
            name = f"up{f}{c}"
            if c == 0:
                project_pair(pe, name, h_hi, h_lo, (hlo_done, 2 * KT * (f - 1)))
            with pe.Fori(0 if c else 1, FF_CHUNKS[c]) as j:
                project(pe, name, 0, j, h_hi, h_lo)
                project(pe, name, 1, j, h_hi, h_lo)
            name = f"down{f}{c}"
            project(pe, name, 0, 0, u_hi, u_lo, FF_CHUNKS[c], tiles_done=(ulo_done, base + 1))
            project(pe, name, 1, 0, u_hi, u_lo, FF_CHUNKS[c])
            with pe.Fori(1, KT // 2) as i:
                project(pe, name, 0, i, u_hi, u_lo, FF_CHUNKS[c])
                project(pe, name, 1, i, u_hi, u_lo, FF_CHUNKS[c])

        def u_base(f, c):
            return (f - 1) * (D_FF // P) + sum(FF_CHUNKS[:c])

        def ada_step(dve, name, i):
            per = dict((n, p) for n, _, p in ADA_PLAN)[name]
            ada_tiles(dve, ADA.first[name] + i * per, tuple(range(per)), [ADA.loads[name][s] + i + 1 for s in range(per)])

        def make_scale(dve, n):
            dve.wait_ge(ada_moved, 1 + (ADA.first["up10"] if n == 0 else ADA.total))
            sc = mod[:, 3 * n + 1, :, :]
            nw = small["norm_w"][:, KT * n:KT * (n + 1)].unsqueeze(2).to_broadcast([P, KT, 2])
            dve.tensor_scalar(sc, sc, 1.0, None, ALU.add).then_inc(coef_done, 1)
            dve.wait_ge(coef_done, 3 * n + 1)
            dve.tensor_tensor(sc, sc, nw, ALU.mult).then_inc(coef_done, 1)

        def make_gate(dve, n):
            dve.wait_ge(ada_moved, 1 + (ADA.first["down10"] if n == 0 else ADA.total))
            g = mod[:, 3 * n + 2, :, :]
            dve.tensor_scalar(g, g, 1.0 if n == 1 else 0.5, None, ALU.mult).then_inc(coef_done, 1)

        def small_chain(dve):
            done = [0]

            def step(instruction):
                done[0] += 1
                instruction.then_inc(small_done, 1)
                dve.wait_ge(small_done, done[0])

            logits = small["lb"][:].rearrange("p (w l k) -> p w l k", w=2, l=2)
            top, e0, e1, total = (soft[:, n, :].rearrange("p (w k) -> p w k", w=2) for n in range(4))
            step(dve.tensor_tensor(top, logits[:, :, 0, :], logits[:, :, 1, :], ALU.max))
            step(dve.tensor_tensor(e0, logits[:, :, 0, :], top, ALU.subtract))
            step(dve.tensor_tensor(e1, logits[:, :, 1, :], top, ALU.subtract))
            y, u, log_u, diff, is_zero = (gam_tmp[:, n, :] for n in range(5))
            z = small["decay"][:]
            step(dve.scalar_tensor_tensor(out=y, in0=z, scalar=-1.0, in1=z, op0=ALU.mult, op1=ALU.max))
            dve.wait_ge(small_act, 1)
            step(dve.tensor_scalar(u, y, 1.0, None, ALU.add))
            step(dve.tensor_scalar(diff, u, -1.0, None, ALU.add))
            step(dve.tensor_scalar(is_zero, diff, 0.0, None, ALU.is_equal))
            step(dve.tensor_tensor(diff, diff, is_zero, ALU.add))
            step(dve.reciprocal(diff, diff))
            dve.wait_ge(small_act, 2)
            step(dve.tensor_tensor(log_u, log_u, y, ALU.mult))
            step(dve.tensor_tensor(log_u, log_u, diff, ALU.mult))
            step(dve.tensor_tensor(is_zero, is_zero, y, ALU.mult))
            step(dve.tensor_tensor(log_u, log_u, is_zero, ALU.add))
            step(dve.scalar_tensor_tensor(out=log_gam[:], in0=z, scalar=0.0, in1=log_u, op0=ALU.min, op1=ALU.subtract))
            step(dve.tensor_tensor(total, e0, e1, ALU.add))
            step(dve.reciprocal(total, total))
            step(dve.tensor_tensor(lb[:].rearrange("p (w k) -> p w k", w=2), e0, total, ALU.mult))
            step(dve.tensor_scalar(lb_rest[:], lb[:], -1.0, 1.0, ALU.mult, ALU.add))

        def small_chain_act(act):
            act.wait_ge(small_done, 4)
            act.activation(soft[:, 1, :], soft[:, 1, :], ACT.Exp)
            act.activation(soft[:, 2, :], soft[:, 2, :], ACT.Exp)
            act.activation(gam_tmp[:, 0, :], gam_tmp[:, 0, :], ACT.Exp, scale=-1.0).then_inc(small_act, 1)
            act.wait_ge(small_done, 5)
            act.activation(gam_tmp[:, 2, :], gam_tmp[:, 1, :], ACT.Ln).then_inc(small_act, 1)
            act.wait_ge(small_done, 14)
            for w in range(2):
                cols = slice(RET_HEADS * w, RET_HEADS * (w + 1))
                act.activation(k_decay[:, cols], log_gam[:, cols], ACT.Exp, scale=small["kpos"][:, w:w + 1])
            act.activation(c_decay[:], log_gam[:], ACT.Exp, scale=float(P))

        F_, B_, Q_, O_, V_ = range(5)
        hg_sig, hg_gate, hg_key, hg_query, hg_og = (sem("hg_" + n) for n in ("sig", "gate", "key", "query", "og"))
        hg_ln, hg_scan, hg_arg, hg_exp, hg_qk = (sem("hg_" + n) for n in ("ln", "scan", "arg", "exp", "qk"))
        hg_lev, hg_ktok, hg_kt, hg_kv, hg_state = (sem("hg_" + n) for n in ("lev", "ktok", "kt", "kv", "state"))
        hg_o, hg_osq, hg_ss, hg_rstd, hg_gated, hg_out = (sem("hg_" + n) for n in ("o", "osq", "ss", "rstd", "gated", "out"))
        hg_vt, hg_sin_ld, hg_dec, hg_fin, hg_att_done = (sem("hg_" + n) for n in ("vt", "sin", "dec", "fin", "att"))
        hg_kk = sem("hg_kk")
        N_ARG = LEVELS + 2
        N_QK = LEVELS + 3

        def tiles5(ap):
            return ap.rearrange("p (c t) -> p c t", c=NT)

        def blocks(ap, u):
            return ap.rearrange("p (a i) -> p a i", i=2 << u)

        def hg_evac(act, h, p):
            projected(act, "hg", p, h)
            again = not (isinstance(h, int) and h == 0)
            if again and p == V_:
                act.wait_ge(hg_vt, h)
            if again and p in (F_, B_):
                act.wait_ge(hg_sig, 6 * h)
            if again and p == Q_:
                act.wait_ge(hg_query, h)
            if again and p == O_:
                act.wait_ge(hg_og, h)
            g = ST.phase["hg"][2][p]
            act.activation(halves(pre[:, p, :]), acc_v[g], ACT.Copy).then_inc(evacuated[g], 1)

        def hg_start_act(act, h):
            act.preload_act_table_set("sigmoid_and_others")
            again = not (isinstance(h, int) and h == 0)
            for n, (src, dst, sc) in enumerate(((F_, g_f, 1.0), (B_, g_b, 1.0), (F_, k_f, -1.0), (B_, k_b, -1.0),
                                                (Q_, q, 1.0), (O_, out_sig, 1.0))):
                if again and n == 0:
                    act.wait_ge(hg_scan, 2 * h)
                if again and n == 2:
                    act.wait_ge(hg_kk, N_ARG * h)
                if again and n == 4:
                    act.wait_ge(hg_qk, N_QK * h)
                if again and n == 5:
                    act.wait_ge(hg_og, h)
                acc_read(act, "hg", src, h)
                act.activation(dst[:], pre[:, src, :], ACT.Sigmoid, scale=sc).then_inc(hg_sig, 1)
            act.preload_act_table_set("natural_log_exp_and_others")
            for n, g in enumerate((g_f, g_b)):
                act.wait_ge(hg_gate, 2 * h + n + 1)
                act.activation(g[:], g[:], ACT.Ln, bias=lb[:, bass.ds(KT * n + h, 1)]).then_inc(hg_ln, 1)

        def hg_act(act, m, h, next_evac):
            act.wait_ge(hg_out, m + 1)
            act.dma_start(s_in[:], d["s_hg"][m]).then_inc(hg_sin_ld, 16)
            act.wait_ge(hg_vt, m + 1)
            act.activation(v_tok[:].rearrange("p c t -> p (c t)"), mix_r[0][:, 0:T], ACT.Copy).then_inc(mixed[0], 1)
            for u in range(LEVELS):
                act.wait_ge(hg_arg, N_ARG * m + u + 1)
                act.activation(e_f[:, u % 2, :], e_f[:, u % 2, :], ACT.Exp)
                act.activation(e_b[:, u % 2, :], e_b[:, u % 2, :], ACT.Exp).then_inc(hg_exp, 1)
                if u in (1, 3, 5):
                    next_evac((1, 3, 5).index(u))
            u = LEVELS
            act.wait_ge(hg_arg, N_ARG * m + u + 1)
            act.activation(e_f[:, u % 2, :], e_f[:, u % 2, :], ACT.Exp)
            act.activation(e_b[:, u % 2, :], b_f[:], ACT.Exp).then_inc(hg_exp, 1)
            u = LEVELS + 1
            act.wait_ge(hg_arg, N_ARG * m + u + 1)
            act.activation(e_f[:, u % 2, :], e_f[:, u % 2, :], ACT.Exp)
            act.activation(tiles5(e_b[:, u % 2, :]), p_b[:, :, 0:P], ACT.Exp).then_inc(hg_exp, 1)
            act.activation(s_dec[:, 0, :], tiles5(b_f[:])[:, :, P - 1], ACT.Exp)
            act.activation(s_dec[:, 1, :], p_b[:, :, P], ACT.Exp).then_inc(hg_dec, 1)
            next_evac(3)
            for n in range(2):
                act.wait_ge(hg_ktok, 2 * m + n + 1)
                act.activation(k_tok[:, n].rearrange("p c t -> p (c t)"), mix_r[n][:, 0:4 * P],
                               ACT.Copy).then_inc(mixed[n], 1)
            if h is not None:
                hg_start_act(act, h)
            act.wait_ge(hg_fin, m + 1)
            act.dma_start(d["out_hg"][m], s_fin[:]).then_inc(states_out, 16)
            act.wait_ge(hg_o, m + 1)
            act.activation(o_sq[:], mix_r[0][:, 0:T], ACT.Square).then_inc(hg_osq, 1)
            next_evac(4)
            act.wait_ge(hg_ss, m + 1)
            act.activation(halves(o_sq[:]), mix_v[1], ACT.Ln, bias=eps[:, 0:1], scale=1.0 / HG_DV).then_inc(mixed[1], 1)
            act.wait_ge(mixed[1], Uses.hg[1] + HG1 * (m + 1))
            act.activation(o_rstd[:], o_sq[:], ACT.Exp, scale=-0.5).then_inc(hg_rstd, 1)

        def hg_arguments(dve, m, u):
            f, b, half = e_f[:, u % 2, :], e_b[:, u % 2, :], 1 << u
            if u >= 2:
                dve.wait_ge(hg_qk, N_QK * m + u)
                dve.wait_ge(hg_kk, N_ARG * m + u - 1)
            elif not (isinstance(m, int) and m == 0):
                dve.wait_ge(hg_qk, N_QK * m)
                dve.wait_ge(hg_kk, N_ARG * m)
            if u < LEVELS:
                fb, src = blocks(f, u), blocks(b_f[:], u)
                na = T // (2 * half)
                mid = src[:, :, half - 1:half].to_broadcast([P, na, half])
                dve.tensor_tensor(fb[:, :, 0:half], mid, src[:, :, 0:half], ALU.subtract)
                dve.tensor_tensor(fb[:, :, half:], src[:, :, half:], mid, ALU.subtract)
                nb = P // (2 * half)
                bb = b.rearrange("p (c a i) -> p c a i", c=NT, a=nb)
                src = p_b[:, :, 0:P].rearrange("p c (a i) -> p c a i", a=nb)
                mid = src[:, :, :, half:half + 1].to_broadcast([P, NT, nb, half])
                dve.tensor_tensor(bb[:, :, :, 0:half], mid, src[:, :, :, 0:half], ALU.subtract)
                dve.tensor_tensor(bb[:, :, :, half:], src[:, :, :, half:], mid, ALU.subtract).then_inc(hg_arg, 1)
            elif u == LEVELS:
                last = tiles5(b_f[:])[:, :, P - 1:P].to_broadcast([P, NT, P])
                dve.tensor_tensor(tiles5(f), last, tiles5(b_f[:]), ALU.subtract).then_inc(hg_arg, 1)
            else:
                last = p_b[:, :, P:P + 1].to_broadcast([P, NT, P])
                dve.tensor_tensor(tiles5(f), last, p_b[:, :, 0:P], ALU.subtract).then_inc(hg_arg, 1)

        def hg_operands(dve, m, u):
            s, half = u % 2, 1 << u
            dve.wait_ge(hg_exp, N_ARG * m + u + 1)
            if u >= 1:
                dve.wait_ge(hg_lev, (LEVELS + 1) * m + u)
            if u < LEVELS:
                first, second = slice(0, half), slice(half, 2 * half)
                fb, bb = blocks(e_f[:, s, :], u), blocks(e_b[:, s, :], u)
                qb, src = blocks(q_lev[:, s, :], u), blocks(q[:], u)
                dve.tensor_tensor(qb[:, :, second], src[:, :, second], fb[:, :, second], ALU.mult)
                dve.tensor_tensor(qb[:, :, first], src[:, :, first], bb[:, :, first], ALU.mult).then_inc(hg_qk, 1)
            else:
                e = e_b if u == LEVELS else e_f
                dve.tensor_tensor(q_lev[:, s, :], q[:], e[:, s, :], ALU.mult).then_inc(hg_qk, 1)

        def hg_keys(pool, m, u):
            s, half = u % 2, 1 << u
            if u == 0:
                pool.wait_ge(hg_key, 2 * m + 2)
            pool.wait_ge(hg_exp, N_ARG * m + u + 1)
            if u >= 1:
                pool.wait_ge(hg_lev, (LEVELS + 1) * m + u)
            if u < LEVELS:
                first, second = slice(0, half), slice(half, 2 * half)
                fb, bb, out = blocks(e_f[:, s, :], u), blocks(e_b[:, s, :], u), blocks(k_lev[:, s, :], u)
                pool.tensor_tensor(out[:, :, first], blocks(k_f[:], u)[:, :, first], fb[:, :, first], ALU.mult)
                pool.tensor_tensor(out[:, :, second], blocks(k_b[:], u)[:, :, second], bb[:, :, second],
                                   ALU.mult).then_inc(hg_kk, 1)
            else:
                k, e = (k_f, e_f) if u == LEVELS else (k_b, e_b)
                pool.tensor_tensor(k_lev[:, s, :], k[:], e[:, s, :], ALU.mult).then_inc(hg_kk, 1)

        def split_hg(pool):
            for p in range(5):
                split_slab(pool, "hg", p, 0)
            split_slab(pool, "hg", 0, 1)
            with pool.Fori(1, HG_HEADS - 1) as h:
                split_and_keys(pool, "hg", h, "hg", 0, h + 1)
            split_and_keys(pool, "hg", HG_HEADS - 1, "ret", 0, 0)
            split_and_keys(pool, "ret", HG_HEADS, "ret", 5, 0)

        def split_and_keys(pool, name, h, next_name, next_p, next_i):
            i = h if name == "hg" else 0
            for p, units in ((1, (0,)), (2, (1, 2)), (3, (3, 4)), (4, (5, 6, 7, 8))):
                split_slab(pool, name, p, i)
                for u in units:
                    hg_keys(pool, h - 1, u)
            split_slab(pool, next_name, next_p, next_i)

        def hg_score_read(dve, m, u):
            dve.wait_ge(hg_lev, (LEVELS + 1) * m + u + 1)
            flat = att[:].rearrange("p c t -> p (c t)")
            if u == 0:
                dve.tensor_copy(flat, mix_r[0][:, 0:T]).then_inc(mixed[0], 1)
            else:
                g, before = (u - 1) % 2, (u - 1) // 2
                dve.wait_ge(mixed[g], (Uses.hg[0] + HG0 * m + 2 if g == 0 else Uses.hg[1] + HG1 * m + 1) + before)
                mask = masks[:, u - 1, :].unsqueeze(1).to_broadcast([P, NT, P])
                dve.sem_inc(dve_waited, 1)
                dve.copy_predicated(att[:], mask, tiles5(mix_r[u % 2][:, 0:T])).then_inc(mixed[u % 2], 1)

        def hg_start_dve(dve, h):
            again = not (isinstance(h, int) and h == 0)
            for n, g in enumerate((g_f, g_b)):
                dve.wait_ge(hg_sig, 6 * h + n + 1)
                dve.tensor_scalar(g[:], g[:], TINY, lb_rest[:, bass.ds(KT * n + h, 1)], ALU.max, ALU.mult).then_inc(hg_gate, 1)
            for n, k in enumerate((k_f, k_b)):
                dve.wait_ge(hg_sig, 6 * h + n + 3)
                dve.tensor_scalar(k[:], k[:], lb_rest[:, bass.ds(KT * n + h, 1)], None, ALU.mult).then_inc(hg_key, 1)
            dve.wait_ge(hg_sig, 6 * h + 5)
            dve.scalar_tensor_tensor(out=q[:], in0=pre[:, Q_, :], scalar=float(HG_DK) ** -0.5, in1=q[:],
                                     op0=ALU.mult, op1=ALU.mult).then_inc(hg_query, 1)
            dve.wait_ge(hg_key, 2 * h + 2)
            if again:
                dve.wait_ge(hg_ktok, 2 * h)
            dve.tensor_tensor(k_lev[:, 1, :], k_f[:], k_b[:], ALU.add).then_inc(hg_qk, 1)

        def hg_sums_dve(dve, h):
            dve.wait_ge(hg_sig, 6 * h + 6)
            dve.tensor_tensor(out_gate[:], pre[:, O_, :], out_sig[:], ALU.mult).then_inc(hg_og, 1)
            for n, g in enumerate((g_f, g_b)):
                dve.wait_ge(hg_ln, 2 * h + n + 1)
                for c in range(NT):
                    out = b_f[:, c * P:(c + 1) * P] if n == 0 else p_b[:, c, 1:P + 1]
                    last = dve.tensor_tensor_scan(out, ones[:], g[:, c * P:(c + 1) * P], 0.0, ALU.mult, ALU.add)
                last.then_inc(hg_scan, 1)
            dve.wait_ge(hg_scan, 2 * h + 2)
            dve.wait_ge(hg_query, h + 1)
            hg_arguments(dve, h, 0)

        def hg_dve(dve, m, h):
            for u in range(LEVELS):
                hg_arguments(dve, m, u + 1)
                hg_operands(dve, m, u)
                hg_score_read(dve, m, u)
            hg_arguments(dve, m, LEVELS + 1)
            hg_score_read(dve, m, LEVELS)
            hg_operands(dve, m, LEVELS)
            hg_operands(dve, m, LEVELS + 1)
            dve.wait_ge(hg_dec, m + 1)
            dve.wait_ge(hg_sin_ld, 16 * (m + 1))
            dve.wait_ge(hg_kv, 2 * m + 2)
            dve.wait_ge(states_out, 16 * (m + 1))
            dve.tensor_copy(s_fin[:, 0, :], mix[0][:, 1, 0:P])
            dve.tensor_copy(s_fin[:, 1, :], mix[1][:, 1, 0:P]).then_inc(hg_fin, 1)
            for n in range(3):
                for w in range(2):
                    tile = 1 + n if w == 0 else 4 - n
                    kv = mix[w][:, 1, (1 + n) * P:(2 + n) * P] if w == 0 else mix[w][:, 1, (3 - n) * P:(4 - n) * P]
                    old = s_in[:, w, :] if n == 0 else s_run[:, w, n - 1, :]
                    if n:
                        dve.wait_ge(hg_state, 6 * m + 2 * (n - 1) + w + 1)
                    last = dve.scalar_tensor_tensor(out=s_run[:, w, n, :], in0=old, scalar=s_dec[:, w, tile:tile + 1],
                                                    in1=kv, op0=ALU.mult, op1=ALU.add)
                    last.then_inc(hg_state, 1)
            if h is not None:
                hg_start_dve(dve, h)
            dve.wait_ge(hg_o, m + 1)
            dve.wait_ge(hg_osq, m + 1)
            dve.wait_ge(hg_og, m + 1)
            dve.wait_ge(hg_out, m + 1)
            dve.scalar_tensor_tensor(out=o_gated[:], in0=mix_r[0][:, 0:T], scalar=small["hg_w"][:, bass.ds(m, 1)],
                                     in1=out_gate[:], op0=ALU.mult, op1=ALU.mult).then_inc(mixed[0], 1)
            dve.wait_ge(mixed[0], Uses.hg[0] + HG0 * (m + 1))
            if h is not None:
                hg_sums_dve(dve, h)
            dve.wait_ge(hg_rstd, m + 1)
            dve.tensor_tensor(o_hg[:, m, :], o_gated[:], o_rstd[:], ALU.mult).then_inc(hg_out, 1)

        def hg_vt_pe(pe, m):
            acc_read(pe, "hg", V_, m)
            mix_free(pe, 0, Uses.hg[0] + HG0 * m)
            for c in range(NT):
                last = pe.transpose(mix_r[0][:, c * P:(c + 1) * P], pre[:, V_, c * P:(c + 1) * P], ident[:])
            last.then_inc(hg_vt, 1)

        def hg_unit_pe(pe, m, u):
            pe.wait_ge(hg_qk, N_QK * m + u + 1)
            if u:
                pe.wait_ge(hg_kk, N_ARG * m + u)
            if u == 0:
                pe.wait_ge(hg_query, m + 1)
            g = u % 2
            mix_free(pe, g, (Uses.hg[0] + HG0 * m + 1 + u // 2) if g == 0 else (Uses.hg[1] + HG1 * m + u // 2))
            ks, qs = (k_lev[:, 1, :], q[:]) if u == 0 else (k_lev[:, (u - 1) % 2, :], q_lev[:, (u - 1) % 2, :])
            for c in range(NT):
                cols = slice(c * P, (c + 1) * P)
                last = pe.matmul(mix_r[g][:, cols], ks[:, cols], qs[:, cols], start=True, stop=True)
            last.then_inc(hg_lev, 1)

        HG_TILES = ((0, 1, 2, 3), (0, 2, 3, 4))

        def hg_kt_pe(pe, m):
            for w in range(2):
                pe.wait_ge(hg_qk, N_QK * m + N_QK - 1 + w)
                pe.wait_ge(hg_kk, N_ARG * m + LEVELS + w + 1)
                mix_free(pe, w, (Uses.hg[0] + HG0 * m + 5, Uses.hg[1] + HG1 * m + 4)[w])
                for j, c in enumerate(HG_TILES[w]):
                    last = pe.transpose(mix_r[w][:, j * P:(j + 1) * P], k_lev[:, (LEVELS + w) % 2, c * P:(c + 1) * P], ident[:])
                last.then_inc(hg_ktok, 1)

        def hg_kv_pe(pe, m):
            for w in range(2):
                mix_free(pe, w, (Uses.hg[0] + HG0 * m + 6, Uses.hg[1] + HG1 * m + 5)[w])
                for j, c in enumerate(HG_TILES[w]):
                    last = pe.matmul(mix[w][:, 1, j * P:(j + 1) * P], k_tok[:, w, j, :], v_tok[:, c, :], start=True, stop=True)
                last.then_inc(hg_kv, 1)

        def hg_out_pe(pe, m):
            pe.wait_ge(hg_state, 6 * m + 6)
            pe.wait_ge(mixed[1], Uses.hg[1] + HG1 * m + 4)
            for c in range(NT):
                cols = slice(c * P, (c + 1) * P)
                last = pe.matmul(mix_r[0][:, cols], v_tok[:, c, :], att[:, c, :], start=True, stop=(c == 0))
                if c:
                    for w in range(2):
                        n = c - 1 if w == 0 else 4 - c
                        st = s_in[:, w, :] if n == 0 else s_run[:, w, n - 1, :]
                        last = pe.matmul(mix_r[0][:, cols], st, q_lev[:, (LEVELS + w) % 2, cols], start=False, stop=(w == 1))
            last.then_inc(hg_o, 1)

        def hg_ss_pe(pe, m):
            pe.wait_ge(hg_osq, m + 1)
            for b in range(2):
                last = pe.matmul(mix[1][:, b, 0:HT], ones[:], o_sq[:, b * HT:(b + 1) * HT], start=True, stop=True)
            last.then_inc(hg_ss, 1)

        def hg_body_pe(pe, m, name, i):
            def next_head(p, ks=None):
                project(pe, name, p, i, h_hi, h_lo, ks=ks)

            next_head(0)
            hg_vt_pe(pe, m)
            next_head(1, range(0, 2))
            hg_unit_pe(pe, m, 0)
            next_head(1, range(2, 5))
            hg_unit_pe(pe, m, 1)
            next_head(1, range(5, 8))
            hg_unit_pe(pe, m, 2)
            next_head(2, range(0, 3))
            hg_unit_pe(pe, m, 3)
            next_head(2, range(3, 6))
            hg_unit_pe(pe, m, 4)
            next_head(2, range(6, 8))
            next_head(3, range(0, 1))
            hg_unit_pe(pe, m, 5)
            next_head(3, range(1, 4))
            hg_unit_pe(pe, m, 6)
            next_head(3, range(4, 6))
            hg_unit_pe(pe, m, 7)
            next_head(3, range(6, 8))
            next_head(4, range(0, 1))
            hg_kt_pe(pe, m)
            next_head(4, range(1, 3))
            hg_kv_pe(pe, m)
            next_head(4, range(3, 6))
            hg_out_pe(pe, m)
            next_head(4, range(6, 8))
            hg_ss_pe(pe, m)

        K_, Q2_, V0_, V1_, G0_, G1_ = range(6)
        rt_rot, rt_tmp, rt_kq, rt_sc, rt_att = (sem("ret_" + n) for n in ("rot", "tmp", "kq", "scores", "att"))
        rt_kt, rt_ktok, rt_kv, rt_qdec, rt_state = (sem("ret_" + n) for n in ("kt", "ktok", "kv", "qdec", "state"))
        rt_o, rt_osq, rt_ss, rt_ln, rt_rstd, rt_out = (sem("ret_" + n) for n in ("o", "osq", "ss", "ln", "rstd", "out"))
        rt_vt, rt_sin_ld, rt_fin, rt_dmat, rt_exp = (sem("ret_" + n) for n in ("vt", "sin", "fin", "dmat", "exp"))
        tab_in, masks_in = sem("tab_in"), sem("masks_in")

        def ret_tables_act(act):
            act.wait_ge(hg_out, HG_HEADS + 1)
            act.wait_ge(states_out, 16 * (HG_HEADS + 1))
            for n, (dst, src) in enumerate(((cos[:], d["cos"]), (sin[:], d["sin"]), (dist, d["dist"]), (upper, d["upper"]),
                                            (lower, d["lower"]), (rows, d["rows"].rearrange("p (d t) -> p d t", d=2)))):
                act.dma_start(dst, src).then_inc(tab_in, 16)
            act.wait_ge(tab_in, 16 * 6)
            for n in range(RET_HEADS):
                for w in range(2):
                    col = RET_HEADS * w + n
                    act.activation(q_rows[:, col, :], rows[:, w, :], ACT.Exp, scale=log_gam[:, col:col + 1])
                if n:
                    act.wait_ge(rt_dmat, n)
                act.activation(e_mat[:, 0, :], dist, ACT.Exp, scale=log_gam[:, n:n + 1])
                act.activation(e_mat[:, 1, :], dist, ACT.Exp, scale=log_gam[:, RET_HEADS + n:RET_HEADS + n + 1]).then_inc(rt_exp, 1)

        def ret_tables_dve(dve):
            for n in range(RET_HEADS):
                dve.wait_ge(rt_exp, n + 1)
                dve.tensor_tensor(r_tmp[:, 1, 2 * P:3 * P], e_mat[:, 0, :], upper, ALU.mult)
                dve.tensor_tensor(r_tmp[:, 1, 3 * P:4 * P], e_mat[:, 1, :], lower, ALU.mult).then_inc(rt_tmp, 1)
                dve.wait_ge(rt_tmp, n + 1)
                dve.tensor_tensor(d_mat[:, n, :], r_tmp[:, 1, 2 * P:3 * P], r_tmp[:, 1, 3 * P:4 * P], ALU.add).then_inc(rt_dmat, 1)

        def ret_evac(act, h, p):
            projected(act, "ret", p, h)
            first = isinstance(h, int) and h == 0
            if first and p < 5:
                s, n = ((hg_sig, 6 * HG_HEADS), (hg_sig, 6 * HG_HEADS), (hg_query, HG_HEADS), (hg_og, HG_HEADS),
                        (hg_vt, HG_HEADS))[p]
                act.wait_ge(s, n)
            if first and p in (K_, Q2_, V0_, V1_):
                pass
            elif p in (K_, Q2_):
                act.wait_ge(rt_kq, 2 * h)
            elif p in (V0_, V1_):
                act.wait_ge(rt_vt, 2 * h)
            else:
                act.wait_ge(rt_out, 2 * h + 1)
            g = ST.phase["ret"][2][p]
            func, scale = (ACT.Silu if p >= G0_ else ACT.Copy), (float(RET_DK) ** -0.5 if p == K_ else 1.0)
            act.activation(halves(r_pre[:, p, :]), acc_v[g], func, scale=scale).then_inc(evacuated[g], 1)

        def gate_evac(act, p, n):
            projected(act, "gate", p, n)
            act.wait_ge(merge_done, n + 1)
            act.activation(halves(sig_buf[:, p, :]), acc_v[p], ACT.Sigmoid).then_inc(evacuated[p], 1)

        def ret_act(act, m, h):
            act.wait_ge(rt_out, 2 * m + 1)
            for e in range(2):
                act.wait_ge(rt_vt, 2 * m + e + 1)
                act.activation(r_v[:, :, e, :], tiles5(mix_r[e][:, 0:T]), ACT.Copy).then_inc(mixed[e], 1)
            act.dma_start(r_sin[:], d["s_ret"][m]).then_inc(rt_sin_ld, 16)
            if h is not None:
                for p in range(3):
                    ret_evac(act, h, p)
            else:
                act.wait_ge(rt_kq, 2 * RET_HEADS)
                gate_evac(act, 0, 0)
            act.wait_ge(rt_fin, m + 1)
            act.dma_start(d["out_ret"][m], r_sfin[:]).then_inc(states_out, 16)
            if h is None:
                gate_evac(act, 1, 0)
            act.preload_act_table_set("natural_log_exp_and_others")
            for e in range(2):
                act.wait_ge(rt_o, 2 * m + e + 1)
                act.activation(r_tmp[:, e, :], mix_r[e][:, 0:T], ACT.Square).then_inc(rt_osq, 1)
            if h is not None:
                ret_evac(act, h, V1_)
            act.wait_ge(rt_ss, m + 1)
            act.activation(halves(r_tmp[:, 0, :]), mix_v[0], ACT.Ln, bias=eps[:, 0:1], scale=1.0 / RET_DV).then_inc(mixed[0], 1)
            act.wait_ge(mixed[0], Uses.ret[0] + RT0 * (m + 1))
            act.activation(r_tmp[:, 1, :], r_tmp[:, 0, :], ACT.Exp, scale=-0.5).then_inc(rt_rstd, 1)
            if h is not None:
                for p in range(4, 6):
                    ret_evac(act, h, p)

        def ret_dve(dve, m):
            dve.wait_ge(rt_out, 2 * m + 1)
            for w, (p, dst) in enumerate(((K_, 0), (Q2_, 1))):
                dve.wait_ge(rt_rot, 2 * m + w + 1)
                dve.tensor_tensor(halves(r_tmp[:, w, :]), mix_v[w], halves(sin[:]), ALU.mult).then_inc(mixed[w], 1)
                acc_read(dve, "ret", p, m)
                dve.tensor_tensor(r_rot[:, dst, :], r_pre[:, p, :], cos[:], ALU.mult).then_inc(rt_tmp, 1)
                dve.wait_ge(rt_tmp, RET_HEADS + 2 * m + w + 1)
                dve.wait_ge(mixed[w], (Uses.ret[w] + (RT0, RT1)[w] * m + 2))
                dve.tensor_tensor(r_rot[:, dst, :], r_rot[:, dst, :], r_tmp[:, w, :], ALU.add).then_inc(rt_kq, 1)
            dve.wait_ge(rt_kq, 2 * m + 2)
            for w in range(2):
                row = q_rows[:, bass.ds(RET_HEADS * w + m, 1), :].to_broadcast([P, 4, P])
                dve.tensor_tensor(r_qdec[:, w, :].rearrange("p (c t) -> p c t", c=4),
                                  r_rot[:, 1, CTX:T].rearrange("p (c t) -> p c t", c=4), row, ALU.mult).then_inc(rt_qdec, 1)
            dve.wait_ge(rt_sc, m + 1)
            dve.wait_ge(rt_dmat, RET_HEADS)
            dve.tensor_tensor(r_att[:], tiles5(mix_r[0][:, 0:T]), d_mat[:, bass.ds(m, 1), :].to_broadcast([P, NT, P]),
                              ALU.mult).then_inc(mixed[0], 1)
            dve.wait_ge(rt_kt, m + 1)
            kt5 = tiles5(mix_r[1][:, 0:T])
            dve.tensor_scalar(r_ktok[:, 0], kt5[:, 0:4, :], k_decay[:, bass.ds(m, 1)], None, ALU.mult)
            dve.tensor_scalar(r_ktok[:, 1, 0, :], kt5[:, 0, :], k_decay[:, bass.ds(RET_HEADS + m, 1)], None, ALU.mult)
            dve.tensor_scalar(r_ktok[:, 1, 1:4, :], kt5[:, 2:5, :], k_decay[:, bass.ds(RET_HEADS + m, 1)], None,
                              ALU.mult).then_inc(mixed[1], 1)
            dve.wait_ge(rt_kv, 2 * m + 2)
            dve.wait_ge(states_out, 16 * (HG_HEADS + m + 1))
            dve.wait_ge(rt_sin_ld, 16 * (m + 1))
            dve.tensor_copy(r_sfin[:, 0, :], mix_r[0][:, 0:RET_DV])
            dve.tensor_copy(r_sfin[:, 1, :], mix_r[1][:, 0:RET_DV]).then_inc(rt_fin, 1)
            for n in range(3):
                for w in range(2):
                    j = 1 + n if w == 0 else 3 - n
                    kv = mix_r[w][:, j * RET_DV:(j + 1) * RET_DV]
                    old = r_sin[:, w, :] if n == 0 else r_srun[:, w, n - 1, :]
                    if n:
                        dve.wait_ge(rt_state, 6 * m + 2 * (n - 1) + w + 1)
                    dve.scalar_tensor_tensor(out=r_srun[:, w, n, :], in0=old,
                                             scalar=c_decay[:, bass.ds(RET_HEADS * w + m, 1)],
                                             in1=kv, op0=ALU.mult, op1=ALU.add).then_inc(rt_state, 1)
            for e in range(2):
                dve.wait_ge(rt_osq, 2 * m + e + 1)
                acc_read(dve, "ret", G0_ + e, m)
                dve.tensor_tensor(r_pre[:, G0_ + e, :], mix_r[e][:, 0:T], r_pre[:, G0_ + e, :], ALU.mult).then_inc(mixed[e], 1)
            dve.wait_ge(mixed[1], Uses.ret[1] + RT1 * (m + 1))
            dve.wait_ge(mixed[0], Uses.ret[0] + RT0 * (m + 1))
            dve.wait_ge(rt_rstd, m + 1)
            for e in range(2):
                dve.tensor_tensor(o_ret[:, m * 2 + e, :], r_pre[:, G0_ + e, :], r_tmp[:, 1, :], ALU.mult).then_inc(rt_out, 1)

        def ret_vt_pe(pe, m):
            for e in range(2):
                acc_read(pe, "ret", V0_ + e, m)
                mix_free(pe, e, Uses.ret[e] + (RT0, RT1)[e] * m)
                for c in range(NT):
                    last = pe.transpose(mix_r[e][:, c * P:(c + 1) * P], r_pre[:, V0_ + e, c * P:(c + 1) * P], ident[:])
                last.then_inc(rt_vt, 1)

        def ret_rot_pe(pe, m):
            for w, p in enumerate((K_, Q2_)):
                acc_read(pe, "ret", p, m)
                mix_free(pe, w, Uses.ret[w] + (RT0, RT1)[w] * m + 1)
                for b in range(2):
                    last = pe.matmul(mix[w][:, b, 0:HT], perm[:], r_pre[:, p, b * HT:(b + 1) * HT], start=True, stop=True)
                last.then_inc(rt_rot, 1)

        def ret_scores_pe(pe, m):
            pe.wait_ge(rt_kq, 2 * m + 2)
            mix_free(pe, 0, Uses.ret[0] + RT0 * m + 2)
            for c in range(NT):
                cols = slice(c * P, (c + 1) * P)
                last = pe.matmul(mix_r[0][:, cols], r_rot[:, 0, cols], r_rot[:, 1, cols], start=True, stop=True)
            last.then_inc(rt_sc, 1)
            mix_free(pe, 1, Uses.ret[1] + RT1 * m + 2)
            for c in range(NT):
                cols = slice(c * P, (c + 1) * P)
                last = pe.transpose(mix_r[1][:, cols], r_rot[:, 0, cols], ident[:])
            last.then_inc(rt_kt, 1)

        def ret_kv_pe(pe, m):
            tiles = ((0, 1, 2, 3), (0, 2, 3, 4))
            for w in (1, 0):
                mix_free(pe, 1, Uses.ret[1] + RT1 * m + 3)
                if w == 0:
                    mix_free(pe, 0, Uses.ret[0] + RT0 * m + 3)
                for j, c in enumerate(tiles[w]):
                    last = pe.matmul(mix_r[w][:, j * RET_DV:(j + 1) * RET_DV], r_ktok[:, w, j, :],
                                     r_v[:, c].rearrange("p e t -> p (e t)"), start=True, stop=True)
                last.then_inc(rt_kv, 1)

        def ret_out_pe(pe, m):
            pe.wait_ge(rt_qdec, 2 * m + 2)
            pe.wait_ge(rt_state, 6 * m + 6)
            for e in range(2):
                dv = slice(e * P, (e + 1) * P)
                for c in range(NT):
                    cols, lat = slice(c * P, (c + 1) * P), slice((c - 1) * P, c * P)
                    last = pe.matmul(mix_r[e][:, cols], r_v[:, c, e, :], r_att[:, c, :], start=True, stop=(c == 0))
                    if c:
                        for w in range(2):
                            n = c - 1 if w == 0 else 4 - c
                            st = r_sin[:, w, dv] if n == 0 else r_srun[:, w, n - 1, dv]
                            last = pe.matmul(mix_r[e][:, cols], st, r_qdec[:, w, lat], start=False, stop=(w == 1))
                last.then_inc(rt_o, 1)

        def ret_ss_pe(pe, m):
            pe.wait_ge(rt_osq, 2 * m + 2)
            mix_free(pe, 0, Uses.ret[0] + RT0 * m + 4)
            for b in range(2):
                for e in range(2):
                    last = pe.matmul(mix[0][:, b, 0:HT], ones[:], r_tmp[:, e, b * HT:(b + 1) * HT],
                                     start=(e == 0), stop=(e == 1))
            last.then_inc(rt_ss, 1)

        part_hi, part_lo = sem("part_hi"), sem("part_lo")
        merge_done = sem("merge_done")

        block = ctx.enter_context(nc.Block())

        @block.sync
        def _(sp):
            sp.dma_start(c_row[:].rearrange("p e k -> p (e k)"), d["in_c"].to_broadcast([P, 2 * D_MODEL])).then_inc(in_c, 16)
            for s in range(ADA_SLOTS):
                load_ada(sp, s, s, 0)
            for n, w in C_NAMES:
                sp.dma_start(small[n][:], d["in_" + n]).then_inc(in_small, 16)
            sp.dma_start(x[:], d["x"]).then_inc(in_x, 16)
            with sp.Fori(1, ADA_PLAN[0][1]) as i:
                for s in range(ADA_SLOTS):
                    load_ada(sp, i * ADA_SLOTS + s, s, i * ADA_SLOTS + s + 1 - ADA_SLOTS)
            sp.dma_start(ident[:], d["ident"]).then_inc(in_tab, 16)
            sp.dma_start(perm[:], d["perm"]).then_inc(in_tab, 16)
            for f in (1, 2):
                if f == 2:
                    for name in ("hg", "ret", "gate", "wo"):
                        steps, slots, _, _, _, _ = ST.phase[name]
                        with sp.Fori(0, steps) as i:
                            for p in range(len(slots)):
                                load_slab(sp, name, p, i)
                for c in range(len(FF_CHUNKS)):
                    with sp.Fori(0, FF_CHUNKS[c]) as i:
                        for p in range(2):
                            load_slab(sp, f"up{f}{c}", p, i)
                        if f == 1:
                            load_ada_step(sp, f"up{f}{c}", i)
                    with sp.Fori(0, KT // 2) as i:
                        for p in range(2):
                            load_slab(sp, f"down{f}{c}", p, i)
                        if f == 1:
                            load_ada_step(sp, f"down{f}{c}", i)
            for k in range(KT):
                sp.wait_ge(xn_done, 3 * KT + k + 1)
                sp.dma_start(d["y"][:, k, :], x[:, k, :]).then_inc(y_out, 16)
            sp.wait_ge(y_out, 16 * KT)
            sp.wait_ge(states_out, 16 * (HG_HEADS + RET_HEADS + 1))

        @block.gpsimd
        def _(pool):
            pool.sem_inc(split_done, CREDIT)
            pool.sem_inc(sq_added, SQ_CREDIT)
            square_clear(pool, 0)
            with pool.Fori(0, KT // 2) as i:
                square_add(pool, 0, i)
            for name, steps, slots, _ in PHASES:
                if name == "hg":
                    split_hg(pool)
                elif name in LAST.values():
                    n = {v: k for k, v in LAST.items()}[name]
                    for p in range(2):
                        split_slab(pool, name, p, 0)
                    if n == 2:
                        pool.wait_ge(part_lo, 3 * KT)
                    square_clear(pool, n)
                    with pool.Fori(1, steps) as i:
                        for p in range(2):
                            split_slab(pool, name, p, i)
                        square_add(pool, n, i - 1)
                    square_add(pool, n, steps - 1)
                else:
                    with pool.Fori(1 if name == "ret" else 0, steps) as i:
                        for p in range(len(slots)):
                            split_slab(pool, name, p, i)

        @block.tensor
        def _(pe):
            pe.sem_inc(slab_done, CREDIT)
            pe.sem_inc(evacuated[0], 1)
            pe.sem_inc(evacuated[1], 1)
            pe.sem_inc(mixed[0], 1)
            pe.sem_inc(mixed[1], 1)
            pe.wait_ge(ones_set, 1)
            norm_pe(pe, 0, Uses.norm1[1])
            for c in range(len(FF_CHUNKS)):
                ff_pe(pe, 1, c, u_base(1, c))
            norm_pe(pe, 1, Uses.norm2[1])
            pe.wait_ge(in_tab, 32)
            project_pair(pe, "hg", h_hi, h_lo, (hlo_done, KT))
            for p in range(2, 5):
                project(pe, "hg", p, 0, h_hi, h_lo)
            with pe.Fori(1, HG_HEADS) as h:
                hg_body_pe(pe, h - 1, "hg", h)
            hg_body_pe(pe, HG_HEADS - 1, "ret", 0)
            project(pe, "ret", 5, 0, h_hi, h_lo)
            ret_vt_pe(pe, 0)
            with pe.Fori(1, RET_HEADS) as h:
                project(pe, "ret", 0, h, h_hi, h_lo)
                ret_rot_pe(pe, h - 1)
                project(pe, "ret", 1, h, h_hi, h_lo)
                ret_scores_pe(pe, h - 1)
                project(pe, "ret", 2, h, h_hi, h_lo)
                ret_kv_pe(pe, h - 1)
                project(pe, "ret", 3, h, h_hi, h_lo)
                ret_out_pe(pe, h - 1)
                project(pe, "ret", 4, h, h_hi, h_lo)
                ret_ss_pe(pe, h - 1)
                project(pe, "ret", 5, h, h_hi, h_lo)
                ret_vt_pe(pe, h)
            m = RET_HEADS - 1
            project(pe, "gate", 0, 0, h_hi, h_lo)
            ret_rot_pe(pe, m)
            project(pe, "gate", 1, 0, h_hi, h_lo, ks=range(0, 3))
            ret_scores_pe(pe, m)
            project(pe, "gate", 1, 0, h_hi, h_lo, ks=range(3, 6))
            ret_kv_pe(pe, m)
            project(pe, "gate", 1, 0, h_hi, h_lo, ks=range(6, 8))
            ret_out_pe(pe, m)
            ret_ss_pe(pe, m)
            project(pe, "gate", 2, 0, ret_hi, ret_lo, tiles_done=(part_lo, 0))
            project(pe, "gate", 3, 0, hg_hi, hg_lo, tiles_done=(part_lo, KT))
            with pe.Fori(1, KT) as n:
                project(pe, "gate", 0, n, h_hi, h_lo)
                project(pe, "gate", 1, n, h_hi, h_lo)
                project(pe, "gate", 2, n, ret_hi, ret_lo)
                project(pe, "gate", 3, n, hg_hi, hg_lo)
            project_pair(pe, "wo", h_hi, h_lo, (part_lo, 2 * KT))
            with pe.Fori(1, KT // 2) as i:
                project(pe, "wo", 0, i, h_hi, h_lo)
                project(pe, "wo", 1, i, h_hi, h_lo)
            norm_pe(pe, 2, Uses.norm3[1])
            for c in range(len(FF_CHUNKS)):
                ff_pe(pe, 2, c, u_base(2, c))
            norm_pe(pe, 3, Uses.norm4[1])

        @block.scalar
        def _(act):
            act.sem_inc(states_out, 16)
            act.wait_ge(in_c, 16)
            act.activation(ada_prod[:], c_row[:], ACT.Sigmoid).then_inc(silu_done, 1)
            norm_stats_act(act, 0)
            act.wait_ge(coef_done, 2)
            norm_rows_act(act, 0)
            for c in range(len(FF_CHUNKS)):
                up_act(act, 1, c, u_base(1, c))
                if c == 0:
                    small_chain_act(act)
            norm_stats_act(act, 1)
            act.wait_ge(coef_done, 9)
            norm_rows_act(act, 1)
            act.wait_ge(hlo_done, 2 * KT)
            act.dma_start(masks[:].rearrange("p u t -> p (u t)"), d["masks"]).then_inc(masks_in, 16)
            for p in range(5):
                hg_evac(act, 0, p)
            hg_start_act(act, 0)
            with act.Fori(1, HG_HEADS) as h:
                hg_act(act, h - 1, h, lambda p: hg_evac(act, h, p))
            hg_act(act, HG_HEADS - 1, None, lambda p: ret_evac(act, 0, p))
            ret_evac(act, 0, 5)
            ret_tables_act(act)
            with act.Fori(1, RET_HEADS) as h:
                ret_act(act, h - 1, h)
            ret_act(act, RET_HEADS - 1, None)
            act.wait_ge(rt_out, 2 * RET_HEADS + 1)
            act.wait_ge(states_out, 16 * (HG_HEADS + RET_HEADS + 1))
            for src, dst in ((o_ret, [ret_hi[:, k, :] for k in range(KT)]), (o_hg, hg_hi)):
                for k in range(KT):
                    act.activation(dst[k], src[:, k, :], ACT.Copy).then_inc(part_hi, 1)
            act.preload_act_table_set("sigmoid_and_others")
            with act.Fori(1, KT) as n:
                for p in range(2):
                    gate_evac(act, p, n)
            act.wait_ge(merge_done, KT + 1)
            for k in range(KT):
                act.activation(h_hi[:, k, :], merged[:, k, :], ACT.Copy).then_inc(part_hi, 1)
            norm_stats_act(act, 2)
            norm_rows_act(act, 2)
            for c in range(len(FF_CHUNKS)):
                up_act(act, 2, c, u_base(2, c))
            norm_stats_act(act, 3)

        @block.vector
        def _(dve):
            for credited, n in ((ulo_done, 1), (hg_out, 1), (rt_out, 1), (merge_done, 1), (ada_read, ADA_SLOTS),
                                (ada_moved, 1)):
                dve.sem_inc(credited, n)
            dve.memset(eps[:], EPS)
            dve.memset(ones[:], 1.0).then_inc(ones_set, 1)
            dve.wait_ge(silu_done, 1)
            dve.tensor_tensor(c_row[:], c_row[:], ada_prod[:], ALU.mult).then_inc(silu_done, 1)
            dve.wait_ge(silu_done, 2)
            dve.wait_ge(in_small, 16 * len(C_NAMES))
            with dve.Fori(0, ADA_PLAN[0][1]) as i:
                ada_step(dve, "head", i)
            make_scale(dve, 0)
            norm_dve(dve, 0, Uses.norm1[1])
            for c in range(len(FF_CHUNKS)):
                up_dve(dve, 1, c, u_base(1, c))
                if c == 0:
                    make_gate(dve, 0)
                    small_chain(dve)
                with dve.Fori(0, KT // 2) as i:
                    ada_step(dve, f"down1{c}", i)
                    residual(dve, f"down1{c}", i, G1)
            for n in (1, 2):
                make_scale(dve, n)
                make_gate(dve, n)
            norm_dve(dve, 1, Uses.norm2[1])
            dve.memset(p_b[:, :, 0:1], 0.0)
            dve.wait_ge(masks_in, 16)
            hg_start_dve(dve, 0)
            hg_sums_dve(dve, 0)
            with dve.Fori(1, HG_HEADS) as h:
                hg_dve(dve, h - 1, h)
            hg_dve(dve, HG_HEADS - 1, None)
            ret_tables_dve(dve)
            with dve.Fori(1, RET_HEADS) as h:
                ret_dve(dve, h - 1)
            ret_dve(dve, RET_HEADS - 1)
            for n, (src, hi, lo) in enumerate(((o_ret, [ret_hi[:, k, :] for k in range(KT)], ret_lo), (o_hg, hg_hi, hg_lo))):
                for k in range(KT):
                    dve.wait_ge(part_hi, KT * n + k + 1)
                    dve.tensor_tensor(lo[:, k, :], src[:, k, :], hi[k].bitcast(F32), ALU.subtract).then_inc(part_lo, 1)
            with dve.Fori(0, KT) as n:
                for p in range(2):
                    acc_read(dve, "gate", p, n)
                    projected(dve, "gate", 2 + p, n)
                    dve.tensor_tensor(halves(sig_buf[:, p, :]), halves(sig_buf[:, p, :]), acc_v[p],
                                      ALU.mult).then_inc(evacuated[p], 1)
                for p in range(2):
                    acc_read(dve, "gate", 2 + p, n)
                dve.tensor_tensor(merged[:, n, :], sig_buf[:, 0, :], sig_buf[:, 1, :], ALU.add).then_inc(merge_done, 1)
            for k in range(KT):
                dve.wait_ge(part_hi, 2 * KT + k + 1)
                dve.tensor_tensor(h_lo[:, k, :], merged[:, k, :], h_hi[:, k, :].bitcast(F32), ALU.subtract).then_inc(part_lo, 1)
            with dve.Fori(0, KT // 2) as i:
                residual(dve, "wo", i, G2)
            norm_dve(dve, 2, Uses.norm3[1])
            for c in range(len(FF_CHUNKS)):
                up_dve(dve, 2, c, u_base(2, c))
                with dve.Fori(0, KT // 2) as i:
                    residual(dve, f"down2{c}", i, G3)
            norm_dve(dve, 3, Uses.norm4[1])


def _tiles(w):
    kt, n = w.shape[0] // P, w.shape[1] // P
    return w.reshape(kt, P, n, P).transpose(2, 1, 0, 3).reshape(n, P, kt * P)


def _columns(v):
    return np.ascontiguousarray(v.reshape(-1, P).T)


def _down(w2, c):
    lo = sum(FF_CHUNKS[:c]) * P
    part = _tiles(w2[lo:lo + FF_CHUNKS[c] * P])
    return np.pad(part, ((0, 0), (0, 0), (0, KT * P - part.shape[2])))


def _up(w13, c):
    t = _tiles(w13)
    n = D_FF // P
    lo = sum(FF_CHUNKS[:c])
    ab = np.stack([t[lo:lo + FF_CHUNKS[c]], t[n + lo:n + lo + FF_CHUNKS[c]]], 1)
    return ab.reshape(-1, P, KT * P)


def kernel(**inputs):
    import concourse.bacc as bacc
    from concourse.bass_utils import run_bass_kernel_spmd

    a = {k: np.asarray(v) for k, v in inputs.items()}
    win = _tiles(a["w_in"][0])
    cuts = np.cumsum([0, 512, 512, 1024, 1024, 1024, 1024, 1024, 1024, 1024, 1024, 1024]) // P
    rq, rk, rv, rg, hq, hff, hfb, hi, hog, gr, gh = [win[cuts[n]:cuts[n + 1]] for n in range(11)]
    hg = np.stack([hff, hfb, hq, hog, hi], 1).reshape(-1, P, KT * P)
    ret = np.stack([rk, rq, rv[0::2], rv[1::2], rg[0::2], rg[1::2]], 1).reshape(-1, P, KT * P)
    gate = np.stack([gr, gh, _tiles(a["w_ret_proj"][0]), _tiles(a["w_hg_proj"][0])], 1).reshape(-1, P, KT * P)
    stream = []
    for f in (1, 2):
        if f == 2:
            stream += [hg, ret, gate, _tiles(a["w_o"][0])]
        for c in range(len(FF_CHUNKS)):
            stream += [_up(a[f"ffn{f}_w13"][0], c), _down(a[f"ffn{f}_w2"][0], c)]
    tables, kpos = shape_constants()
    x = np.concatenate([a["x_prompt"][0], a["x_sample"][0]], 0)
    arrays = {
        "w": np.concatenate(stream, 0),
        "ada": a["ada_w"][0].T.reshape(-1, P, D_MODEL),
        "x": np.ascontiguousarray(x.T.reshape(KT, P, T).transpose(1, 0, 2)),
        "s_hg": np.ascontiguousarray(a["state_hgrn"][0, 0].transpose(1, 2, 0, 3)),
        "s_ret": np.ascontiguousarray(a["state_ret"][0, 0].transpose(1, 2, 0, 3)),
        "in_c": np.concatenate([a["c_ctx"], a["c"][0]])[None],
        "in_ada_b": _columns(a["ada_b"][0]),
        "in_norm_w": _columns(a["norm_w"][0]),
        "in_final_w": _columns(a["final_norm_w"]),
        "in_hg_w": _columns(a["hg_norm_w"][0]),
        "in_lb": _columns(a["hg_lb_logits"]),
        "in_decay": np.ascontiguousarray(np.broadcast_to(a["ret_decay"][0].reshape(1, 8), (P, 8))),
        "in_kpos": kpos,
        **tables,
    }
    outs = {"y": (P, KT, T), "out_hg": (HG_HEADS, P, 2, HG_DV), "out_ret": (RET_HEADS, P, 2, RET_DV)}
    nc = bacc.Bacc("TRN2", target_bir_lowering=False, num_devices=1)
    d = {}
    for n, v in arrays.items():
        d[n] = nc.dram_tensor(n + "_dram", v.shape, mybir.dt.from_np(v.dtype), kind="ExternalInput").ap()
    for n, shape in outs.items():
        d[n] = nc.dram_tensor(n + "_dram", shape, F32, kind="ExternalOutput").ap()
    build(nc, d)
    r = run_bass_kernel_spmd(nc, [{n + "_dram": v for n, v in arrays.items()}], core_ids=[0]).results[0]
    y = r["y_dram"].transpose(1, 0, 2).reshape(D_MODEL, T).T
    out_ret = r["out_ret_dram"].transpose(2, 0, 1, 3)[None, None]
    out_hg = r["out_hg_dram"].transpose(2, 0, 1, 3)[None, None]
    return (np.ascontiguousarray(y[:CTX])[None], np.ascontiguousarray(y[CTX:])[None],
            np.ascontiguousarray(out_ret), np.ascontiguousarray(out_hg))
```

```python
from contextlib import ExitStack

import numpy as np

import concourse.bass as bass
from concourse import mybir

F32 = mybir.dt.float32
F32R = mybir.dt.float32r
U32 = mybir.dt.uint32
ALU = mybir.AluOpType
ACT = mybir.ActivationFunctionType

P = 128
D_MODEL = 1024
KT = D_MODEL // P
CTX, LAT = 128, 512
T = CTX + LAT
NT = T // P
HT = T // 2
D_FF = 2816
RET_HEADS, RET_DK, RET_DV = 4, 128, 256
HG_HEADS, HG_DK, HG_DV = 8, 128, 128
GRID_W = 64
ROPE_BASE = 10000.0
EPS = 1e-6
N_MOD = 9
LEVELS = 7
TINY = 2.0 ** -62
SH1, SC1, G1, SH2, SC2, G2, SH3, SC3, G3 = range(N_MOD)

FF_CHUNKS = (8, 8, 6)
ADA_SLOTS = 4
HEAD_DVE, HEAD_PE = 9, 7
ADA_PLAN = []
for _c, _n in enumerate(FF_CHUNKS):
    ADA_PLAN += [(f"up1{_c}", _n // 2, 4), (f"down1{_c}", KT // 4, 2)]
SLOTS = 3
CREDIT = 4

PHASES = []
for _f in (1, 2):
    if _f == 2:
        PHASES += [("hg", HG_HEADS, (0, 1, 2, 0, 1), (0, 1, 0, 1, 0)),
                   ("ret", RET_HEADS, (0, 1, 2, 0, 1, 2), (0, 1, 0, 1, 0, 1)),
                   ("gate", KT, (0, 1, 2, 1), (0, 1, 0, 1)),
                   ("wo", KT // 4, (0, 2, 1, 2), (0, 1, 0, 1))]
    for _c, _n in enumerate(FF_CHUNKS):
        PHASES += [(f"up{_f}{_c}", _n // 2, (0, 1, 2, 1), (0, 1, 0, 1)),
                   (f"down{_f}{_c}", KT // 4, (0, 1, 2, 1), (0, 1, 0, 1))]


class Stream:

    def __init__(self):
        self.phase, at, slots, sets, order = {}, 0, [0] * SLOTS, [0, 0], []
        for name, steps, slot, group in PHASES:
            self.phase[name] = (steps, slot, group, at, tuple(slots), tuple(sets))
            order += list(slot) * steps
            at += steps * len(slot)
            for s in slot:
                slots[s] += steps
            for g in group:
                sets[g] += steps
        self.total, self.gap = at, {}
        for name, (steps, slot, _, base, _, _) in self.phase.items():
            for p in range(len(slot)):
                gaps = []
                for i in range(steps):
                    n = base + i * len(slot) + p
                    before = [m for m in range(n) if order[m] == order[n]]
                    gaps.append(n - before[-1] if before else CREDIT)
                self.gap[name, p] = min(gaps)

    def index(self, name, p, i):
        _, slot, _, base, _, _ = self.phase[name]
        return base + i * len(slot) + p

    def after(self, name, p, i):
        return self.index(name, p, i) + 1 + CREDIT

    def slot_clear(self, name, p, i):
        return self.after(name, p, i) - self.gap[name, p]

    def loads(self, name, p, i):
        _, slot, _, _, slots, _ = self.phase[name]
        return slots[slot[p]] + i * slot.count(slot[p]) + slot[:p].count(slot[p]) + 1

    def uses(self, name, p, i):
        _, _, group, _, _, sets = self.phase[name]
        return sets[group[p]] + i * group.count(group[p]) + group[:p].count(group[p]) + 1


ST = Stream()


class Ada:

    def __init__(self):
        self.first, self.loads, self.total = {}, {}, HEAD_DVE
        loads = [len(range(s, HEAD_DVE, ADA_SLOTS)) for s in range(ADA_SLOTS)]
        for name, steps, per in ADA_PLAN:
            self.first[name], self.loads[name] = self.total, tuple(loads)
            self.total += steps * per
            for s in range(per):
                loads[s] += steps


ADA = Ada()
assert HEAD_DVE + HEAD_PE == 2 * KT and ADA.total + HEAD_PE == N_MOD * KT
C_NAMES = [("ada_b", 72), ("norm_w", 24), ("final_w", 8), ("hg_w", 8), ("lb", 32), ("decay", 8), ("kpos", 2)]


def shape_constants():
    s, t = np.arange(P)[:, None], np.arange(P)[None, :]
    ident = (s == t).astype(np.float32)
    q = RET_DK // 4
    perm = np.zeros((P, P), np.float32)
    for base in (0, 2 * q):
        for j in range(q):
            perm[base + q + j, base + j] = -1.0
            perm[base + j, base + q + j] = 1.0
    freq = np.float32(ROPE_BASE) ** (-np.arange(q, dtype=np.float32) / np.float32(q))
    n = np.arange(LAT)
    row, col = (n // GRID_W).astype(np.float32), (n % GRID_W).astype(np.float32)
    ang = np.concatenate([freq[:, None] * row, freq[:, None] * row, freq[:, None] * col, freq[:, None] * col])
    ang = ang.astype(np.float32)
    cos = np.concatenate([np.ones((P, CTX), np.float32), np.cos(ang)], 1)
    sin = np.concatenate([np.zeros((P, CTX), np.float32), np.sin(ang)], 1)
    dist = np.abs(t - s).astype(np.float32)
    upper, lower = (t >= s).astype(np.float32), (t <= s).astype(np.float32)
    rows = np.stack([np.broadcast_to(t + 1, (P, P)), np.broadcast_to(P - t, (P, P))], 1).astype(np.float32)
    masks = np.zeros((P, LEVELS, P), np.uint32)
    for u in range(LEVELS):
        half = 1 << u
        masks[:, u, :] = (s // (2 * half) == t // (2 * half)) & (s // half != t // half)
    kpos = np.stack([P - 1 - np.arange(P), np.arange(P)], 1).astype(np.float32)
    return dict(ident=ident, perm=perm, cos=cos, sin=sin, dist=dist, upper=upper, lower=lower,
                rows=rows.reshape(P, 2 * P), masks=masks.reshape(P, LEVELS * P)), kpos


def build(nc, d):
    ctx = ExitStack()
    with ctx:
        def sb(name, shape, dt=F32, scope=ctx):
            return scope.enter_context(nc.sbuf_tensor(name, shape, dt))

        def sem(name):
            return ctx.enter_context(nc.semaphore(name))

        x = sb("x", [P, KT, T])
        h_hi, h_lo = sb("h_hi", [P, KT, T], F32R), sb("h_lo", [P, KT, T], F32R)
        w_hi = sb("w_hi", [P, SLOTS, KT * P], F32R)
        w_lo = sb("w_lo", [P, SLOTS, KT * P], F32R)
        raw = sb("raw", [P, SLOTS, KT * P])
        small = {n: sb("in_" + n, [P, w]) for n, w in C_NAMES}
        mod = sb("mod", [P, N_MOD, KT, 2])
        ident, perm, ones = sb("ident", [P, P]), sb("perm", [P, P]), sb("ones", [P, P])
        eps = sb("eps", [P, 1])
        lb, lb_rest = sb("lb", [P, 2 * KT]), sb("lb_rest", [P, 2 * KT])
        log_gam, gam_tmp = sb("log_gam", [P, 8]), sb("gam_tmp", [P, 5, 8])
        k_decay, c_decay = sb("k_decay", [P, 8]), sb("c_decay", [P, 8])
        soft = sb("soft", [P, 4, 16])
        scope = ExitStack()
        ada_pe = sb("ada_pe", [P, HEAD_PE, KT * P], F32, scope)
        scope.close()
        scope = ExitStack()
        u_hi, u_lo = sb("u_hi", [P, 8, T], F32R, scope), sb("u_lo", [P, 8, T], F32R, scope)
        gate_a, u_full = sb("gate_a", [P, T], F32, scope), sb("u_full", [P, T], F32, scope)
        square = sb("square", [P, 2, T], F32, scope)
        log_ms, rstd = sb("log_ms", [P, T], F32, scope), sb("rstd", [P, T], F32, scope)
        x_norm, h_full = sb("x_norm", [P, 2, T], F32, scope), sb("h_full", [P, 2, T], F32, scope)
        ada_raw = sb("ada_raw", [P, ADA_SLOTS, D_MODEL], F32, scope)
        c_row, ada_prod = sb("c_row", [P, 2, D_MODEL], F32, scope), sb("ada_prod", [P, 2, D_MODEL], F32, scope)
        ada_sum = sb("ada_sum", [P, ADA_SLOTS, 2], F32, scope)
        c_col, c_sig = sb("c_col", [P, KT, 2], F32, scope), sb("c_sig", [P, KT, 2], F32, scope)
        sq_sum = sb("sq_sum", [P, 2, T], F32, scope)
        scope.close()
        mixer = ExitStack()
        o_hg = sb("o_hg", [P, KT, T], F32, mixer)
        pre = sb("pre", [P, 6, T], F32, mixer)
        scope = ExitStack()
        q, k_f, k_b = (sb(n, [P, T], F32, scope) for n in ("hg_q", "hg_kf", "hg_kb"))
        g_f, g_b, b_f = (sb(n, [P, T], F32, scope) for n in ("hg_gf", "hg_gb", "hg_bf"))
        p_b = sb("hg_pb", [P, NT, P + 1], F32, scope)
        out_gate, out_sig = sb("hg_outgate", [P, T], F32, scope), sb("hg_outsig", [P, T], F32, scope)
        o_sq, o_rstd, o_gated = (sb(n, [P, T], F32, scope) for n in ("hg_osquare", "hg_orstd", "hg_ogated"))
        v_tok = sb("hg_v", [P, NT, P], F32, scope)
        e_f, e_b = sb("hg_ef", [P, 2, T], F32, scope), sb("hg_eb", [P, 2, T], F32, scope)
        q_lev, k_lev = sb("hg_qlev", [P, 2, T], F32, scope), sb("hg_klev", [P, 2, T], F32, scope)
        att = sb("hg_att", [P, NT, P], F32, scope)
        k_tok = sb("hg_ktok", [P, 2, 4, P], F32, scope)
        s_in, s_run = sb("hg_sin", [P, 2, P], F32, scope), sb("hg_srun", [P, 2, 3, P], F32, scope)
        masks = sb("hg_masks", [P, LEVELS, P], U32, scope)
        s_fin, s_dec = sb("hg_sfin", [P, 2, P], F32, scope), sb("hg_sdec", [P, 2, NT], F32, scope)
        scope.close()
        o_ret = sb("o_ret", [P, KT, T], F32, mixer)
        scope = ExitStack()
        r_pre = pre
        r_rot = sb("ret_rot", [P, 2, T], F32, scope)
        r_tmp = sb("ret_tmp", [P, 2, T], F32, scope)
        r_att = sb("ret_att", [P, NT, P], F32, scope)
        r_v = sb("ret_v", [P, NT, 2, P], F32, scope)
        r_sin, _ = sb("ret_sin", [P, 2, RET_DV], F32, scope), sb("ret_pad", [P, P], F32, scope)
        cos, sin = sb("cos", [P, T], F32, scope), sb("sin", [P, T], F32, scope)
        d_mat = sb("ret_d", [P, RET_HEADS, P], F32, scope)
        q_rows = sb("ret_qrows", [P, 8, P], F32, scope)
        r_ktok = sb("ret_ktok", [P, 2, 4, P], F32, scope)
        r_qdec = sb("ret_qdec", [P, 2, LAT], F32, scope)
        r_srun = sb("ret_srun", [P, 2, 3, RET_DV], F32, scope)
        r_sfin = sb("ret_sfin", [P, 2, RET_DV], F32, scope)
        scope.close()
        mixer.close()
        scope = ExitStack()
        hg_lo = sb("hg_lo", [P, KT, T], F32R, scope)
        sig_buf, hg_hi_a = sb("sig_buf", [P, 2, T], F32, scope), sb("hg_hi_a", [P, 4, T], F32R, scope)
        ret_lo = sb("ret_lo", [P, KT, T], F32R, scope)
        ret_hi, hg_hi_b = sb("ret_hi", [P, KT, T], F32R, scope), sb("hg_hi_b", [P, 4, T], F32R, scope)
        merged = sb("merged", [P, KT, T], F32, scope)
        hg_hi = [hg_hi_a[:, k, :] for k in (0, 1)] + [hg_hi_b[:, k, :] for k in range(4)] + [hg_hi_a[:, k, :] for k in (2, 3)]
        HG_EARLY = 6
        scope.close()
        dist = r_tmp[:, 0, 0:P]
        upper, lower = r_tmp[:, 0, P:2 * P], r_tmp[:, 0, 2 * P:3 * P]
        rows = r_tmp[:, 0, 3 * P:5 * P].rearrange("p (d t) -> p d t", d=2)
        e_mat = r_tmp[:, 1, 0:2 * P].rearrange("p (d t) -> p d t", d=2)

        acc = [ctx.enter_context(nc.psum_tensor(f"acc{g}", [P, 2, 512], F32)) for g in range(2)]
        mix = [ctx.enter_context(nc.psum_tensor(f"mix{g}", [P, 2, 512], F32)) for g in range(2)]
        acc_v = [a[:, :, 0:HT] for a in acc]
        mix_v = [m[:, :, 0:HT] for m in mix]
        mix_r = [m[:].rearrange("p b n -> p (b n)") for m in mix]

        def halves(ap):
            return ap.rearrange("p (b n) -> p b n", b=2)

        loaded = [sem(f"slab_loaded{s}") for s in range(SLOTS)]
        hi_done, split_done, slab_done = sem("hi_done"), sem("split_done"), sem("slab_done")
        evacuated = [sem(f"acc_evacuated{g}") for g in range(2)]
        mixed = [sem(f"mix_evacuated{g}") for g in range(2)]
        in_c, in_small, in_tab = sem("in_c"), sem("in_small"), sem("in_tab")
        in_x = [sem(f"in_x{n}") for n in range(2)]
        ada_pe_loaded = [sem(f"ada_pe_loaded{m}") for m in range(HEAD_PE)]
        ada_pe_done, silu_col_done = sem("ada_pe_done"), sem("silu_col_done")
        ones_set, silu_done = sem("ones_set"), sem("silu_done")
        ada_loaded = [sem(f"ada_loaded{s}") for s in range(ADA_SLOTS)]
        ada_read, ada_moved = sem("ada_read"), sem("ada_moved")
        small_done, small_act = sem("small_done"), sem("small_act")
        coef_done = sem("coef_done")
        sq_done, sq_summed, rstd_done, log_done = sem("sq_done"), sem("sq_summed"), sem("rstd_done"), sem("log_done")
        xn_done, mod_done, hhi_done, hlo_done = sem("xn_done"), sem("mod_done"), sem("hhi_done"), sem("hlo_done")
        uhi_done, ulo_done = sem("uhi_done"), sem("ulo_done")
        y_out, states_out = sem("y_out"), sem("states_out")

        pool_waited, dve_waited = sem("pool_waited"), sem("dve_waited")

        def load_slab(sp, name, p, i):
            slot = ST.phase[name][1][p]
            sp.wait_ge(split_done, ST.slot_clear(name, p, i))
            sp.dma_start(raw[:, slot, :], d["w"][ST.index(name, p, i)]).then_inc(loaded[slot], 16)

        def split_slab(pool, name, p, i):
            slot = ST.phase[name][1][p]
            pool.wait_ge(loaded[slot], 16 * ST.loads(name, p, i))
            pool.wait_ge(slab_done, ST.slot_clear(name, p, i))
            pool.sem_inc(pool_waited, 1)
            pool.tensor_scalar(w_hi[:, slot, :], raw[:, slot, :], 1.0, 1.0, ALU.mult, ALU.mult).then_inc(hi_done, 1)
            pool.wait_ge(hi_done, ST.index(name, p, i) + 1)
            pool.tensor_tensor(w_lo[:, slot, :], raw[:, slot, :], w_hi[:, slot, :].bitcast(F32),
                               ALU.subtract).then_inc(split_done, 1)

        def products(pe, name, p, k, src_hi, src_lo, k_tiles=KT):
            _, slots, sets, _, _, _ = ST.phase[name]
            s, g = slots[p], sets[p]
            for n, (w, r) in enumerate(((w_hi, src_hi), (w_hi, src_lo), (w_lo, src_hi))):
                tile = r[k] if isinstance(r, list) else r[:, k, :]
                for b in range(2):
                    last = pe.matmul(acc[g][:, b, 0:HT], w[:, s, k * P:(k + 1) * P], tile[:, b * HT:(b + 1) * HT],
                                     start=(k == 0 and n == 0), stop=(k == k_tiles - 1 and n == 2))
            if k == k_tiles - 1:
                last.then_inc(slab_done, 1)

        def project(pe, name, p, i, src_hi, src_lo, k_tiles=KT, ks=None, tiles_done=None):
            ks = ks or range(k_tiles)
            if ks[0] == 0:
                pe.wait_ge(split_done, ST.after(name, p, i))
                pe.wait_ge(evacuated[ST.phase[name][2][p]], ST.uses(name, p, i))
            for k in ks:
                if tiles_done:
                    pe.wait_ge(tiles_done[0], tiles_done[1] + k + 1)
                products(pe, name, p, k, src_hi, src_lo, k_tiles)

        def project_pair(pe, name, src_hi, src_lo, tiles_done):
            for p in range(2):
                pe.wait_ge(split_done, ST.after(name, p, 0))
                pe.wait_ge(evacuated[ST.phase[name][2][p]], ST.uses(name, p, 0))
            for k in range(KT):
                pe.wait_ge(tiles_done[0], tiles_done[1] + k + 1)
                for p in range(2):
                    products(pe, name, p, k, src_hi, src_lo)

        def projected(eng, name, p, i):
            eng.wait_ge(slab_done, ST.after(name, p, i))

        def acc_read(eng, name, p, i):
            eng.wait_ge(evacuated[ST.phase[name][2][p]], ST.uses(name, p, i) + 1)

        HG0, HG1, RT0, RT1 = 7, 6, 5, 4

        class Uses:
            norm1 = [1, 1]
            norm2 = [norm1[0] + 1, norm1[1] + 1]
            hg = [norm2[0], norm2[1] + 1]
            ret = [hg[0] + HG0 * HG_HEADS, hg[1] + HG1 * HG_HEADS]
            norm3 = [ret[0] + RT0 * RET_HEADS, ret[1] + RT1 * RET_HEADS]
            norm4 = [norm3[0], norm3[1] + 1]

        def mix_free(pe, g, n):
            pe.wait_ge(mixed[g], n)

        def load_ada(sp, m, slot, before):
            sp.wait_ge(ada_read, before + ADA_SLOTS)
            sp.dma_start(ada_raw[:, slot, :], d["ada"][m]).then_inc(ada_loaded[slot], 16)

        def load_ada_step(sp, name, i):
            per = dict((n, p) for n, _, p in ADA_PLAN)[name]
            m = ADA.first[name] + i * per
            for s in range(per):
                load_ada(sp, m + s, s, m)

        def ada_bias(dve, first, count, sums):
            out = mod[:].rearrange("p a k e -> p (a k) e")[:, bass.ds(first, count), :]
            bias = small["ada_b"][:, bass.ds(first, count)].unsqueeze(2).to_broadcast([P, count, 2])
            return dve.tensor_tensor(out, sums, bias, ALU.add)

        def ada_pe_tiles(pe, tiles):
            for m in tiles:
                pe.wait_ge(ada_pe_loaded[m], 16)
                for k in range(KT):
                    last = pe.matmul(mix_r[0][:, 2 * m:2 * m + 2], ada_pe[:, m, k * P:(k + 1) * P], c_col[:, k, :],
                                     start=(k == 0), stop=(k == KT - 1))
                if m == HEAD_PE - 1:
                    last.then_inc(ada_pe_done, 1)

        def ada_tiles(dve, m, slots, n_load, shift=HEAD_PE):
            dve.wait_ge(ada_moved, m + 1)
            for n, s in enumerate(slots):
                dve.wait_ge(ada_loaded[s], 16 * n_load[n])
                if n:
                    dve.wait_ge(ada_read, ADA_SLOTS + m + n)
                for e in range(2):
                    last = dve.tensor_tensor_reduce(out=ada_prod[:, e, :], in0=ada_raw[:, s, :], in1=c_row[:, e, :],
                                                    scale=1.0, scalar=0.0, op0=ALU.mult, op1=ALU.add,
                                                    accum_out=ada_sum[:, n, e:e + 1])
                last.then_inc(ada_read, 1)
            count = len(slots)
            dve.wait_ge(ada_read, ADA_SLOTS + m + count)
            ada_bias(dve, m + shift, count, ada_sum[:, 0:count, :]).then_inc(ada_moved, count)

        SQ_CREDIT = 2
        sq_added = sem("sq_added")
        LAST = {1: "down12", 2: "wo", 3: "down22"}

        def residual_final(eng, n):
            if n == 0:
                for s in in_x:
                    eng.wait_ge(s, 16)
            else:
                for p in (2, 3):
                    acc_read(eng, LAST[n], p, KT // 4 - 1)

        def norm_stats_act(act, n):
            act.preload_act_table_set("natural_log_exp_and_others")
            for i in range(KT // 4):
                for p in range(4):
                    k = i * 4 + p
                    if n:
                        acc_read(act, LAST[n], p, i)
                    else:
                        act.wait_ge(in_x[i], 16)
                    act.wait_ge(sq_added, KT * n + k + SQ_CREDIT)
                    act.activation(square[:, k % 2, :], x[:, k, :], ACT.Square).then_inc(sq_done, 1)
            act.wait_ge(sq_summed, n + 1)
            act.activation(halves(log_ms[:]), mix_v[1], ACT.Ln, bias=eps[:, 0:1],
                           scale=1.0 / D_MODEL).then_inc(log_done, 1)
            act.wait_ge(log_done, n + 1)
            act.activation(rstd[:], log_ms[:], ACT.Exp, scale=-0.5).then_inc(rstd_done, 1)

        def norm_rows_act(act, n):
            for k in range(KT):
                act.wait_ge(xn_done, KT * n + k + 1)
                if k >= 2:
                    act.wait_ge(hlo_done, KT * n + k - 1)
                act.activation(h_full[:, k % 2, 0:CTX], x_norm[:, k % 2, 0:CTX], ACT.Identity,
                               bias=mod[:, 3 * n, k, 0:1], scale=mod[:, 3 * n + 1, k, 0:1])
                act.activation(h_full[:, k % 2, CTX:T], x_norm[:, k % 2, CTX:T], ACT.Identity,
                               bias=mod[:, 3 * n, k, 1:2], scale=mod[:, 3 * n + 1, k, 1:2]).then_inc(mod_done, 1)
                act.wait_ge(mod_done, KT * n + k + 1)
                act.activation(h_hi[:, k, :], h_full[:, k % 2, :], ACT.Copy).then_inc(hhi_done, 1)

        def square_clear(pool, n):
            if n:
                pool.wait_ge(sq_summed, n)
            pool.memset(sq_sum[:], 0.0).then_inc(sq_added, 1)

        def square_add(pool, n, k):
            p = k % 2
            pool.wait_ge(sq_done, KT * n + k + 1)
            pool.wait_ge(sq_added, KT * n + k + 1 + SQ_CREDIT)
            pool.tensor_tensor(sq_sum[:, p, :], sq_sum[:, p, :], square[:, p, :], ALU.add).then_inc(sq_added, 1)

        def norm_pe(pe, n, use):
            mix_free(pe, 1, use)
            for step, (tile, counter, value) in enumerate(((sq_sum[:, 1, :], sq_added, KT * n + KT - 1 + SQ_CREDIT),
                                                           (sq_sum[:, 0, :], sq_added, KT * n + KT + SQ_CREDIT),
                                                           (square[:, (KT - 1) % 2, :], sq_done, KT * (n + 1)))):
                pe.wait_ge(counter, value)
                for b in range(2):
                    last = pe.matmul(mix[1][:, b, 0:HT], ones[:], tile[:, b * HT:(b + 1) * HT],
                                     start=(step == 0), stop=(step == 2))
            last.then_inc(sq_summed, 1)

        def norm_dve(dve, n, use):
            residual_final(dve, n)
            dve.wait_ge(rstd_done, 3 * n + 1)
            dve.scalar_tensor_tensor(out=halves(log_ms[:]), in0=mix_v[1], scalar=D_MODEL * EPS, in1=halves(rstd[:]),
                                     op0=ALU.add, op1=ALU.mult).then_inc(mixed[1], 1)
            dve.wait_ge(mixed[1], use + 1)
            dve.scalar_tensor_tensor(out=log_ms[:], in0=log_ms[:], scalar=-0.5 / D_MODEL, in1=rstd[:],
                                     op0=ALU.mult, op1=ALU.mult).then_inc(rstd_done, 1)
            dve.wait_ge(rstd_done, 3 * n + 2)
            dve.scalar_tensor_tensor(out=rstd[:], in0=log_ms[:], scalar=1.5, in1=rstd[:],
                                     op0=ALU.add, op1=ALU.mult).then_inc(rstd_done, 1)
            dve.wait_ge(rstd_done, 3 * n + 3)
            for k in range(KT):
                if n == 3:
                    dve.scalar_tensor_tensor(out=x[:, k, :], in0=x[:, k, :], scalar=small["final_w"][:, k:k + 1],
                                             in1=rstd[:], op0=ALU.mult, op1=ALU.mult).then_inc(xn_done, 1)
                    continue
                if k >= 2:
                    dve.wait_ge(mod_done, KT * n + k - 1)
                dve.tensor_tensor(x_norm[:, k % 2, :], x[:, k, :], rstd[:], ALU.mult).then_inc(xn_done, 1)
                if k:
                    lo_part(dve, n, k - 1)
            if n < 3:
                lo_part(dve, n, KT - 1)

        def lo_part(dve, n, k):
            dve.wait_ge(hhi_done, KT * n + k + 1)
            dve.tensor_tensor(h_lo[:, k, :], h_full[:, k % 2, :], h_hi[:, k, :].bitcast(F32),
                              ALU.subtract).then_inc(hlo_done, 1)

        def residual(dve, name, i, part):
            for p in range(4):
                g = ST.phase[name][2][p]
                projected(dve, name, p, i)
                tile = i * 4 + p
                for lo, hi, e in ((0, CTX, 0), (CTX, HT, 1), (HT, T, 1)):
                    src = acc[g][:, lo // HT, lo % HT:lo % HT + hi - lo]
                    last = dve.scalar_tensor_tensor(out=x[:, tile, lo:hi], in0=src, scalar=mod[:, part, tile, e:e + 1],
                                                    in1=x[:, tile, lo:hi], op0=ALU.mult, op1=ALU.add)
                last.then_inc(evacuated[g], 1)

        def up_act(act, f, c):
            name = f"up{f}{c}"
            act.preload_act_table_set("silu_and_others")
            with act.Fori(0, FF_CHUNKS[c] // 2) as i:
                for half in range(2):
                    j, pa, pb = i * 2 + half, 2 * half, 2 * half + 1
                    projected(act, name, pa, i)
                    act.wait_ge(evacuated[1], ST.uses(name, pb, i))
                    act.activation(halves(gate_a[:]), acc_v[0], ACT.Silu).then_inc(evacuated[0], 1)
                    acc_read(act, name, pb, i)
                    act.activation(u_hi[:, j, :], u_full[:], ACT.Copy).then_inc(uhi_done, 1)

        def up_dve(dve, f, c, base):
            name = f"up{f}{c}"
            with dve.Fori(0, FF_CHUNKS[c] // 2) as i:
                for half in range(2):
                    j, pa, pb = i * 2 + half, 2 * half, 2 * half + 1
                    if f == 1:
                        ada_step(dve, name, i, (pa, pb))
                    acc_read(dve, name, pa, i)
                    projected(dve, name, pb, i)
                    dve.wait_ge(ulo_done, base + j + 1)
                    dve.tensor_tensor(halves(u_full[:]), halves(gate_a[:]), acc_v[1], ALU.mult).then_inc(evacuated[1], 1)
                    dve.wait_ge(uhi_done, base + j + 1)
                    dve.tensor_tensor(u_lo[:, j, :], u_full[:], u_hi[:, j, :].bitcast(F32),
                                      ALU.subtract).then_inc(ulo_done, 1)

        def ff_pe(pe, f, c, base):
            name = f"up{f}{c}"
            if c == 0:
                project_pair(pe, name, h_hi, h_lo, (hlo_done, 2 * KT * (f - 1)))
                project(pe, name, 2, 0, h_hi, h_lo)
                project(pe, name, 3, 0, h_hi, h_lo)
            with pe.Fori(0 if c else 1, FF_CHUNKS[c] // 2) as i:
                for p in range(4):
                    project(pe, name, p, i, h_hi, h_lo)
            name = f"down{f}{c}"
            for i in range(KT // 4):
                for p in range(4):
                    project(pe, name, p, i, u_hi, u_lo, FF_CHUNKS[c],
                            tiles_done=(ulo_done, base + 1) if i == p == 0 else None)

        def u_base(f, c):
            return (f - 1) * (D_FF // P) + sum(FF_CHUNKS[:c])

        def ada_step(dve, name, i, slots):
            per = dict((n, p) for n, _, p in ADA_PLAN)[name]
            ada_tiles(dve, ADA.first[name] + i * per + slots[0], slots, [ADA.loads[name][s] + i + 1 for s in slots])

        def make_scale(dve, n):
            dve.wait_ge(ada_moved, 1 + (ADA.first["up10"] if n == 0 else ADA.total))
            dve.wait_ge(mixed[0], Uses.norm2[0])
            sc = mod[:, 3 * n + 1, :, :]
            nw = small["norm_w"][:, KT * n:KT * (n + 1)].unsqueeze(2).to_broadcast([P, KT, 2])
            dve.tensor_scalar(sc, sc, 1.0, None, ALU.add).then_inc(coef_done, 1)
            dve.wait_ge(coef_done, 3 * n + 1)
            dve.tensor_tensor(sc, sc, nw, ALU.mult).then_inc(coef_done, 1)

        def make_gate(dve, n):
            dve.wait_ge(ada_moved, 1 + (ADA.first["down10"] if n == 0 else ADA.total))
            g = mod[:, 3 * n + 2, :, :]
            dve.tensor_scalar(g, g, 1.0 if n == 1 else 0.5, None, ALU.mult).then_inc(coef_done, 1)

        def small_chain(dve):
            done = [0]

            def step(instruction):
                done[0] += 1
                instruction.then_inc(small_done, 1)
                dve.wait_ge(small_done, done[0])

            logits = small["lb"][:].rearrange("p (w l k) -> p w l k", w=2, l=2)
            top, e0, e1, total = (soft[:, n, :].rearrange("p (w k) -> p w k", w=2) for n in range(4))
            step(dve.tensor_tensor(top, logits[:, :, 0, :], logits[:, :, 1, :], ALU.max))
            step(dve.tensor_tensor(e0, logits[:, :, 0, :], top, ALU.subtract))
            step(dve.tensor_tensor(e1, logits[:, :, 1, :], top, ALU.subtract))
            y, u, log_u, diff, is_zero = (gam_tmp[:, n, :] for n in range(5))
            z = small["decay"][:]
            step(dve.scalar_tensor_tensor(out=y, in0=z, scalar=-1.0, in1=z, op0=ALU.mult, op1=ALU.max))
            dve.wait_ge(small_act, 1)
            step(dve.tensor_scalar(u, y, 1.0, None, ALU.add))
            step(dve.tensor_scalar(diff, u, -1.0, None, ALU.add))
            step(dve.tensor_scalar(is_zero, diff, 0.0, None, ALU.is_equal))
            step(dve.tensor_tensor(diff, diff, is_zero, ALU.add))
            step(dve.reciprocal(diff, diff))
            dve.wait_ge(small_act, 2)
            step(dve.tensor_tensor(log_u, log_u, y, ALU.mult))
            step(dve.tensor_tensor(log_u, log_u, diff, ALU.mult))
            step(dve.tensor_tensor(is_zero, is_zero, y, ALU.mult))
            step(dve.tensor_tensor(log_u, log_u, is_zero, ALU.add))
            step(dve.scalar_tensor_tensor(out=log_gam[:], in0=z, scalar=0.0, in1=log_u, op0=ALU.min, op1=ALU.subtract))
            step(dve.tensor_tensor(total, e0, e1, ALU.add))
            step(dve.reciprocal(total, total))
            step(dve.tensor_tensor(lb[:].rearrange("p (w k) -> p w k", w=2), e0, total, ALU.mult))
            step(dve.tensor_scalar(lb_rest[:], lb[:], -1.0, 1.0, ALU.mult, ALU.add))

        def small_chain_act(act):
            act.wait_ge(small_done, 4)
            act.activation(soft[:, 1, :], soft[:, 1, :], ACT.Exp)
            act.activation(soft[:, 2, :], soft[:, 2, :], ACT.Exp)
            act.activation(gam_tmp[:, 0, :], gam_tmp[:, 0, :], ACT.Exp, scale=-1.0).then_inc(small_act, 1)
            act.wait_ge(small_done, 5)
            act.activation(gam_tmp[:, 2, :], gam_tmp[:, 1, :], ACT.Ln).then_inc(small_act, 1)
            act.wait_ge(small_done, 14)
            for w in range(2):
                cols = slice(RET_HEADS * w, RET_HEADS * (w + 1))
                act.activation(k_decay[:, cols], log_gam[:, cols], ACT.Exp, scale=small["kpos"][:, w:w + 1])
            act.activation(c_decay[:], log_gam[:], ACT.Exp, scale=float(P))

        F_, B_, Q_, O_, V_ = range(5)
        hg_sig, hg_gate, hg_key, hg_query, hg_og = (sem("hg_" + n) for n in ("sig", "gate", "key", "query", "og"))
        hg_ln, hg_scan, hg_arg, hg_exp, hg_qk = (sem("hg_" + n) for n in ("ln", "scan", "arg", "exp", "qk"))
        hg_lev, hg_ktok, hg_kv, hg_state = (sem("hg_" + n) for n in ("lev", "ktok", "kv", "state"))
        hg_o, hg_osq, hg_ss, hg_rstd, hg_out = (sem("hg_" + n) for n in ("o", "osq", "ss", "rstd", "out"))
        hg_vt, hg_sin_ld, hg_dec, hg_fin = (sem("hg_" + n) for n in ("vt", "sin", "dec", "fin"))
        hg_kk = sem("hg_kk")
        N_ARG = LEVELS + 2
        N_QK = LEVELS + 3

        def tiles5(ap):
            return ap.rearrange("p (c t) -> p c t", c=NT)

        def blocks(ap, u):
            return ap.rearrange("p (a i) -> p a i", i=2 << u)

        def hg_evac(act, h, p):
            projected(act, "hg", p, h)
            again = not (isinstance(h, int) and h == 0)
            if again and p == V_:
                act.wait_ge(hg_vt, h)
            if again and p in (F_, B_):
                act.wait_ge(hg_sig, 6 * h)
            if again and p == Q_:
                act.wait_ge(hg_query, h)
            if again and p == O_:
                act.wait_ge(hg_og, h)
            g = ST.phase["hg"][2][p]
            act.activation(halves(pre[:, p, :]), acc_v[g], ACT.Copy).then_inc(evacuated[g], 1)

        def hg_start_act(act, h):
            act.preload_act_table_set("sigmoid_and_others")
            again = not (isinstance(h, int) and h == 0)
            for n, (src, dst, sc) in enumerate(((F_, g_f, 1.0), (B_, g_b, 1.0), (F_, k_f, -1.0), (B_, k_b, -1.0),
                                                (Q_, q, 1.0), (O_, out_sig, 1.0))):
                if again and n == 0:
                    act.wait_ge(hg_scan, 2 * h)
                if again and n == 2:
                    act.wait_ge(hg_kk, N_ARG * h)
                if again and n == 4:
                    act.wait_ge(hg_qk, N_QK * h)
                if again and n == 5:
                    act.wait_ge(hg_og, h)
                acc_read(act, "hg", src, h)
                act.activation(dst[:], pre[:, src, :], ACT.Sigmoid, scale=sc).then_inc(hg_sig, 1)
            act.preload_act_table_set("natural_log_exp_and_others")
            for n, g in enumerate((g_f, g_b)):
                act.wait_ge(hg_gate, 2 * h + n + 1)
                act.activation(g[:], g[:], ACT.Ln, bias=lb[:, bass.ds(KT * n + h, 1)]).then_inc(hg_ln, 1)

        def hg_act(act, m, h, next_evac):
            act.wait_ge(hg_out, m + 1)
            act.dma_start(s_in[:], d["s_hg"][m]).then_inc(hg_sin_ld, 16)
            act.wait_ge(hg_vt, m + 1)
            act.activation(v_tok[:].rearrange("p c t -> p (c t)"), mix_r[0][:, 0:T], ACT.Copy).then_inc(mixed[0], 1)
            for u in range(LEVELS):
                act.wait_ge(hg_arg, N_ARG * m + u + 1)
                act.activation(e_f[:, u % 2, :], e_f[:, u % 2, :], ACT.Exp)
                act.activation(e_b[:, u % 2, :], e_b[:, u % 2, :], ACT.Exp).then_inc(hg_exp, 1)
                if u in (1, 3, 5):
                    next_evac((1, 3, 5).index(u))
            u = LEVELS
            act.wait_ge(hg_arg, N_ARG * m + u + 1)
            act.activation(e_f[:, u % 2, :], e_f[:, u % 2, :], ACT.Exp)
            act.activation(e_b[:, u % 2, :], b_f[:], ACT.Exp).then_inc(hg_exp, 1)
            u = LEVELS + 1
            act.wait_ge(hg_arg, N_ARG * m + u + 1)
            act.activation(e_f[:, u % 2, :], e_f[:, u % 2, :], ACT.Exp)
            act.activation(tiles5(e_b[:, u % 2, :]), p_b[:, :, 0:P], ACT.Exp).then_inc(hg_exp, 1)
            act.activation(s_dec[:, 0, :], tiles5(b_f[:])[:, :, P - 1], ACT.Exp)
            act.activation(s_dec[:, 1, :], p_b[:, :, P], ACT.Exp).then_inc(hg_dec, 1)
            next_evac(3)
            for n in range(2):
                act.wait_ge(hg_ktok, 2 * m + n + 1)
                act.activation(k_tok[:, n].rearrange("p c t -> p (c t)"), mix_r[n][:, 0:4 * P],
                               ACT.Copy).then_inc(mixed[n], 1)
            if h is not None:
                hg_start_act(act, h)
            act.wait_ge(hg_fin, m + 1)
            act.dma_start(d["out_hg"][m], s_fin[:]).then_inc(states_out, 16)
            act.wait_ge(hg_o, m + 1)
            act.activation(o_sq[:], mix_r[0][:, 0:T], ACT.Square).then_inc(hg_osq, 1)
            next_evac(4)
            if h is None:
                act.preload_act_table_set("natural_log_exp_and_others")
            act.wait_ge(hg_ss, m + 1)
            act.activation(halves(o_sq[:]), mix_v[1], ACT.Ln, bias=eps[:, 0:1], scale=1.0 / HG_DV).then_inc(mixed[1], 1)
            act.wait_ge(mixed[1], Uses.hg[1] + HG1 * (m + 1))
            act.activation(o_rstd[:], o_sq[:], ACT.Exp, scale=-0.5).then_inc(hg_rstd, 1)

        def hg_arguments(dve, m, u):
            f, b, half = e_f[:, u % 2, :], e_b[:, u % 2, :], 1 << u
            if u >= 2:
                dve.wait_ge(hg_qk, N_QK * m + u)
                dve.wait_ge(hg_kk, N_ARG * m + u - 1)
            elif not (isinstance(m, int) and m == 0):
                dve.wait_ge(hg_qk, N_QK * m)
                dve.wait_ge(hg_kk, N_ARG * m)
            if u < LEVELS:
                fb, src = blocks(f, u), blocks(b_f[:], u)
                na = T // (2 * half)
                mid = src[:, :, half - 1:half].to_broadcast([P, na, half])
                dve.tensor_tensor(fb[:, :, 0:half], mid, src[:, :, 0:half], ALU.subtract)
                dve.tensor_tensor(fb[:, :, half:], src[:, :, half:], mid, ALU.subtract)
                nb = P // (2 * half)
                bb = b.rearrange("p (c a i) -> p c a i", c=NT, a=nb)
                src = p_b[:, :, 0:P].rearrange("p c (a i) -> p c a i", a=nb)
                mid = src[:, :, :, half:half + 1].to_broadcast([P, NT, nb, half])
                dve.tensor_tensor(bb[:, :, :, 0:half], mid, src[:, :, :, 0:half], ALU.subtract)
                dve.tensor_tensor(bb[:, :, :, half:], src[:, :, :, half:], mid, ALU.subtract).then_inc(hg_arg, 1)
            elif u == LEVELS:
                last = tiles5(b_f[:])[:, :, P - 1:P].to_broadcast([P, NT, P])
                dve.tensor_tensor(tiles5(f), last, tiles5(b_f[:]), ALU.subtract).then_inc(hg_arg, 1)
            else:
                last = p_b[:, :, P:P + 1].to_broadcast([P, NT, P])
                dve.tensor_tensor(tiles5(f), last, p_b[:, :, 0:P], ALU.subtract).then_inc(hg_arg, 1)

        def hg_operands(dve, m, u):
            s, half = u % 2, 1 << u
            dve.wait_ge(hg_exp, N_ARG * m + u + 1)
            if u >= 1:
                dve.wait_ge(hg_lev, (LEVELS + 1) * m + u)
            if u < LEVELS:
                first, second = slice(0, half), slice(half, 2 * half)
                fb, bb = blocks(e_f[:, s, :], u), blocks(e_b[:, s, :], u)
                qb, src = blocks(q_lev[:, s, :], u), blocks(q[:], u)
                dve.tensor_tensor(qb[:, :, second], src[:, :, second], fb[:, :, second], ALU.mult)
                dve.tensor_tensor(qb[:, :, first], src[:, :, first], bb[:, :, first], ALU.mult).then_inc(hg_qk, 1)
            else:
                e = e_b if u == LEVELS else e_f
                dve.tensor_tensor(q_lev[:, s, :], q[:], e[:, s, :], ALU.mult).then_inc(hg_qk, 1)

        def hg_keys(pool, m, u):
            s, half = u % 2, 1 << u
            if u == 0:
                pool.wait_ge(hg_key, 2 * m + 2)
            pool.wait_ge(hg_exp, N_ARG * m + u + 1)
            if u >= 1:
                pool.wait_ge(hg_lev, (LEVELS + 1) * m + u)
            if u < LEVELS:
                first, second = slice(0, half), slice(half, 2 * half)
                fb, bb, out = blocks(e_f[:, s, :], u), blocks(e_b[:, s, :], u), blocks(k_lev[:, s, :], u)
                pool.tensor_tensor(out[:, :, first], blocks(k_f[:], u)[:, :, first], fb[:, :, first], ALU.mult)
                pool.tensor_tensor(out[:, :, second], blocks(k_b[:], u)[:, :, second], bb[:, :, second],
                                   ALU.mult).then_inc(hg_kk, 1)
            else:
                k, e = (k_f, e_f) if u == LEVELS else (k_b, e_b)
                pool.tensor_tensor(k_lev[:, s, :], k[:], e[:, s, :], ALU.mult).then_inc(hg_kk, 1)

        def split_hg(pool):
            for p in range(5):
                split_slab(pool, "hg", p, 0)
            split_slab(pool, "hg", 0, 1)
            with pool.Fori(1, HG_HEADS - 1) as h:
                split_and_keys(pool, "hg", h, "hg", 0, h + 1)
            split_and_keys(pool, "hg", HG_HEADS - 1, "ret", 0, 0)
            split_and_keys(pool, "ret", HG_HEADS, "ret", 5, 0)

        def split_and_keys(pool, name, h, next_name, next_p, next_i):
            i = h if name == "hg" else 0
            for p, units in ((1, (0,)), (2, (1, 2)), (3, (3, 4)), (4, (5, 6, 7, 8))):
                split_slab(pool, name, p, i)
                for u in units:
                    hg_keys(pool, h - 1, u)
            split_slab(pool, next_name, next_p, next_i)

        def hg_score_read(dve, m, u):
            dve.wait_ge(hg_lev, (LEVELS + 1) * m + u + 1)
            flat = att[:].rearrange("p c t -> p (c t)")
            if u == 0:
                dve.tensor_copy(flat, mix_r[0][:, 0:T]).then_inc(mixed[0], 1)
            else:
                g, before = (u - 1) % 2, (u - 1) // 2
                dve.wait_ge(mixed[g], (Uses.hg[0] + HG0 * m + 2 if g == 0 else Uses.hg[1] + HG1 * m + 1) + before)
                mask = masks[:, u - 1, :].unsqueeze(1).to_broadcast([P, NT, P])
                dve.sem_inc(dve_waited, 1)
                dve.copy_predicated(att[:], mask, tiles5(mix_r[u % 2][:, 0:T])).then_inc(mixed[u % 2], 1)

        def hg_start_dve(dve, h):
            again = not (isinstance(h, int) and h == 0)
            for n, g in enumerate((g_f, g_b)):
                dve.wait_ge(hg_sig, 6 * h + n + 1)
                dve.tensor_scalar(g[:], g[:], TINY, lb_rest[:, bass.ds(KT * n + h, 1)], ALU.max, ALU.mult).then_inc(hg_gate, 1)
            for n, k in enumerate((k_f, k_b)):
                dve.wait_ge(hg_sig, 6 * h + n + 3)
                dve.tensor_scalar(k[:], k[:], lb_rest[:, bass.ds(KT * n + h, 1)], None, ALU.mult).then_inc(hg_key, 1)
            dve.wait_ge(hg_sig, 6 * h + 5)
            dve.scalar_tensor_tensor(out=q[:], in0=pre[:, Q_, :], scalar=float(HG_DK) ** -0.5, in1=q[:],
                                     op0=ALU.mult, op1=ALU.mult).then_inc(hg_query, 1)
            dve.wait_ge(hg_key, 2 * h + 2)
            if again:
                dve.wait_ge(hg_ktok, 2 * h)
            dve.tensor_tensor(k_lev[:, 1, :], k_f[:], k_b[:], ALU.add).then_inc(hg_qk, 1)

        def hg_sums_dve(dve, h):
            dve.wait_ge(hg_sig, 6 * h + 6)
            dve.tensor_tensor(out_gate[:], pre[:, O_, :], out_sig[:], ALU.mult).then_inc(hg_og, 1)
            for n, g in enumerate((g_f, g_b)):
                dve.wait_ge(hg_ln, 2 * h + n + 1)
                for c in range(NT):
                    out = b_f[:, c * P:(c + 1) * P] if n == 0 else p_b[:, c, 1:P + 1]
                    last = dve.tensor_tensor_scan(out, ones[:], g[:, c * P:(c + 1) * P], 0.0, ALU.mult, ALU.add)
                last.then_inc(hg_scan, 1)
            dve.wait_ge(hg_scan, 2 * h + 2)
            dve.wait_ge(hg_query, h + 1)
            hg_arguments(dve, h, 0)

        def hg_dve(dve, m, h):
            for u in range(LEVELS):
                hg_arguments(dve, m, u + 1)
                hg_operands(dve, m, u)
                hg_score_read(dve, m, u)
            hg_arguments(dve, m, LEVELS + 1)
            hg_score_read(dve, m, LEVELS)
            hg_operands(dve, m, LEVELS)
            hg_operands(dve, m, LEVELS + 1)
            dve.wait_ge(hg_dec, m + 1)
            dve.wait_ge(hg_sin_ld, 16 * (m + 1))
            dve.wait_ge(hg_kv, 2 * m + 2)
            dve.wait_ge(states_out, 16 * (m + 1))
            dve.tensor_copy(s_fin[:, 0, :], mix[0][:, 1, 0:P])
            dve.tensor_copy(s_fin[:, 1, :], mix[1][:, 1, 0:P]).then_inc(hg_fin, 1)
            for n in range(3):
                for w in range(2):
                    tile = 1 + n if w == 0 else 4 - n
                    kv = mix[w][:, 1, (1 + n) * P:(2 + n) * P] if w == 0 else mix[w][:, 1, (3 - n) * P:(4 - n) * P]
                    old = s_in[:, w, :] if n == 0 else s_run[:, w, n - 1, :]
                    if n:
                        dve.wait_ge(hg_state, 6 * m + 2 * (n - 1) + w + 1)
                    last = dve.scalar_tensor_tensor(out=s_run[:, w, n, :], in0=old, scalar=s_dec[:, w, tile:tile + 1],
                                                    in1=kv, op0=ALU.mult, op1=ALU.add)
                    last.then_inc(hg_state, 1)
            if h is not None:
                hg_start_dve(dve, h)
            dve.wait_ge(hg_o, m + 1)
            dve.wait_ge(hg_osq, m + 1)
            dve.wait_ge(hg_og, m + 1)
            dve.wait_ge(hg_out, m + 1)
            dve.scalar_tensor_tensor(out=o_gated[:], in0=mix_r[0][:, 0:T], scalar=small["hg_w"][:, bass.ds(m, 1)],
                                     in1=out_gate[:], op0=ALU.mult, op1=ALU.mult).then_inc(mixed[0], 1)
            dve.wait_ge(mixed[0], Uses.hg[0] + HG0 * (m + 1))
            if h is not None:
                hg_sums_dve(dve, h)
            dve.wait_ge(hg_rstd, m + 1)
            dve.tensor_tensor(o_hg[:, m, :], o_gated[:], o_rstd[:], ALU.mult).then_inc(hg_out, 1)

        def hg_vt_pe(pe, m):
            acc_read(pe, "hg", V_, m)
            mix_free(pe, 0, Uses.hg[0] + HG0 * m)
            for c in range(NT):
                last = pe.transpose(mix_r[0][:, c * P:(c + 1) * P], pre[:, V_, c * P:(c + 1) * P], ident[:])
            last.then_inc(hg_vt, 1)

        def hg_unit_pe(pe, m, u):
            pe.wait_ge(hg_qk, N_QK * m + u + 1)
            if u:
                pe.wait_ge(hg_kk, N_ARG * m + u)
            if u == 0:
                pe.wait_ge(hg_query, m + 1)
            g = u % 2
            mix_free(pe, g, (Uses.hg[0] + HG0 * m + 1 + u // 2) if g == 0 else (Uses.hg[1] + HG1 * m + u // 2))
            ks, qs = (k_lev[:, 1, :], q[:]) if u == 0 else (k_lev[:, (u - 1) % 2, :], q_lev[:, (u - 1) % 2, :])
            for c in range(NT):
                cols = slice(c * P, (c + 1) * P)
                last = pe.matmul(mix_r[g][:, cols], ks[:, cols], qs[:, cols], start=True, stop=True)
            last.then_inc(hg_lev, 1)

        HG_TILES = ((0, 1, 2, 3), (0, 2, 3, 4))

        def hg_kt_pe(pe, m):
            for w in range(2):
                pe.wait_ge(hg_qk, N_QK * m + N_QK - 1 + w)
                pe.wait_ge(hg_kk, N_ARG * m + LEVELS + w + 1)
                mix_free(pe, w, (Uses.hg[0] + HG0 * m + 5, Uses.hg[1] + HG1 * m + 4)[w])
                for j, c in enumerate(HG_TILES[w]):
                    last = pe.transpose(mix_r[w][:, j * P:(j + 1) * P], k_lev[:, (LEVELS + w) % 2, c * P:(c + 1) * P], ident[:])
                last.then_inc(hg_ktok, 1)

        def hg_kv_pe(pe, m):
            for w in range(2):
                mix_free(pe, w, (Uses.hg[0] + HG0 * m + 6, Uses.hg[1] + HG1 * m + 5)[w])
                for j, c in enumerate(HG_TILES[w]):
                    last = pe.matmul(mix[w][:, 1, j * P:(j + 1) * P], k_tok[:, w, j, :], v_tok[:, c, :], start=True, stop=True)
                last.then_inc(hg_kv, 1)

        def hg_out_pe(pe, m):
            pe.wait_ge(hg_state, 6 * m + 6)
            pe.wait_ge(mixed[1], Uses.hg[1] + HG1 * m + 4)
            for c in range(NT):
                cols = slice(c * P, (c + 1) * P)
                last = pe.matmul(mix_r[0][:, cols], v_tok[:, c, :], att[:, c, :], start=True, stop=(c == 0))
                if c:
                    for w in range(2):
                        n = c - 1 if w == 0 else 4 - c
                        st = s_in[:, w, :] if n == 0 else s_run[:, w, n - 1, :]
                        last = pe.matmul(mix_r[0][:, cols], st, q_lev[:, (LEVELS + w) % 2, cols], start=False, stop=(w == 1))
            last.then_inc(hg_o, 1)

        def hg_ss_pe(pe, m):
            pe.wait_ge(hg_osq, m + 1)
            for b in range(2):
                last = pe.matmul(mix[1][:, b, 0:HT], ones[:], o_sq[:, b * HT:(b + 1) * HT], start=True, stop=True)
            last.then_inc(hg_ss, 1)

        def hg_body_pe(pe, m, name, i):
            def next_head(p, ks=None):
                project(pe, name, p, i, h_hi, h_lo, ks=ks)

            next_head(0)
            hg_vt_pe(pe, m)
            next_head(1, range(0, 2))
            hg_unit_pe(pe, m, 0)
            next_head(1, range(2, 5))
            hg_unit_pe(pe, m, 1)
            next_head(1, range(5, 8))
            next_head(2, range(0, 1))
            hg_unit_pe(pe, m, 2)
            next_head(2, range(1, 3))
            hg_unit_pe(pe, m, 3)
            next_head(2, range(3, 6))
            hg_unit_pe(pe, m, 4)
            next_head(2, range(6, 8))
            next_head(3, range(0, 1))
            hg_unit_pe(pe, m, 5)
            next_head(3, range(1, 4))
            hg_unit_pe(pe, m, 6)
            next_head(3, range(4, 6))
            hg_unit_pe(pe, m, 7)
            next_head(3, range(6, 8))
            next_head(4, range(0, 1))
            hg_kt_pe(pe, m)
            next_head(4, range(1, 3))
            hg_kv_pe(pe, m)
            next_head(4, range(3, 6))
            hg_out_pe(pe, m)
            next_head(4, range(6, 8))
            hg_ss_pe(pe, m)

        part_hi, part_lo = sem("part_hi"), sem("part_lo")
        merge_done = sem("merge_done")
        ret_hi_tiles = [ret_hi[:, k, :] for k in range(KT)]
        K_, Q2_, V0_, V1_, G0_, G1_ = range(6)
        rt_rot, rt_tmp, rt_kq, rt_sc = (sem("ret_" + n) for n in ("rot", "tmp", "kq", "scores"))
        rt_kt, rt_kv, rt_qdec, rt_state = (sem("ret_" + n) for n in ("kt", "kv", "qdec", "state"))
        rt_o, rt_osq, rt_ss, rt_rstd, rt_out = (sem("ret_" + n) for n in ("o", "osq", "ss", "rstd", "out"))
        rt_vt, rt_sin_ld, rt_fin, rt_dmat, rt_exp = (sem("ret_" + n) for n in ("vt", "sin", "fin", "dmat", "exp"))
        tab_in, masks_in = sem("tab_in"), sem("masks_in")

        def ret_tables_load(act):
            act.wait_ge(hg_out, HG_HEADS + 1)
            act.wait_ge(states_out, 16 * (HG_HEADS + 1))
            for n, (dst, src) in enumerate(((cos[:], d["cos"]), (sin[:], d["sin"]), (dist, d["dist"]), (upper, d["upper"]),
                                            (lower, d["lower"]), (rows, d["rows"].rearrange("p (d t) -> p d t", d=2)))):
                act.dma_start(dst, src).then_inc(tab_in, 16)

        def ret_tables_act(act):
            act.wait_ge(tab_in, 16 * 6)
            for n in range(RET_HEADS):
                for w in range(2):
                    col = RET_HEADS * w + n
                    act.activation(q_rows[:, col, :], rows[:, w, :], ACT.Exp, scale=log_gam[:, col:col + 1])
                if n:
                    act.wait_ge(rt_dmat, n)
                act.activation(e_mat[:, 0, :], dist, ACT.Exp, scale=log_gam[:, n:n + 1])
                act.activation(e_mat[:, 1, :], dist, ACT.Exp, scale=log_gam[:, RET_HEADS + n:RET_HEADS + n + 1]).then_inc(rt_exp, 1)

        def ret_tables_dve(dve):
            for n in range(RET_HEADS):
                dve.wait_ge(rt_exp, n + 1)
                dve.tensor_tensor(r_tmp[:, 1, 2 * P:3 * P], e_mat[:, 0, :], upper, ALU.mult)
                dve.tensor_tensor(r_tmp[:, 1, 3 * P:4 * P], e_mat[:, 1, :], lower, ALU.mult).then_inc(rt_tmp, 1)
                dve.wait_ge(rt_tmp, n + 1)
                dve.tensor_tensor(d_mat[:, n, :], r_tmp[:, 1, 2 * P:3 * P], r_tmp[:, 1, 3 * P:4 * P], ALU.add).then_inc(rt_dmat, 1)

        def ret_evac(act, h, p):
            projected(act, "ret", p, h)
            first = isinstance(h, int) and h == 0
            if first and p < 5:
                s, n = ((hg_sig, 6 * HG_HEADS), (hg_sig, 6 * HG_HEADS), (hg_query, HG_HEADS), (hg_og, HG_HEADS),
                        (hg_vt, HG_HEADS))[p]
                act.wait_ge(s, n)
            if first and p in (K_, Q2_, V0_, V1_):
                pass
            elif p in (K_, Q2_):
                act.wait_ge(rt_kq, 2 * h)
            elif p in (V0_, V1_):
                act.wait_ge(rt_vt, 2 * h)
            else:
                act.wait_ge(rt_out, 2 * h + 1)
            g = ST.phase["ret"][2][p]
            func, scale = (ACT.Silu if p >= G0_ else ACT.Copy), (float(RET_DK) ** -0.5 if p == K_ else 1.0)
            act.activation(halves(r_pre[:, p, :]), acc_v[g], func, scale=scale).then_inc(evacuated[g], 1)

        def ret_v_act(act, m):
            act.wait_ge(rt_out, 2 * m + 1)
            for e in range(2):
                act.wait_ge(rt_vt, 2 * m + e + 1)
                act.activation(r_v[:, :, e, :], tiles5(mix_r[e][:, 0:T]), ACT.Copy).then_inc(mixed[e], 1)
            act.dma_start(r_sin[:], d["s_ret"][m]).then_inc(rt_sin_ld, 16)

        def gate_evac(act, p, n):
            projected(act, "gate", p, n)
            act.wait_ge(merge_done, n + 1)
            act.activation(halves(sig_buf[:, p, :]), acc_v[p], ACT.Sigmoid).then_inc(evacuated[p], 1)

        def ret_act(act, m, h):
            if h is not None:
                for p in range(3):
                    ret_evac(act, h, p)
            else:
                act.wait_ge(rt_kq, 2 * RET_HEADS)
                gate_evac(act, 0, 0)
                for k in range(HG_EARLY):
                    if k == 4:
                        act.wait_ge(rt_qdec, 2 * RET_HEADS)
                        act.wait_ge(mixed[0], Uses.ret[0] + RT0 * m + 3)
                    act.activation(hg_hi[k], o_hg[:, k, :], ACT.Copy).then_inc(part_hi, 1)
            act.wait_ge(rt_fin, m + 1)
            act.dma_start(d["out_ret"][m], r_sfin[:]).then_inc(states_out, 16)
            if h is None:
                gate_evac(act, 1, 0)
            act.preload_act_table_set("natural_log_exp_and_others")
            for e in range(2):
                act.wait_ge(rt_o, 2 * m + e + 1)
                act.activation(r_tmp[:, e, :], mix_r[e][:, 0:T], ACT.Square).then_inc(rt_osq, 1)
            if h is not None:
                ret_evac(act, h, V1_)
            act.wait_ge(rt_ss, m + 1)
            act.activation(halves(r_tmp[:, 0, :]), mix_v[0], ACT.Ln, bias=eps[:, 0:1], scale=1.0 / RET_DV).then_inc(mixed[0], 1)
            act.wait_ge(mixed[0], Uses.ret[0] + RT0 * (m + 1))
            act.activation(r_tmp[:, 1, :], r_tmp[:, 0, :], ACT.Exp, scale=-0.5).then_inc(rt_rstd, 1)
            if h is not None:
                for p in range(4, 6):
                    ret_evac(act, h, p)
                ret_v_act(act, h)

        def part_lo_dve(dve, name, k):
            src, hi, lo, before = (o_hg, hg_hi, hg_lo, 0) if name == "hg" else (o_ret, ret_hi_tiles, ret_lo, KT)
            dve.wait_ge(part_hi, before + k + 1)
            dve.tensor_tensor(lo[:, k, :], src[:, k, :], hi[k].bitcast(F32), ALU.subtract).then_inc(part_lo, 1)

        def ret_dve(dve, m, last):
            dve.wait_ge(rt_out, 2 * m + 1)
            for w, (p, dst) in enumerate(((K_, 0), (Q2_, 1))):
                dve.wait_ge(rt_rot, 2 * m + w + 1)
                dve.tensor_tensor(halves(r_tmp[:, w, :]), mix_v[w], halves(sin[:]), ALU.mult).then_inc(mixed[w], 1)
                acc_read(dve, "ret", p, m)
                dve.tensor_tensor(r_rot[:, dst, :], r_pre[:, p, :], cos[:], ALU.mult).then_inc(rt_tmp, 1)
                dve.wait_ge(rt_tmp, RET_HEADS + 2 * m + w + 1)
                dve.wait_ge(mixed[w], (Uses.ret[w] + (RT0, RT1)[w] * m + 2))
                dve.tensor_tensor(r_rot[:, dst, :], r_rot[:, dst, :], r_tmp[:, w, :], ALU.add).then_inc(rt_kq, 1)
            dve.wait_ge(rt_kq, 2 * m + 2)
            for w in range(2):
                row = q_rows[:, bass.ds(RET_HEADS * w + m, 1), :].to_broadcast([P, 4, P])
                dve.tensor_tensor(r_qdec[:, w, :].rearrange("p (c t) -> p c t", c=4),
                                  r_rot[:, 1, CTX:T].rearrange("p (c t) -> p c t", c=4), row, ALU.mult).then_inc(rt_qdec, 1)
            dve.wait_ge(rt_sc, m + 1)
            dve.wait_ge(rt_dmat, RET_HEADS)
            dve.tensor_tensor(r_att[:], tiles5(mix_r[0][:, 0:T]), d_mat[:, bass.ds(m, 1), :].to_broadcast([P, NT, P]),
                              ALU.mult).then_inc(mixed[0], 1)
            dve.wait_ge(rt_kt, m + 1)
            kt5 = tiles5(mix_r[1][:, 0:T])
            dve.tensor_scalar(r_ktok[:, 0], kt5[:, 0:4, :], k_decay[:, bass.ds(m, 1)], None, ALU.mult)
            dve.tensor_scalar(r_ktok[:, 1, 0, :], kt5[:, 0, :], k_decay[:, bass.ds(RET_HEADS + m, 1)], None, ALU.mult)
            dve.tensor_scalar(r_ktok[:, 1, 1:4, :], kt5[:, 2:5, :], k_decay[:, bass.ds(RET_HEADS + m, 1)], None,
                              ALU.mult).then_inc(mixed[1], 1)
            if last:
                for k in range(HG_EARLY):
                    part_lo_dve(dve, "hg", k)
            dve.wait_ge(rt_kv, 2 * m + 2)
            dve.wait_ge(states_out, 16 * (HG_HEADS + m + 1))
            dve.wait_ge(rt_sin_ld, 16 * (m + 1))
            dve.tensor_copy(r_sfin[:, 0, :], mix_r[0][:, 0:RET_DV])
            dve.tensor_copy(r_sfin[:, 1, :], mix_r[1][:, 0:RET_DV]).then_inc(rt_fin, 1)
            for n in range(3):
                for w in range(2):
                    j = 1 + n if w == 0 else 3 - n
                    kv = mix_r[w][:, j * RET_DV:(j + 1) * RET_DV]
                    old = r_sin[:, w, :] if n == 0 else r_srun[:, w, n - 1, :]
                    if n:
                        dve.wait_ge(rt_state, 6 * m + 2 * (n - 1) + w + 1)
                    dve.scalar_tensor_tensor(out=r_srun[:, w, n, :], in0=old,
                                             scalar=c_decay[:, bass.ds(RET_HEADS * w + m, 1)],
                                             in1=kv, op0=ALU.mult, op1=ALU.add).then_inc(rt_state, 1)
            for e in range(2):
                dve.wait_ge(rt_osq, 2 * m + e + 1)
                acc_read(dve, "ret", G0_ + e, m)
                dve.tensor_tensor(r_pre[:, G0_ + e, :], mix_r[e][:, 0:T], r_pre[:, G0_ + e, :], ALU.mult).then_inc(mixed[e], 1)
            dve.wait_ge(mixed[1], Uses.ret[1] + RT1 * (m + 1))
            dve.wait_ge(mixed[0], Uses.ret[0] + RT0 * (m + 1))
            dve.wait_ge(rt_rstd, m + 1)
            for e in range(2):
                dve.tensor_tensor(o_ret[:, m * 2 + e, :], r_pre[:, G0_ + e, :], r_tmp[:, 1, :], ALU.mult).then_inc(rt_out, 1)

        def ret_vt_pe(pe, m):
            for e in range(2):
                acc_read(pe, "ret", V0_ + e, m)
                mix_free(pe, e, Uses.ret[e] + (RT0, RT1)[e] * m)
                for c in range(NT):
                    last = pe.transpose(mix_r[e][:, c * P:(c + 1) * P], r_pre[:, V0_ + e, c * P:(c + 1) * P], ident[:])
                last.then_inc(rt_vt, 1)

        def ret_rot_pe(pe, m):
            for w, p in enumerate((K_, Q2_)):
                acc_read(pe, "ret", p, m)
                mix_free(pe, w, Uses.ret[w] + (RT0, RT1)[w] * m + 1)
                for b in range(2):
                    last = pe.matmul(mix[w][:, b, 0:HT], perm[:], r_pre[:, p, b * HT:(b + 1) * HT], start=True, stop=True)
                last.then_inc(rt_rot, 1)

        def ret_scores_pe(pe, m):
            pe.wait_ge(rt_kq, 2 * m + 2)
            mix_free(pe, 0, Uses.ret[0] + RT0 * m + 2)
            for c in range(NT):
                cols = slice(c * P, (c + 1) * P)
                last = pe.matmul(mix_r[0][:, cols], r_rot[:, 0, cols], r_rot[:, 1, cols], start=True, stop=True)
            last.then_inc(rt_sc, 1)
            mix_free(pe, 1, Uses.ret[1] + RT1 * m + 2)
            for c in range(NT):
                cols = slice(c * P, (c + 1) * P)
                last = pe.transpose(mix_r[1][:, cols], r_rot[:, 0, cols], ident[:])
            last.then_inc(rt_kt, 1)

        def ret_kv_pe(pe, m):
            tiles = ((0, 1, 2, 3), (0, 2, 3, 4))
            for w in (1, 0):
                mix_free(pe, 1, Uses.ret[1] + RT1 * m + 3)
                if w == 0:
                    mix_free(pe, 0, Uses.ret[0] + RT0 * m + 3)
                for j, c in enumerate(tiles[w]):
                    last = pe.matmul(mix_r[w][:, j * RET_DV:(j + 1) * RET_DV], r_ktok[:, w, j, :],
                                     r_v[:, c].rearrange("p e t -> p (e t)"), start=True, stop=True)
                last.then_inc(rt_kv, 1)

        def ret_out_pe(pe, m):
            pe.wait_ge(rt_qdec, 2 * m + 2)
            pe.wait_ge(rt_state, 6 * m + 6)
            for e in range(2):
                dv = slice(e * P, (e + 1) * P)
                for c in range(NT):
                    cols, lat = slice(c * P, (c + 1) * P), slice((c - 1) * P, c * P)
                    last = pe.matmul(mix_r[e][:, cols], r_v[:, c, e, :], r_att[:, c, :], start=True, stop=(c == 0))
                    if c:
                        for w in range(2):
                            n = c - 1 if w == 0 else 4 - c
                            st = r_sin[:, w, dv] if n == 0 else r_srun[:, w, n - 1, dv]
                            last = pe.matmul(mix_r[e][:, cols], st, r_qdec[:, w, lat], start=False, stop=(w == 1))
                last.then_inc(rt_o, 1)

        def ret_ss_pe(pe, m):
            pe.wait_ge(rt_osq, 2 * m + 2)
            mix_free(pe, 0, Uses.ret[0] + RT0 * m + 4)
            for b in range(2):
                for e in range(2):
                    last = pe.matmul(mix[0][:, b, 0:HT], ones[:], r_tmp[:, e, b * HT:(b + 1) * HT],
                                     start=(e == 0), stop=(e == 1))
            last.then_inc(rt_ss, 1)


        def merge_dve(dve, n):
            for p in range(2):
                acc_read(dve, "gate", p, n)
                projected(dve, "gate", 2 + p, n)
                dve.tensor_tensor(halves(sig_buf[:, p, :]), halves(sig_buf[:, p, :]), acc_v[p],
                                  ALU.mult).then_inc(evacuated[p], 1)
            for p in range(2):
                acc_read(dve, "gate", 2 + p, n)
            dve.tensor_tensor(merged[:, n, :], sig_buf[:, 0, :], sig_buf[:, 1, :], ALU.add).then_inc(merge_done, 1)

        def merged_lo(dve, k):
            dve.wait_ge(part_hi, 2 * KT + k + 1)
            dve.tensor_tensor(h_lo[:, k, :], merged[:, k, :], h_hi[:, k, :].bitcast(F32), ALU.subtract).then_inc(part_lo, 1)

        block = ctx.enter_context(nc.Block())

        @block.sync
        def _(sp):
            sp.dma_start(c_col[:].rearrange("p k e -> p (k e)"), d["in_ccol"]).then_inc(in_c, 16)
            sp.dma_start(c_row[:].rearrange("p e k -> p (e k)"), d["in_c"].to_broadcast([P, 2 * D_MODEL])).then_inc(in_c, 16)
            def head(m):
                load_ada(sp, m, m % ADA_SLOTS, m + 1 - ADA_SLOTS)

            def head_pe(m):
                sp.dma_start(ada_pe[:, m, :], d["ada_pe"][m]).then_inc(ada_pe_loaded[m], 16)

            def x_part(n):
                sp.dma_start(x[:, 4 * n:4 * n + 4, :], d["x"][:, 4 * n:4 * n + 4, :]).then_inc(in_x[n], 16)

            head(0)
            head_pe(0)
            for n, w in C_NAMES:
                sp.dma_start(small[n][:], d["in_" + n]).then_inc(in_small, 16)
            head(1)
            head_pe(1)
            x_part(0)
            head(2)
            head_pe(2)
            x_part(1)
            head(3)
            head_pe(3)
            for m in range(4, HEAD_DVE):
                head(m)
                if m < HEAD_PE:
                    head_pe(m)
            sp.dma_start(ident[:], d["ident"]).then_inc(in_tab, 16)
            sp.dma_start(perm[:], d["perm"]).then_inc(in_tab, 16)
            for f in (1, 2):
                if f == 2:
                    for name in ("hg", "ret", "gate", "wo"):
                        steps, slots, _, _, _, _ = ST.phase[name]
                        with sp.Fori(0, steps) as i:
                            for p in range(len(slots)):
                                load_slab(sp, name, p, i)
                for c in range(len(FF_CHUNKS)):
                    for name, steps in ((f"up{f}{c}", FF_CHUNKS[c] // 2), (f"down{f}{c}", KT // 4)):
                        with sp.Fori(0, steps) as i:
                            load_slab(sp, name, 0, i)
                            load_slab(sp, name, 1, i)
                            if f == 1:
                                load_ada_step(sp, name, i)
                            load_slab(sp, name, 2, i)
                            load_slab(sp, name, 3, i)
            for k in range(KT):
                sp.wait_ge(xn_done, 3 * KT + k + 1)
                sp.dma_start(d["y"][:, k, :], x[:, k, :]).then_inc(y_out, 16)
            sp.wait_ge(y_out, 16 * KT)
            sp.wait_ge(states_out, 16 * (HG_HEADS + RET_HEADS + 1))

        @block.gpsimd
        def _(pool):
            pool.sem_inc(split_done, CREDIT)
            pool.sem_inc(sq_added, SQ_CREDIT)
            square_clear(pool, 0)
            for k in range(KT - 1):
                square_add(pool, 0, k)
            for name, steps, slots, _ in PHASES:
                if name == "hg":
                    split_hg(pool)
                elif name in LAST.values():
                    n = {v: k for k, v in LAST.items()}[name]
                    for p in range(4):
                        split_slab(pool, name, p, 0)
                    if n == 2:
                        pool.wait_ge(part_lo, 3 * KT)
                    square_clear(pool, n)
                    for k in range(KT):
                        if k < 4:
                            split_slab(pool, name, k, 1)
                        if k < KT - 1:
                            square_add(pool, n, k)
                else:
                    with pool.Fori(1 if name == "ret" else 0, steps) as i:
                        for p in range(len(slots)):
                            split_slab(pool, name, p, i)

        @block.tensor
        def _(pe):
            pe.sem_inc(slab_done, CREDIT)
            pe.sem_inc(evacuated[0], 1)
            pe.sem_inc(evacuated[1], 1)
            pe.sem_inc(mixed[0], 1)
            pe.sem_inc(mixed[1], 1)
            pe.wait_ge(ones_set, 1)
            pe.wait_ge(silu_col_done, 1)
            mix_free(pe, 0, Uses.norm1[0])
            ada_pe_tiles(pe, range(0, 4))
            norm_pe(pe, 0, Uses.norm1[1])
            ada_pe_tiles(pe, range(4, HEAD_PE))
            for c in range(len(FF_CHUNKS)):
                ff_pe(pe, 1, c, u_base(1, c))
            norm_pe(pe, 1, Uses.norm2[1])
            pe.wait_ge(in_tab, 32)
            project_pair(pe, "hg", h_hi, h_lo, (hlo_done, KT))
            for p in range(2, 5):
                project(pe, "hg", p, 0, h_hi, h_lo)
            with pe.Fori(1, HG_HEADS) as h:
                hg_body_pe(pe, h - 1, "hg", h)
            hg_body_pe(pe, HG_HEADS - 1, "ret", 0)
            project(pe, "ret", 5, 0, h_hi, h_lo)
            ret_vt_pe(pe, 0)
            with pe.Fori(1, RET_HEADS) as h:
                project(pe, "ret", 0, h, h_hi, h_lo)
                ret_rot_pe(pe, h - 1)
                project(pe, "ret", 1, h, h_hi, h_lo)
                ret_scores_pe(pe, h - 1)
                project(pe, "ret", 2, h, h_hi, h_lo)
                ret_kv_pe(pe, h - 1)
                project(pe, "ret", 3, h, h_hi, h_lo)
                ret_out_pe(pe, h - 1)
                project(pe, "ret", 4, h, h_hi, h_lo)
                ret_ss_pe(pe, h - 1)
                project(pe, "ret", 5, h, h_hi, h_lo)
                ret_vt_pe(pe, h)
            m = RET_HEADS - 1
            project(pe, "gate", 0, 0, h_hi, h_lo)
            ret_rot_pe(pe, m)
            project(pe, "gate", 1, 0, h_hi, h_lo, ks=range(0, 5))
            ret_scores_pe(pe, m)
            project(pe, "gate", 1, 0, h_hi, h_lo, ks=range(5, 8))
            ret_kv_pe(pe, m)
            project(pe, "gate", 2, 0, hg_hi, hg_lo, ks=range(0, 3), tiles_done=(part_lo, 0))
            ret_out_pe(pe, m)
            project(pe, "gate", 2, 0, hg_hi, hg_lo, ks=range(3, 5), tiles_done=(part_lo, 0))
            ret_ss_pe(pe, m)
            project(pe, "gate", 2, 0, hg_hi, hg_lo, ks=range(5, 8), tiles_done=(part_lo, 0))
            project(pe, "gate", 3, 0, ret_hi, ret_lo, tiles_done=(part_lo, KT))
            with pe.Fori(1, KT) as n:
                project(pe, "gate", 0, n, h_hi, h_lo)
                project(pe, "gate", 1, n, h_hi, h_lo)
                project(pe, "gate", 2, n, hg_hi, hg_lo)
                project(pe, "gate", 3, n, ret_hi, ret_lo)
            for i in range(KT // 4):
                for p in range(4):
                    project(pe, "wo", p, i, h_hi, h_lo, tiles_done=(part_lo, 2 * KT) if i == p == 0 else None)
            norm_pe(pe, 2, Uses.norm3[1])
            for c in range(len(FF_CHUNKS)):
                ff_pe(pe, 2, c, u_base(2, c))
            norm_pe(pe, 3, Uses.norm4[1])

        @block.scalar
        def _(act):
            act.sem_inc(states_out, 16)
            act.wait_ge(in_c, 32)
            act.activation(c_sig[:], c_col[:], ACT.Sigmoid)
            act.activation(ada_prod[:], c_row[:], ACT.Sigmoid).then_inc(silu_done, 1)
            norm_stats_act(act, 0)
            act.wait_ge(coef_done, 2)
            norm_rows_act(act, 0)
            for c in range(len(FF_CHUNKS)):
                up_act(act, 1, c)
                if c == 0:
                    small_chain_act(act)
            norm_stats_act(act, 1)
            act.wait_ge(coef_done, 9)
            norm_rows_act(act, 1)
            act.wait_ge(hlo_done, 2 * KT)
            act.dma_start(masks[:].rearrange("p u t -> p (u t)"), d["masks"]).then_inc(masks_in, 16)
            for p in range(5):
                hg_evac(act, 0, p)
            hg_start_act(act, 0)
            with act.Fori(1, HG_HEADS) as h:
                hg_act(act, h - 1, h, lambda p: hg_evac(act, h, p))
            hg_act(act, HG_HEADS - 1, None, lambda p: ret_evac(act, 0, p))
            ret_tables_load(act)
            ret_evac(act, 0, 5)
            ret_v_act(act, 0)
            ret_tables_act(act)
            with act.Fori(1, RET_HEADS) as h:
                ret_act(act, h - 1, h)
            ret_act(act, RET_HEADS - 1, None)
            act.wait_ge(rt_out, 2 * RET_HEADS + 1)
            act.wait_ge(states_out, 16 * (HG_HEADS + RET_HEADS + 1))
            for k in range(HG_EARLY, KT):
                act.activation(hg_hi[k], o_hg[:, k, :], ACT.Copy).then_inc(part_hi, 1)
            for k in range(KT):
                act.activation(ret_hi_tiles[k], o_ret[:, k, :], ACT.Copy).then_inc(part_hi, 1)
            act.preload_act_table_set("sigmoid_and_others")
            with act.Fori(1, KT) as n:
                for p in range(2):
                    gate_evac(act, p, n)
            for k in range(KT):
                act.wait_ge(merge_done, k + 2)
                act.activation(h_hi[:, k, :], merged[:, k, :], ACT.Copy).then_inc(part_hi, 1)
            norm_stats_act(act, 2)
            norm_rows_act(act, 2)
            for c in range(len(FF_CHUNKS)):
                up_act(act, 2, c)
            norm_stats_act(act, 3)

        @block.vector
        def _(dve):
            for credited, n in ((ulo_done, 1), (hg_out, 1), (rt_out, 1), (merge_done, 1), (ada_read, ADA_SLOTS),
                                (ada_moved, 1)):
                dve.sem_inc(credited, n)
            dve.memset(eps[:], EPS)
            dve.memset(ones[:], 1.0).then_inc(ones_set, 1)
            dve.wait_ge(silu_done, 1)
            dve.tensor_tensor(c_col[:], c_col[:], c_sig[:], ALU.mult).then_inc(silu_col_done, 1)
            dve.tensor_tensor(c_row[:], c_row[:], ada_prod[:], ALU.mult).then_inc(silu_done, 1)
            dve.wait_ge(silu_done, 2)
            dve.wait_ge(in_small, 16 * len(C_NAMES))
            for m in range(HEAD_DVE):
                ada_tiles(dve, m, (m % ADA_SLOTS,), (m // ADA_SLOTS + 1,), 0)
            dve.wait_ge(ada_pe_done, 1)
            ada_bias(dve, HEAD_DVE, HEAD_PE, mix_r[0][:, 0:2 * HEAD_PE].rearrange("p (m e) -> p m e", e=2)).then_inc(mixed[0], 1)
            make_scale(dve, 0)
            norm_dve(dve, 0, Uses.norm1[1])
            for c in range(len(FF_CHUNKS)):
                up_dve(dve, 1, c, u_base(1, c))
                if c == 0:
                    make_gate(dve, 0)
                    small_chain(dve)
                with dve.Fori(0, KT // 4) as i:
                    ada_step(dve, f"down1{c}", i, (0, 1))
                    residual(dve, f"down1{c}", i, G1)
            for n in (1, 2):
                make_scale(dve, n)
                make_gate(dve, n)
            norm_dve(dve, 1, Uses.norm2[1])
            dve.memset(p_b[:, :, 0:1], 0.0)
            dve.wait_ge(masks_in, 16)
            hg_start_dve(dve, 0)
            hg_sums_dve(dve, 0)
            with dve.Fori(1, HG_HEADS) as h:
                hg_dve(dve, h - 1, h)
            hg_dve(dve, HG_HEADS - 1, None)
            ret_tables_dve(dve)
            with dve.Fori(1, RET_HEADS) as h:
                ret_dve(dve, h - 1, False)
            ret_dve(dve, RET_HEADS - 1, True)
            for k in range(HG_EARLY, KT):
                part_lo_dve(dve, "hg", k)
            for k in range(KT):
                part_lo_dve(dve, "ret", k)
            with dve.Fori(0, KT - 1) as n:
                merge_dve(dve, n)
            projected(dve, "gate", 1, KT - 1)
            for k in range(KT - 1):
                merged_lo(dve, k)
            merge_dve(dve, KT - 1)
            merged_lo(dve, KT - 1)
            with dve.Fori(0, KT // 4) as i:
                residual(dve, "wo", i, G2)
            norm_dve(dve, 2, Uses.norm3[1])
            for c in range(len(FF_CHUNKS)):
                up_dve(dve, 2, c, u_base(2, c))
                with dve.Fori(0, KT // 4) as i:
                    residual(dve, f"down2{c}", i, G3)
            norm_dve(dve, 3, Uses.norm4[1])


def _tiles(w):
    kt, n = w.shape[0] // P, w.shape[1] // P
    return w.reshape(kt, P, n, P).transpose(2, 1, 0, 3).reshape(n, P, kt * P)


def _columns(v):
    return np.ascontiguousarray(v.reshape(-1, P).T)


def _down(w2, c):
    lo = sum(FF_CHUNKS[:c]) * P
    part = _tiles(w2[lo:lo + FF_CHUNKS[c] * P])
    return np.pad(part, ((0, 0), (0, 0), (0, KT * P - part.shape[2])))


def _up(w13, c):
    t = _tiles(w13)
    n = D_FF // P
    lo = sum(FF_CHUNKS[:c])
    ab = np.stack([t[lo:lo + FF_CHUNKS[c]], t[n + lo:n + lo + FF_CHUNKS[c]]], 1)
    return ab.reshape(-1, P, KT * P)


def kernel(**inputs):
    import concourse.bacc as bacc
    from concourse.bass_utils import run_bass_kernel_spmd

    a = {k: np.asarray(v) for k, v in inputs.items()}
    win = _tiles(a["w_in"][0])
    cuts = np.cumsum([0, 512, 512, 1024, 1024, 1024, 1024, 1024, 1024, 1024, 1024, 1024]) // P
    rq, rk, rv, rg, hq, hff, hfb, hi, hog, gr, gh = [win[cuts[n]:cuts[n + 1]] for n in range(11)]
    hg = np.stack([hff, hfb, hq, hog, hi], 1).reshape(-1, P, KT * P)
    ret = np.stack([rk, rq, rv[0::2], rv[1::2], rg[0::2], rg[1::2]], 1).reshape(-1, P, KT * P)
    gate = np.stack([gh, gr, _tiles(a["w_hg_proj"][0]), _tiles(a["w_ret_proj"][0])], 1).reshape(-1, P, KT * P)
    stream = []
    for f in (1, 2):
        if f == 2:
            stream += [hg, ret, gate, _tiles(a["w_o"][0])]
        for c in range(len(FF_CHUNKS)):
            stream += [_up(a[f"ffn{f}_w13"][0], c), _down(a[f"ffn{f}_w2"][0], c)]
    tables, kpos = shape_constants()
    x = np.concatenate([a["x_prompt"][0], a["x_sample"][0]], 0)
    arrays = {
        "w": np.concatenate(stream, 0),
        "ada": np.delete(a["ada_w"][0].T.reshape(-1, P, D_MODEL), range(HEAD_DVE, HEAD_DVE + HEAD_PE), 0),
        "ada_pe": _tiles(a["ada_w"][0][:, HEAD_DVE * P:(HEAD_DVE + HEAD_PE) * P]),
        "in_ccol": np.stack([_columns(a["c_ctx"]), _columns(a["c"][0])], 2).reshape(P, 2 * KT),
        "x": np.ascontiguousarray(x.T.reshape(KT, P, T).transpose(1, 0, 2)),
        "s_hg": np.ascontiguousarray(a["state_hgrn"][0, 0].transpose(1, 2, 0, 3)),
        "s_ret": np.ascontiguousarray(a["state_ret"][0, 0].transpose(1, 2, 0, 3)),
        "in_c": np.concatenate([a["c_ctx"], a["c"][0]])[None],
        "in_ada_b": _columns(a["ada_b"][0]),
        "in_norm_w": _columns(a["norm_w"][0]),
        "in_final_w": _columns(a["final_norm_w"]),
        "in_hg_w": _columns(a["hg_norm_w"][0]),
        "in_lb": _columns(a["hg_lb_logits"]),
        "in_decay": np.ascontiguousarray(np.broadcast_to(a["ret_decay"][0].reshape(1, 8), (P, 8))),
        "in_kpos": kpos,
        **tables,
    }
    outs = {"y": (P, KT, T), "out_hg": (HG_HEADS, P, 2, HG_DV), "out_ret": (RET_HEADS, P, 2, RET_DV)}
    nc = bacc.Bacc("TRN2", target_bir_lowering=False, num_devices=1)
    d = {}
    for n, v in arrays.items():
        d[n] = nc.dram_tensor(n + "_dram", v.shape, mybir.dt.from_np(v.dtype), kind="ExternalInput").ap()
    for n, shape in outs.items():
        d[n] = nc.dram_tensor(n + "_dram", shape, F32, kind="ExternalOutput").ap()
    build(nc, d)
    r = run_bass_kernel_spmd(nc, [{n + "_dram": v for n, v in arrays.items()}], core_ids=[0]).results[0]
    y = r["y_dram"].transpose(1, 0, 2).reshape(D_MODEL, T).T
    out_ret = r["out_ret_dram"].transpose(2, 0, 1, 3)[None, None]
    out_hg = r["out_hg_dram"].transpose(2, 0, 1, 3)[None, None]
    return (np.ascontiguousarray(y[:CTX])[None], np.ascontiguousarray(y[CTX:])[None],
            np.ascontiguousarray(out_ret), np.ascontiguousarray(out_hg))
```
